# Optimizing a Trainium2 kernel written in Bass

```python
import math
import jax
import jax.numpy as jnp
from jax import lax
import numpy as np

D_MODEL = 1024
BATCH = 1
SEQ = 1024
DEPTH = 2
DEC_BATCH = 8
DEC_SEQ = 16
PAST_LEN = 1024

CHUNK = 64
N_A = DEPTH // 2
N_B = DEPTH - N_A
HGRN_EXPAND = 128
A_WIDTH = D_MODEL
A_HEADS = A_WIDTH // HGRN_EXPAND
A_DK = HGRN_EXPAND
A_DV = A_WIDTH // A_HEADS
B_HEADS = 16
Q_LORA = 512
KV_LORA = 256
NOPE_DIM = 128
ROPE_DIM = 64
B_DV = 128
B_WIDTH = B_HEADS * B_DV
Q_BLOCK = 128
ROPE_BASE = 10000.0
EPS = 1e-6
NEG_INF = -1e30
ATTN_SCALE = (NOPE_DIM + ROPE_DIM) ** -0.5
ALPHA = (2 * DEPTH) ** 0.25
BETA = (8 * DEPTH) ** -0.25

kernel_name = 'hybrid_hgrn2_mla_yoco_stream_step'

def rms_norm(x, g):
    xf = x.astype(jnp.float32)
    y = xf * lax.rsqrt(jnp.mean(xf * xf, axis=-1, keepdims=True) + EPS)
    return (y * g.astype(jnp.float32)).astype(x.dtype)

def layer_norm(x, g, b):
    xf = x.astype(jnp.float32)
    mu = jnp.mean(xf, axis=-1, keepdims=True)
    var = jnp.mean(jnp.square(xf - mu), axis=-1, keepdims=True)
    y = (xf - mu) * lax.rsqrt(var + EPS) * g.astype(jnp.float32) + b.astype(jnp.float32)
    return y.astype(x.dtype)

def rope(x, pos):
    half = ROPE_DIM // 2
    inv = jnp.power(ROPE_BASE, -jnp.arange(half, dtype=jnp.float32) / half)
    ang = pos.astype(jnp.float32)[:, None] * inv[None, :]
    ang = ang.reshape((ang.shape[0],) + (1,) * (x.ndim - 3) + (half,))
    cos, sin = jnp.cos(ang), jnp.sin(ang)
    xf = x.astype(jnp.float32)
    x1, x2 = xf[..., :half], xf[..., half:]
    return jnp.concatenate([x1 * cos - x2 * sin, x1 * sin + x2 * cos], axis=-1).astype(x.dtype)

def gla_chunked(q, k, v, log_f, s0, chunk):
    bsz, t, h, dk = q.shape
    dv = v.shape[-1]
    n = t // chunk
    f32 = jnp.float32
    q, k, log_f = [a.astype(f32).reshape(bsz, n, chunk, h, dk) for a in (q, k, log_f)]
    v = v.astype(f32).reshape(bsz, n, chunk, h, dv)
    b = jnp.cumsum(log_f, axis=2)
    mid = chunk // 2
    b_mid = b[:, :, mid:mid + 1]
    q_in = q * jnp.exp(b - b_mid)
    k_in = k * jnp.exp(b_mid - b)
    causal = jnp.tril(jnp.ones((chunk, chunk), dtype=bool))
    scores = jnp.einsum('bnlhk,bnshk->bnhls', q_in, k_in)
    scores = jnp.where(causal, scores, 0.0)
    o_intra = jnp.einsum('bnhls,bnshv->bnlhv', scores, v)
    b_last = b[:, :, -1]
    chunk_state = jnp.einsum('bnshk,bnshv->bnhkv', k * jnp.exp(b_last[:, :, None] - b), v)
    decay = jnp.exp(b_last)

    def step(s, inp):
        d, cs = inp
        return d[..., None] * s + cs, s

    s_final, s_prev = lax.scan(step, s0.astype(f32),
                               (jnp.moveaxis(decay, 1, 0), jnp.moveaxis(chunk_state, 1, 0)))
    s_prev = jnp.moveaxis(s_prev, 0, 1)
    o_inter = jnp.einsum('bnlhk,bnhkv->bnlhv', q * jnp.exp(b), s_prev)
    o = (o_intra + o_inter).reshape(bsz, t, h, dv)
    return o, s_final

def mixer_hgrn2(x, w_in, lb, norm_g, w_out, s0, chunk):
    bsz, t, _ = x.shape
    proj = jnp.einsum('btd,de->bte', x, w_in)
    qa, za, ia, ga = jnp.split(proj, 4, axis=-1)
    shp = (bsz, t, A_HEADS, A_DK)
    lbh = lb.reshape(A_HEADS, A_DK)
    zf = za.astype(jnp.float32).reshape(shp)
    log_f = jnp.log(lbh + (1.0 - lbh) * jax.nn.sigmoid(zf))
    k = (1.0 - lbh) * jax.nn.sigmoid(-zf)
    o, s = gla_chunked(qa.reshape(shp), k, ia.reshape(bsz, t, A_HEADS, A_DV), log_f, s0, chunk)
    o = rms_norm(o, norm_g).reshape(bsz, t, A_WIDTH).astype(x.dtype) * jax.nn.silu(ga)
    return jnp.einsum('bte,ed->btd', o, w_out), s

def shared_latent_kv(x, pos, w_dkv, kv_norm_g):
    kv = jnp.einsum('btd,de->bte', x, w_dkv)
    c = rms_norm(kv[..., :KV_LORA], kv_norm_g)
    kr = rope(kv[..., KV_LORA:], pos)
    return c, kr

def mla_queries(x, pos, w_in, q_norm_g, w_uq, w_uk):
    bsz, t, _ = x.shape
    proj = jnp.einsum('btd,de->bte', x, w_in)
    cq = rms_norm(proj[..., :Q_LORA], q_norm_g)
    gate = proj[..., Q_LORA:]
    q = jnp.einsum('btr,re->bte', cq, w_uq).reshape(bsz, t, B_HEADS, NOPE_DIM + ROPE_DIM)
    q_lat = jnp.einsum('bthn,khn->bthk', q[..., :NOPE_DIM], w_uk)
    q_rope = rope(q[..., NOPE_DIM:], pos)
    return q_lat, q_rope, gate

def latent_attend(q_lat, q_rope, c, kr, w_uv, mask):
    s = (jnp.einsum('bqhk,bsk->bhqs', q_lat, c)
         + jnp.einsum('bqhr,bsr->bhqs', q_rope, kr)).astype(jnp.float32) * ATTN_SCALE
    if mask is not None:
        s = jnp.where(mask, s, NEG_INF)
    p = jax.nn.softmax(s, axis=-1).astype(c.dtype)
    o_lat = jnp.einsum('bhqs,bsk->bqhk', p, c)
    return jnp.einsum('bqhk,khv->bqhv', o_lat, w_uv)

def attend_prompt(q_lat, q_rope, c, kr, w_uv):
    bsz, t = q_lat.shape[:2]
    nb = t // Q_BLOCK
    key_chunk = jnp.arange(t, dtype=jnp.int32) // CHUNK

    def blk(args):
        ql, qr, start = args
        q_chunk = (start + jnp.arange(Q_BLOCK, dtype=jnp.int32)) // CHUNK
        mask = key_chunk[None, :] <= q_chunk[:, None]
        return latent_attend(ql, qr, c, kr, w_uv, mask[None, None])

    to_blocks = lambda a: jnp.moveaxis(a.reshape((bsz, nb, Q_BLOCK) + a.shape[2:]), 1, 0)
    o = lax.map(blk, (to_blocks(q_lat), to_blocks(q_rope), jnp.arange(nb, dtype=jnp.int32) * Q_BLOCK))
    return jnp.moveaxis(o, 0, 1).reshape(bsz, t, B_WIDTH)

def trunk(x, pos, s0, c_past, kr_past, chunk, p):
    bsz, t, _ = x.shape
    lb_all = jnp.cumsum(jax.nn.softmax(p['lb_gamma'].astype(jnp.float32), axis=0), axis=0)
    states = []
    c_new, kr_new = None, None
    for l in range(DEPTH):
        if l < N_A:
            out, s = mixer_hgrn2(x, p['w_in_a'][l], lb_all[l], p['a_norm_g'][l], p['w_out_a'][l], s0[l], chunk)
            states.append(s)
        else:
            if l == N_A:
                c_new, kr_new = shared_latent_kv(x, pos, p['w_dkv'], p['kv_norm_g'])
            j = l - N_A
            q_lat, q_rope, gate = mla_queries(x, pos, p['w_in_b'][j], p['q_norm_g'][j], p['w_uq'][j], p['w_uk'])
            if c_past is None:
                o = attend_prompt(q_lat, q_rope, c_new, kr_new, p['w_uv'])
            else:
                c_all = jnp.concatenate([c_past.astype(c_new.dtype), c_new], axis=1)
                kr_all = jnp.concatenate([kr_past.astype(kr_new.dtype), kr_new], axis=1)
                o = latent_attend(q_lat, q_rope, c_all, kr_all, p['w_uv'], None).reshape(bsz, t, B_WIDTH)
            out = jnp.einsum('bte,ed->btd', o * jax.nn.silu(gate), p['w_out_b'][j])
        x = layer_norm(ALPHA * x + out, p['ln_g'][l], p['ln_b'][l])
    return x, jnp.stack(states), c_new, kr_new

def setup_inputs(seed: int = 0) -> dict:
    key = jax.random.key(seed)
    ks = jax.random.split(key, 20)
    nrm = lambda k, shp, s: jax.random.normal(k, shp, jnp.float32) * s
    return {
        'x_prompt': nrm(ks[0], (BATCH, SEQ, D_MODEL), 1.0),
        'x_sample': nrm(ks[1], (DEC_BATCH, DEC_SEQ, D_MODEL), 1.0),
        'state_hgrn': nrm(ks[2], (N_A, DEC_BATCH, A_HEADS, A_DK, A_DV), 0.5),
        'cache_ckv': nrm(ks[3], (DEC_BATCH, PAST_LEN, KV_LORA), 1.0),
        'cache_krope': nrm(ks[4], (DEC_BATCH, PAST_LEN, ROPE_DIM), 1.0),
        'w_in_a': nrm(ks[5], (N_A, D_MODEL, 4 * A_WIDTH), D_MODEL ** -0.5),
        'lb_gamma': nrm(ks[6], (N_A + 1, A_WIDTH), 0.1),
        'a_norm_g': 1.0 + nrm(ks[7], (N_A, A_DV), 0.02),
        'w_out_a': nrm(ks[8], (N_A, A_WIDTH, D_MODEL), BETA * A_WIDTH ** -0.5),
        'w_dkv': nrm(ks[9], (D_MODEL, KV_LORA + ROPE_DIM), D_MODEL ** -0.5),
        'kv_norm_g': 1.0 + nrm(ks[10], (KV_LORA,), 0.02),
        'w_uk': nrm(ks[11], (KV_LORA, B_HEADS, NOPE_DIM), KV_LORA ** -0.5),
        'w_uv': nrm(ks[12], (KV_LORA, B_HEADS, B_DV), KV_LORA ** -0.5),
        'w_in_b': nrm(ks[13], (N_B, D_MODEL, Q_LORA + B_WIDTH), D_MODEL ** -0.5),
        'q_norm_g': 1.0 + nrm(ks[14], (N_B, Q_LORA), 0.02),
        'w_uq': nrm(ks[15], (N_B, Q_LORA, B_HEADS * (NOPE_DIM + ROPE_DIM)), Q_LORA ** -0.5),
        'w_out_b': nrm(ks[16], (N_B, B_WIDTH, D_MODEL), BETA * B_WIDTH ** -0.5),
        'ln_g': 1.0 + nrm(ks[17], (DEPTH, D_MODEL), 0.02),
        'ln_b': nrm(ks[18], (DEPTH, D_MODEL), 0.02),
    }

def reference(x_prompt, x_sample, state_hgrn, cache_ckv, cache_krope,
              w_in_a, lb_gamma, a_norm_g, w_out_a, w_dkv, kv_norm_g, w_uk, w_uv,
              w_in_b, q_norm_g, w_uq, w_out_b, ln_g, ln_b):
    p = dict(w_in_a=w_in_a, lb_gamma=lb_gamma, a_norm_g=a_norm_g, w_out_a=w_out_a,
             w_dkv=w_dkv, kv_norm_g=kv_norm_g, w_uk=w_uk, w_uv=w_uv,
             w_in_b=w_in_b, q_norm_g=q_norm_g, w_uq=w_uq, w_out_b=w_out_b,
             ln_g=ln_g, ln_b=ln_b)
    t_p = x_prompt.shape[1]
    pos_p = jnp.arange(t_p, dtype=jnp.int32)
    s0_p = jnp.zeros((N_A, x_prompt.shape[0], A_HEADS, A_DK, A_DV), jnp.float32)
    y_prompt, state_hgrn_prompt, ckv_prompt, krope_prompt = trunk(
        x_prompt, pos_p, s0_p, None, None, CHUNK, p)
    t_s = x_sample.shape[1]
    past = cache_ckv.shape[1]
    pos_s = past + jnp.arange(t_s, dtype=jnp.int32)
    y_sample, state_hgrn_sample, ckv_sample, krope_sample = trunk(
        x_sample, pos_s, state_hgrn, cache_ckv, cache_krope, t_s, p)
    return (y_prompt, y_sample, state_hgrn_prompt, ckv_prompt, krope_prompt,
            state_hgrn_sample, ckv_sample, krope_sample)


_drawn_inputs = setup_inputs


def setup_inputs(seed=0):
    import zlib

    import numpy as np

    out = dict(_drawn_inputs(seed))
    spreads = {}
    factors = {'cache_ckv': 5.324,
     'cache_krope': 8.0,
     'a_norm_g': 8.0,
     'kv_norm_g': 2.73,
     'w_uk': 3.165,
     'q_norm_g': 8.0,
     'w_uq': 2.881}
    for name, (base, spread) in spreads.items():
        noise = np.random.default_rng([zlib.crc32(name.encode()), seed]).standard_normal(out[name].shape)
        drawn = base * np.exp(spread * noise) if base else spread * noise
        out[name] = jnp.asarray(drawn.astype(out[name].dtype))
    for name, factor in factors.items():
        out[name] = (out[name] * factor).astype(out[name].dtype)
    return out
```

```python
from contextlib import ExitStack

import numpy as np
import concourse.bass as bass
from concourse import mybir

F32 = mybir.dt.float32
F32R = mybir.dt.float32r
I32 = mybir.dt.int32
ACT = mybir.ActivationFunctionType
ALU = mybir.AluOpType
AX = mybir.AxisListType

P = 128
D = 1024
KD = D // P
SEQ, NSEQ, SLEN, PAST = 1024, 8, 16, 1024
T = SEQ + NSEQ * SLEN
NT = T // P
NPB = SEQ // P
TG = 384
NTG = T // TG
CH = 64
NCH = SEQ // CH
AH = 8
HEADS, QL, KVL, RD, NOPE, DV = 16, 512, 256, 64, 128, 128
QD = NOPE + RD
EPS = 1e-6
ALPHA = 4 ** 0.25
SCALE = QD ** -0.5
Z_MIN = -80.0
MASKED = -1e30
BANK = 512


def flat(ap):
    return ap.rearrange("p a b -> p (a b)")


def shape_constants():
    f = np.float32
    s, l = np.arange(P)[:, None], np.arange(P)[None, :]
    c = {}
    c["ident"] = np.eye(P, dtype=f)
    c["mask_prompt"] = np.tile(((s <= l) & (s // CH == l // CH)).astype(np.int32), (1, 4))
    c["mask_sample"] = ((s <= l) & (s // SLEN == l // SLEN)).astype(np.int32)
    r = np.ones((P, T), f)
    r[:, 0:SEQ:CH] = 0
    r[:, SEQ::SLEN] = 0
    c["restart"] = r
    c["member"] = (s // SLEN == np.arange(NSEQ)[None, :]).astype(f)
    pos = np.concatenate([np.arange(SEQ), np.tile(PAST + np.arange(SLEN), NSEQ)]).astype(f)
    half = RD // 2
    inv = np.power(f(10000.0), -np.arange(half, dtype=f) / f(half)).astype(f)
    ang = (pos[:, None] * inv[None, :]).astype(f)
    cos, sin = np.cos(ang).astype(f), np.sin(ang).astype(f)
    c["cos_nat"] = cos.reshape(NT, P, half).transpose(1, 0, 2).reshape(P, NT * half).copy()
    c["sin_nat"] = sin.reshape(NT, P, half).transpose(1, 0, 2).reshape(P, NT * half).copy()
    c["cos_t"] = np.tile(cos.T, (4, 1))
    c["sin_t"] = np.concatenate([sin.T, -sin.T] * 2, 0)
    return c


class Core:

    def __init__(self, nc, ctx):
        self.nc, self.ctx, self.sems = nc, ctx, []
        ctx.callback(self.clear)

    def clear(self):
        self.nc.all_engine_barrier()
        numbers = sorted(s.num for s in self.sems)
        start = 0
        for i in range(1, len(numbers) + 1):
            if i == len(numbers) or numbers[i] != numbers[i - 1] + 1:
                self.nc.gpsimd.sem_clear(range(numbers[start], numbers[i - 1] + 1))
                start = i
        self.nc.all_engine_barrier()
        for s in reversed(self.sems):
            self.nc.release_semaphore(s)

    def sb(self, name, shape, dt=F32):
        return self.ctx.enter_context(self.nc.sbuf_tensor(name, [P] + list(shape), dt))

    def ps(self, name, shape, dt=F32):
        return self.ctx.enter_context(self.nc.psum_tensor(name, [P] + list(shape), dt))

    def sem(self, name):
        self.sems.append(self.nc.alloc_semaphore(name))
        return self.sems[-1]


def round_high(nc, high, x):
    return nc.scalar.activation(high, x, ACT.Identity)


def round_low(nc, low, x, high):
    return nc.vector.tensor_tensor(low, x, high.bitcast(F32), ALU.subtract)


def product(nc, out, left, right, first, last):
    (lh, ll), (rh, rl) = left, right
    nc.tensor.matmul(out, ll, rh, start=first, stop=False)
    nc.tensor.matmul(out, lh, rl, start=False, stop=False)
    return nc.tensor.matmul(out, lh, rh, start=False, stop=last)


def phase_transpose_x(nc, k, x_all):
    with ExitStack() as ctx:
        m = Core(nc, ctx)
        xn = m.sb("p0_x", [2, D])
        ps = m.ps("p0_ps", [8, BANK])
        x_loaded = [m.sem(f"p0_x_loaded{i}") for i in range(2)]
        ident_loaded = m.sem("p0_ident_loaded")
        turned = m.sem("p0_turned")
        high_done = m.sem("p0_high_done")
        low_done = m.sem("p0_low_done")
        block = ctx.enter_context(nc.Block())

        @block.sync
        def _(sp):
            sp.dma_start(k.ident[:], k.d["ident"]).then_inc(ident_loaded, 16)
            for t in range(NT):
                if t >= 2:
                    sp.wait_ge(turned, 2 * (t - 1))
                sp.dma_start(xn[:, t % 2, :], x_all(t)).then_inc(x_loaded[t % 2], 16)

        @block.tensor
        def _(pe):
            pe.wait_ge(ident_loaded, 16)
            for t in range(NT):
                pe.wait_ge(x_loaded[t % 2], 16 * (t // 2 + 1))
                for g in range(2):
                    n = 2 * t + g
                    if n >= 8:
                        pe.wait_ge(low_done, n - 7)
                    for j in range(4):
                        c = 4 * g + j
                        last = nc.tensor.transpose(ps[:, n % 8, j * P:(j + 1) * P],
                                                   xn[:, t % 2, c * P:(c + 1) * P], k.ident[:])
                    last.then_inc(turned, 1)

        @block.scalar
        def _(act):
            for n in range(2 * NT):
                act.wait_ge(turned, n + 1)
                t, g = n // 2, n % 2
                round_high(nc, k.act_h[:, 4 * g:4 * g + 4, t * P:(t + 1) * P],
                           ps[:, n % 8, :].rearrange("p (j q) -> p j q", j=4)).then_inc(high_done, 1)

        @block.vector
        def _(dve):
            for n in range(2 * NT):
                dve.wait_ge(high_done, n + 1)
                t, g = n // 2, n % 2
                at = (slice(None), slice(4 * g, 4 * g + 4), slice(t * P, (t + 1) * P))
                round_low(nc, k.act_l[at], ps[:, n % 8, :].rearrange("p (j q) -> p j q", j=4),
                          k.act_h[at]).then_inc(low_done, 1)


GLA_STEPS = ["V0", "V1", "K0", "C0", "S0", "S1", "O0", "SI", "K1", "C1", "S2", "OT0", "S3", "O1",
             "SO", "SS0", "OT1", "SS1", "SOT"]


def phase_mixer_a(nc, k):
    d = k.d
    w_in = d["w_in_a"][0].rearrange("(a p) e -> p a e", p=P)
    COLUMN = [D, 0, 2 * D, 3 * D]
    with ExitStack() as ctx:
        m = Core(nc, ctx)
        w_raw = m.sb("a_w_raw", [2, KD, P])
        w_h = m.sb("a_w_h", [2, KD, P], F32R)
        w_l = m.sb("a_w_l", [2, KD, P], F32R)
        zc = m.sb("a_zc", [T])
        ez = m.sb("a_ez", [T])
        fz = m.sb("a_fz", [T])
        kk = m.sb("a_kk", [T])
        bb = m.sb("a_bb", [T])
        qq = m.sb("a_qq", [T])
        vt = m.sb("a_vt", [T])
        sg = m.sb("a_sg", [T])
        qin = m.sb("a_qin", [T])
        kin = m.sb("a_kin", [T])
        qex = m.sb("a_qex", [T])
        kdec = m.sb("a_kdec", [T])
        decay = m.sb("a_decay", [NCH + NSEQ])
        vn = m.sb("a_vn", [NT, P])
        kdn = m.sb("a_kdn", [4, 2, P])
        kd8 = m.sb("a_kd8", [P])
        sct = m.sb("a_sct", [4, P])
        sct8 = m.sb("a_sct8", [P])
        vexp = m.sb("a_vexp", [NSEQ, P])
        qdiag = m.sb("a_qdiag", [NSEQ, P])
        st = m.sb("a_st", [9, P])
        sts = m.sb("a_sts", [NSEQ, P])
        osb = m.sb("a_osb", [4, P])
        on = m.sb("a_on", [4, P])
        og = m.sb("a_og", [T])
        ms = m.sb("a_ms", [4])
        rs = m.sb("a_rs", [4])
        mhalf = m.sb("a_mhalf", [4])
        eps = m.sb("a_eps", [4])
        mask_p = m.sb("a_mask_p", [4 * P], I32)
        mask_s = m.sb("a_mask_s", [P], I32)
        restart = m.sb("a_restart", [T])
        member = m.sb("a_member", [NSEQ])
        lbg = m.sb("a_lbg", [2, AH])
        lbe = m.sb("a_lbe", [2, AH])
        lbs = m.sb("a_lbs", [AH])
        lb = m.sb("a_lb", [AH])
        oml = m.sb("a_oml", [AH])
        ang = m.sb("a_ang", [1])
        pj = m.ps("a_pj", [2, 3, BANK])
        gb = m.ps("a_gb", [2, BANK])

        w_loaded = [m.sem(f"a_w_loaded{i}") for i in range(2)]
        wh_ready, wl_ready, proj_done = m.sem("a_wh_ready"), m.sem("a_wl_ready"), m.sem("a_proj_done")
        const_loaded = m.sem("a_const_loaded")
        states_loaded, states_stored = m.sem("a_states_loaded"), m.sem("a_states_stored")
        final_stored, og_stored = m.sem("a_final_stored"), m.sem("a_og_stored")
        prep = m.sem("a_prep")
        zeroed = m.sem("a_zeroed")
        z_out, q_out, v_out, g_out = (m.sem(f"a_{x}_out") for x in "zqvg")
        g_exp = m.sem("a_g_exp")
        g_step = m.sem("a_g_step")
        ez_done, fz_done, logf_done = m.sem("a_ez_done"), m.sem("a_fz_done"), m.sem("a_logf_done")
        key_step = m.sem("a_key_step")
        b_step = m.sem("a_b_step")
        gates = [m.sem(f"a_gate{i}") for i in range(4)]
        operand = [m.sem(f"a_operand{i}") for i in range(4)]
        pe_did = {s: m.sem(f"a_pe_{s}") for s in GLA_STEPS}
        out_of = {s: m.sem(f"a_out_{s}") for s in GLA_STEPS}
        spread_done = m.sem("a_spread")
        sq_done, ms_done, rs_step, on_ready = (m.sem("a_" + x) for x in
                                               ("sq_done", "ms_done", "rs_step", "on_ready"))
        state_step = m.sem("a_state_step")
        decay_done = m.sem("a_decay_done")
        block = ctx.enter_context(nc.Block())

        def heads(eng, body):
            body(0, True, False)
            body(1, True, True)
            with eng.Fori(2, AH - 1) as h:
                body(h, True, True)
            body(AH - 1, True, True)
            body(AH, False, True)

        def step_out(eng, s, h):
            if s in ("S0", "S1", "S2", "S3"):
                eng.wait_ge(state_step, h * NCH + (4 * int(s[1]) + 4 - NCH))
            else:
                eng.wait_ge(out_of[s], h)

        def chunks(x):
            return (x[:, 0:SEQ].rearrange("p (c l) -> p c l", l=CH),
                    x[:, SEQ:T].rearrange("p (c l) -> p c l", l=SLEN))

        @block.sync
        def _(sp):
            loads = [(mask_p, d["mask_prompt"]), (mask_s, d["mask_sample"]), (restart, d["restart"]),
                     (member, d["member"])]
            with nc.allow_non_contiguous_dma(reason="a few KB of vectors, once"):
                for row in range(2):
                    sp.dma_start(lbg[:, row, :], d["lb_gamma"][row].rearrange("(h p) -> p h", p=P)).then_inc(const_loaded, 16)
                sp.dma_start(ang[:], d["a_norm_g"].rearrange("o p -> p o")).then_inc(const_loaded, 16)
                for dst, src in loads:
                    sp.dma_start(dst[:], src).then_inc(const_loaded, 16)

            def load_w(h, c):
                if not (isinstance(h, int) and h == 0 and c < 2):
                    sp.wait_ge(w_loaded[c % 2], 16)
                    sp.wait_ge(wl_ready, h * 4 + (c - 1))
                sp.dma_start(w_raw[:, c % 2], w_in[:, :, bass.ds(h * P + COLUMN[c], P)]).then_inc(w_loaded[c % 2], 16)

            def body(h, proj, gla):
                if gla:
                    g = h - 1
                    if not (isinstance(h, int) and h == 1):
                        sp.wait_ge(states_stored, h * 16 - 16)
                    sp.dma_start(sts[:], d["state_hgrn"][0, :, bass.ds(g, 1)].rearrange("b o k v -> k (b o) v")).then_inc(states_loaded, 16)
                if proj:
                    load_w(h, 2)
                    load_w(h, 3)
                    if not (isinstance(h, int) and h == AH - 1):
                        load_w(h + 1, 0)
                        load_w(h + 1, 1)
                if gla:
                    g = h - 1
                    step_out(sp, "S3", h)
                    sp.dma_start(d["state_prompt"][0, 0, bass.ds(g, 1)].rearrange("o k v -> k (o v)"), st[:, 8]).then_inc(final_stored, 16)
                    sp.wait_ge(out_of["SS1"], h)
                    sp.dma_start(d["state_sample"][0, :, bass.ds(g, 1)].rearrange("b o k v -> k (b o) v"), sts[:]).then_inc(states_stored, 16)
                    sp.wait_ge(out_of["SOT"], h)
                    sp.dma_start(d["scratch_o"][bass.ds(g, 1)].rearrange("o p t -> p (o t)"), og[:]).then_inc(og_stored, 16)

            load_w(0, 0)
            load_w(0, 1)
            heads(sp, body)
            for s in (states_stored, final_stored, og_stored):
                sp.wait_ge(s, AH * 16)

        @block.tensor
        def _(pe):
            def tr(bank, slot, src):
                return nc.tensor.transpose(gb[:, bank, slot * P:(slot + 1) * P], src, k.ident[:])

            def blk(x, b):
                return x[:, b * P:(b + 1) * P]

            def step(i, h):
                s = GLA_STEPS[i]
                bank = i % 2
                if i >= 2:
                    step_out(pe, GLA_STEPS[i - 2], h)
                elif not (isinstance(h, int) and h == 1):
                    last = len(GLA_STEPS) - 1
                    pe.wait_ge(out_of[GLA_STEPS[last - (last - i) % 2]], h - 1)

                def out(slot, n=1):
                    return gb[:, bank, slot * P:(slot + n) * P]

                if s in ("V0", "V1"):
                    pe.wait_ge(v_out, h)
                    for j in range(4):
                        mm = tr(bank, j, blk(vt, 4 * int(s[1]) + j))
                elif s in ("K0", "K1"):
                    pe.wait_ge(operand[0], h)
                    for j in range(4):
                        mm = tr(bank, j, blk(kdec, 4 * int(s[1]) + j))
                elif s in ("C0", "C1"):
                    pe.wait_ge(operand[1], h)
                    pe.wait_ge(operand[2], h)
                    for j in range(4):
                        b = 4 * int(s[1]) + j
                        mm = nc.tensor.matmul(out(j), blk(kin, b), blk(qin, b), start=True, stop=True)
                elif s in ("S0", "S1", "S2", "S3"):
                    n = int(s[1])
                    if n % 2 == 0:
                        pe.wait_ge(out_of[f"V{n // 2}"], h)
                        pe.wait_ge(out_of[f"K{n // 2}"], h)
                    for j in range(4):
                        c = 4 * n + j
                        mm = nc.tensor.matmul(out(j), kdn[:, c // 2 % 4, c % 2], vn[:, c // 2], start=True, stop=True)
                elif s in ("O0", "O1"):
                    n = int(s[1])
                    pe.wait_ge(out_of[f"C{n}"], h)
                    step_out(pe, f"S{2 * n + 1}", h)
                    pe.wait_ge(operand[3], h)
                    for j in range(4):
                        b = 4 * n + j
                        if b == 0:
                            for half in range(2):
                                rows = slice(CH * half, CH * half + CH)
                                nc.tensor.matmul(gb[rows, bank, 0:P], sct[:, 0, rows], vn[:, 0], start=True, stop=half == 0)
                        else:
                            nc.tensor.matmul(out(j), sct[:, j], vn[:, b], start=True, stop=False)
                        for half in range(2):
                            c = 2 * b + half
                            if c == 0:
                                continue
                            rows = slice(CH * half, CH * half + CH)
                            mm = nc.tensor.matmul(gb[rows, bank, j * P:(j + 1) * P],
                                                  qex[:, c * CH:(c + 1) * CH], st[:, c % 8],
                                                  start=False, stop=True)
                elif s in ("OT0", "OT1", "SOT"):
                    n = ["OT0", "OT1", "SOT"].index(s)
                    pe.wait_ge(on_ready, h * 3 + (n - 2))
                    for j in range(4 if n < 2 else 1):
                        mm = tr(bank, j, on[:, j])
                elif s == "SI":
                    tr(bank, 0, blk(vt, NPB))
                    tr(bank, 1, blk(kdec, NPB))
                    mm = nc.tensor.matmul(out(2), blk(kin, NPB), blk(qin, NPB), start=True, stop=True)
                elif s == "SO":
                    pe.wait_ge(out_of["SI"], h)
                    pe.wait_ge(spread_done, h * 2)
                    pe.wait_ge(states_loaded, h * 16)
                    nc.tensor.matmul(out(0), sct8[:], vn[:, NPB], start=True, stop=False)
                    for i in range(NSEQ):
                        mm = nc.tensor.matmul(out(0), qdiag[:, i], sts[:, i], start=False, stop=i == NSEQ - 1)
                else:
                    n = int(s[2])
                    mm = nc.tensor.matmul(out(0, 4), kd8[:], flat(vexp[:, 4 * n:4 * n + 4]), start=True, stop=True)
                mm.then_inc(pe_did[s], 1)

            def body(h, proj, gla):
                if not proj:
                    for i in range(len(GLA_STEPS)):
                        step(i, h)
                    return
                hook = 0
                for c in range(4):
                    pe.wait_ge(wl_ready, h * 4 + c + 1)
                    if c >= 2:
                        pe.wait_ge((z_out, q_out)[c - 2], h + 1)
                    elif gla:
                        pe.wait_ge((v_out, g_out)[c], h)
                    for tg in range(NTG):
                        for kt in range(KD):
                            cols = slice(tg * TG, (tg + 1) * TG)
                            mm = product(nc, pj[:, c % 2, tg, 0:TG],
                                         (w_h[:, c % 2, kt], w_l[:, c % 2, kt]),
                                         (k.act_h[:, kt, cols], k.act_l[:, kt, cols]),
                                         kt == 0, kt == KD - 1)
                            if kt == KD - 1 and tg == NTG - 1:
                                mm.then_inc(proj_done, 1)
                            if kt % 4 == 3:
                                if gla and 2 <= hook < 2 + len(GLA_STEPS):
                                    step(hook - 2, h)
                                hook += 1

            heads(pe, body)

        @block.scalar
        def _(act):
            act.wait_ge(const_loaded, 16 * 7)
            act.wait_ge(prep, 3)
            nc.scalar.activation(flat(lbe[:]), flat(lbg[:]), ACT.Exp).then_inc(prep, 1)

            def high(h, c):
                act.wait_ge(w_loaded[c % 2], h * 32 + 16 * (c // 2 + 1))
                if not (isinstance(h, int) and h == 0 and c < 2):
                    act.wait_ge(proj_done, h * 4 + (c - 1))
                round_high(nc, w_h[:, c % 2], w_raw[:, c % 2]).then_inc(wh_ready, 1)

            def copy_o(s, n, h):
                act.wait_ge(pe_did[s], h)
                if not (isinstance(h, int) and h == 1 and n == 0):
                    act.wait_ge(on_ready, h * 3 + (n - 3))
                w = 4 * P if n < 2 else P
                nc.scalar.copy(flat(osb[:])[:, 0:w], gb[:, GLA_STEPS.index(s) % 2, 0:w]).then_inc(out_of[s], 1)

            high(0, 0)

            def body(h, proj, gla):
                if proj:
                    high(h, 1)
                if gla:
                    act.wait_ge(proj_done, h * 4)
                    if not (isinstance(h, int) and h == 1):
                        act.wait_ge(out_of["SOT"], h - 1)
                    nc.scalar.activation(sg[:].rearrange("p (a b) -> p a b", a=3), pj[:, 1, :, 0:TG], ACT.Exp, scale=-1.0).then_inc(g_exp, 1)
                    for n in range(2):
                        act.wait_ge(pe_did[f"V{n}"], h)
                        nc.scalar.copy(flat(vn[:, 4 * n:4 * n + 4]), gb[:, n]).then_inc(out_of[f"V{n}"], 1)
                if proj:
                    act.wait_ge(z_out, h + 1)
                    nc.scalar.activation(ez[:], zc[:], ACT.Exp, scale=-1.0).then_inc(ez_done, 1)
                    high(h, 2)
                if gla:
                    copy_o("O0", 0, h)
                if proj:
                    act.wait_ge(key_step, h * 3 + 3)
                    if isinstance(h, int):
                        a, b = oml[:, h:h + 1], lb[:, h:h + 1]
                    else:
                        a, b = oml[:, bass.ds(h, 1)], lb[:, bass.ds(h, 1)]
                    if isinstance(h, int) and h == 0:
                        act.wait_ge(prep, 7)
                    nc.scalar.activation(fz[:], fz[:], ACT.Ln, scale=a, bias=b).then_inc(logf_done, 1)
                    act.wait_ge(proj_done, h * 4 + 2)
                    if gla:
                        act.wait_ge(operand[2], h)
                        act.wait_ge(operand[3], h)
                    nc.scalar.copy(qq[:].rearrange("p (a b) -> p a b", a=3), pj[:, 1, :, 0:TG]).then_inc(q_out, 1)
                    high(h, 3)
                if gla:
                    copy_o("O1", 1, h)
                    copy_o("SO", 2, h)
                if proj:
                    act.wait_ge(proj_done, h * 4 + 3)
                    if gla:
                        act.wait_ge(pe_did["SI"], h)
                    nc.scalar.copy(vt[:].rearrange("p (a b) -> p a b", a=3), pj[:, 0, :, 0:TG]).then_inc(v_out, 1)
                    if not (isinstance(h, int) and h == AH - 1):
                        high(h + 1, 0)
                    act.wait_ge(b_step, h * 2 + 2)
                    for i, (dst, src, sc) in enumerate(((kdec, ez, 1.0), (kin, zc, -1.0), (qin, zc, 1.0), (qex, bb, 1.0))):
                        if gla:
                            act.wait_ge(pe_did["SO"], h)
                        nc.scalar.activation(dst[:], src[:], ACT.Exp, scale=sc).then_inc(gates[i], 1)

            heads(act, body)

        @block.gpsimd
        def _(pool):
            for x in (flat(kdn[:].rearrange("p a b c -> p (a b) c")), flat(sct[:]), sct8[:], flat(qdiag[:])):
                nc.gpsimd.memset(x, 0.0).then_inc(zeroed, 1)
            nc.gpsimd.memset(mhalf[:], -0.5).then_inc(zeroed, 1)
            nc.gpsimd.memset(eps[:], EPS).then_inc(zeroed, 1)
            pool.wait_ge(zeroed, 6)

            def body(h, proj, gla):
                if gla:
                    def norm(n):
                        w = 4 if n < 2 else 1
                        pool.wait_ge(ms_done, h * 3 + (n - 2))
                        nc.gpsimd.tensor_tensor(rs[:, 0:w], ms[:, 0:w], eps[:, 0:w], ALU.add).then_inc(rs_step, 1)
                        pool.wait_ge(rs_step, h * 6 + (2 * n - 5))
                        nc.gpsimd.tensor_tensor(rs[:, 0:w], rs[:, 0:w], mhalf[:, 0:w], ALU.pow).then_inc(rs_step, 1)
                    pool.wait_ge(zeroed, 5)
                    pool.wait_ge(operand[3], h)
                    q = qdiag[:]
                    diag = bass.AP(q.tensor, q.offset, [q.ap[0], [P + SLEN, NSEQ], [1, SLEN]])
                    nc.gpsimd.tensor_copy(diag, qex[:, SEQ:T].rearrange("p (a b) -> p a b", a=NSEQ)).then_inc(spread_done, 1)
                    norm(0)
                    pool.wait_ge(out_of["SI"], h)
                    v8 = vn[:, NPB:NPB + 1].broadcast_to([P, NSEQ, P])
                    nc.gpsimd.tensor_tensor(vexp[:], v8, member[:].rearrange("p (a o) -> p a o", o=1).broadcast_to([P, NSEQ, P]), ALU.mult).then_inc(spread_done, 1)
                    norm(1)
                    norm(2)
                if proj:
                    for i, (dst, src) in enumerate(((kdec, kk), (kin, kk))):
                        pool.wait_ge(gates[i], h + 1)
                        nc.gpsimd.tensor_tensor(dst[:], dst[:], src[:], ALU.mult).then_inc(operand[i], 1)

            pool.wait_ge(const_loaded, 16 * 7)
            heads(pool, body)

        @block.vector
        def _(dve):
            dve.wait_ge(const_loaded, 16 * 7)
            nc.vector.tensor_tensor(lbs[:], lbg[:, 0], lbg[:, 1], ALU.max).then_inc(prep, 1)
            dve.wait_ge(prep, 1)
            for row in range(2):
                nc.vector.tensor_tensor(lbg[:, row], lbg[:, row], lbs[:], ALU.subtract).then_inc(prep, 1)
            dve.wait_ge(prep, 4)
            nc.vector.tensor_tensor(lbs[:], lbe[:, 0], lbe[:, 1], ALU.add).then_inc(prep, 1)
            dve.wait_ge(prep, 5)
            nc.vector.reciprocal(lbs[:], lbs[:]).then_inc(prep, 1)
            dve.wait_ge(prep, 6)
            nc.vector.tensor_tensor(lb[:], lbe[:, 0], lbs[:], ALU.mult)
            nc.vector.tensor_tensor(oml[:], lbe[:, 1], lbs[:], ALU.mult).then_inc(prep, 1)
            dve.wait_ge(prep, 7)
            dve.wait_ge(zeroed, 6)

            def low(h, c, key=None):
                dve.wait_ge(wh_ready, h * 4 + c + 1)
                round_low(nc, w_l[:, c % 2], w_raw[:, c % 2], w_h[:, c % 2]).then_inc(wl_ready, 1)

            low(0, 0)

            def body(h, proj, gla):
                def bank(s):
                    return gb[:, GLA_STEPS.index(s) % 2]

                def keys(n):
                    dve.wait_ge(pe_did[f"K{n}"], h)
                    for half in range(2):
                        rows = slice(CH * half, CH * half + CH)
                        last = nc.vector.tensor_copy(kdn[rows, :, half], gb[rows, GLA_STEPS.index(f"K{n}") % 2].rearrange("p (j q) -> p j q", j=4))
                    last.then_inc(out_of[f"K{n}"], 1)

                def scores(n):
                    dve.wait_ge(zeroed, 5)
                    dve.wait_ge(pe_did[f"C{n}"], h)
                    nc.vector.copy_predicated(flat(sct[:]), mask_p[:], bank(f"C{n}")).then_inc(out_of[f"C{n}"], 1)

                def states(n):
                    dve.wait_ge(pe_did[f"S{n}"], h)
                    if n == 0:
                        dve.wait_ge(operand[3], h)
                    if n == 3 and not (isinstance(h, int) and h == 1):
                        dve.wait_ge(final_stored, h * 16 - 16)
                    for j in range(4):
                        c = 4 * n + j
                        to = st[:, (c + 1) % 8 if c + 1 < NCH else 8]
                        cs = bank(f"S{n}")[:, j * P:(j + 1) * P]
                        if c == 0:
                            last = nc.vector.tensor_copy(to, cs)
                        else:
                            dve.wait_ge(state_step, h * NCH + (c - NCH))
                            last = nc.vector.scalar_tensor_tensor(out=to, in0=st[:, c % 8], scalar=decay[:, c:c + 1], in1=cs, op0=ALU.mult, op1=ALU.add)
                        last.then_inc(state_step, 1)

                def square(n):
                    w = 4 if n < 2 else 1
                    dve.wait_ge(out_of[("O0", "O1", "SO")[n]], h)
                    if n == 0:
                        if not (isinstance(h, int) and h == 1):
                            dve.wait_ge(pe_did["SOT"], h - 1)
                    else:
                        dve.wait_ge(pe_did[f"OT{n - 1}"], h)
                    nc.vector.scalar_tensor_tensor(out=on[:, 0:w], in0=osb[:, 0:w], scalar=1.0 / P, in1=osb[:, 0:w], op0=ALU.mult, op1=ALU.mult).then_inc(sq_done, 1)
                    dve.wait_ge(sq_done, h * 3 + (n - 2))
                    nc.vector.tensor_reduce(ms[:, 0:w], on[:, 0:w], AX.X, ALU.add).then_inc(ms_done, 1)

                def normed(n):
                    w = 4 if n < 2 else 1
                    dve.wait_ge(rs_step, h * 6 + (2 * n - 4))
                    nc.vector.tensor_tensor(on[:, 0:w], osb[:, 0:w], rs[:, 0:w].rearrange("p (a o) -> p a o", o=1).broadcast_to([P, w, P]), ALU.mult).then_inc(on_ready, 1)

                def gated(s, n):
                    dve.wait_ge(pe_did[s], h)
                    if n == 0 and not (isinstance(h, int) and h == 1):
                        dve.wait_ge(og_stored, h * 16 - 16)
                    w = 4 * P if n < 2 else P
                    cols = slice(4 * P * n, 4 * P * n + w)
                    nc.vector.scalar_tensor_tensor(out=og[:, cols], in0=bank(s)[:, 0:w], scalar=ang[:, 0:1], in1=sg[:, cols], op0=ALU.mult, op1=ALU.mult).then_inc(out_of[s], 1)

                def sample_states(n):
                    dve.wait_ge(pe_did[f"SS{n}"], h)
                    for j in range(4):
                        i = 4 * n + j
                        last = nc.vector.scalar_tensor_tensor(out=sts[:, i], in0=sts[:, i], scalar=decay[:, NCH + i:NCH + i + 1], in1=bank(f"SS{n}")[:, j * P:(j + 1) * P], op0=ALU.mult, op1=ALU.add)
                    last.then_inc(out_of[f"SS{n}"], 1)

                if proj:
                    low(h, 1)
                if gla:
                    dve.wait_ge(g_exp, h)
                    nc.vector.tensor_scalar(sg[:], sg[:], 1.0, None, ALU.add).then_inc(g_step, 1)
                    dve.wait_ge(g_step, h * 2 - 1)
                    nc.vector.reciprocal(sg[:], sg[:]).then_inc(g_step, 1)
                    dve.wait_ge(g_step, h * 2)
                    nc.vector.tensor_tensor(sg[:].rearrange("p (a b) -> p a b", a=3), pj[:, 1, :, 0:TG], sg[:].rearrange("p (a b) -> p a b", a=3), ALU.mult).then_inc(g_out, 1)
                    dve.wait_ge(gates[3], h)
                    keys(0)
                    scores(0)
                    states(0)
                    states(1)
                if proj:
                    dve.wait_ge(proj_done, h * 4 + 1)
                    if gla:
                        dve.wait_ge(gates[2], h)
                    nc.vector.tensor_scalar(zc[:].rearrange("p (a b) -> p a b", a=3), pj[:, 0, :, 0:TG], Z_MIN, None, ALU.max).then_inc(z_out, 1)
                if gla:
                    square(0)
                if proj:
                    dve.wait_ge(ez_done, h + 1)
                    nc.vector.tensor_scalar(fz[:], ez[:], 1.0, None, ALU.add).then_inc(key_step, 1)
                    dve.wait_ge(key_step, h * 3 + 1)
                    nc.vector.reciprocal(fz[:], fz[:]).then_inc(key_step, 1)
                    low(h, 2)
                    dve.wait_ge(key_step, h * 3 + 2)
                    o1 = oml[:, h:h + 1] if isinstance(h, int) else oml[:, bass.ds(h, 1)]
                    if gla:
                        dve.wait_ge(operand[0], h)
                        dve.wait_ge(operand[1], h)
                    nc.vector.scalar_tensor_tensor(out=kk[:], in0=ez[:], scalar=o1, in1=fz[:], op0=ALU.mult, op1=ALU.mult).then_inc(key_step, 1)
                if gla:
                    dve.wait_ge(pe_did["SI"], h)
                    nc.vector.tensor_copy(vn[:, NPB], bank("SI")[:, 0:P])
                    nc.vector.tensor_copy(kd8[:], bank("SI")[:, P:2 * P])
                    nc.vector.copy_predicated(sct8[:], mask_s[:], bank("SI")[:, 2 * P:3 * P]).then_inc(out_of["SI"], 1)
                    normed(0)
                    keys(1)
                    scores(1)
                    states(2)
                    gated("OT0", 0)
                    states(3)
                if proj:
                    dve.wait_ge(logf_done, h + 1)
                    nc.vector.tensor_tensor_scan(bb[:], restart[:], fz[:], 0.0, ALU.mult, ALU.add).then_inc(b_step, 1)
                    dve.wait_ge(b_step, h * 2 + 1)
                    (bp, bs), (zp, zs), (ep, es) = chunks(bb), chunks(zc), chunks(ez)
                    for b, o, n, w in ((bp, zp, NCH, CH), (bs, zs, NSEQ, SLEN)):
                        last = nc.vector.tensor_tensor(o, b, b[:, :, w // 2:w // 2 + 1].broadcast_to([P, n, w]), ALU.subtract)
                    for b, o, n, w in ((bp, ep, NCH, CH), (bs, es, NSEQ, SLEN)):
                        last = nc.vector.tensor_tensor(o, b[:, :, w - 1:w].broadcast_to([P, n, w]), b, ALU.subtract)
                    last.then_inc(b_step, 1)
                    low(h, 3)
                if gla:
                    square(1)
                    normed(1)
                    sample_states(0)
                    gated("OT1", 1)
                    square(2)
                    normed(2)
                    sample_states(1)
                    gated("SOT", 2)
                if proj:
                    if not (isinstance(h, int) and h == AH - 1):
                        low(h + 1, 0)
                    for i, (dst, src) in enumerate(((qin, qq), (qex, qq))):
                        dve.wait_ge(gates[2 + i], h + 1)
                        if i == 1:
                            xp, xs = chunks(qex)
                            if gla:
                                dve.wait_ge(out_of["SS1"], h)
                            for at, x, w in ((slice(0, NCH), xp, CH), (slice(NCH, NCH + NSEQ), xs, SLEN)):
                                nc.vector.tensor_copy(decay[:, at].rearrange("p (c o) -> p c o", o=1), x[:, :, w - 1:w]).then_inc(decay_done, 1)
                            dve.wait_ge(decay_done, h * 2 + 2)
                        nc.vector.tensor_tensor(dst[:], dst[:], src[:], ALU.mult).then_inc(operand[2 + i], 1)

            heads(dve, body)


def token_tiles(eng, body):
    body(0, 0, False, False)
    body(1, 1, True, False)
    with eng.Fori(1, NT // 2) as pair:
        body(pair * 2, 0, True, True)
        body(pair * 2 + 1, 1, True, True)
    body(NT - 1, (NT - 1) % 2, True, True)


def tile_cols(t):
    return slice(t * P, (t + 1) * P) if isinstance(t, int) else bass.ds(t * P, P)


def phase_output(nc, k, name, nk, w, gated, residual, ln, turn, store):
    with ExitStack() as ctx:
        m = Core(nc, ctx)
        n = name
        w_raw = m.sb(n + "_w_raw", [2, D])
        w_h = m.sb(n + "_w_h", [nk, D], F32R)
        w_l = m.sb(n + "_w_l", [nk, D], F32R)
        g_raw = m.sb(n + "_g_raw", [2, nk, P])
        g_h = m.sb(n + "_g_h", [2, nk, P], F32R)
        g_l = m.sb(n + "_g_l", [2, nk, P], F32R)
        x = m.sb(n + "_x", [2, D])
        gain = m.sb(n + "_gain", [D])
        shift = m.sb(n + "_shift", [D])
        stats = m.sb(n + "_stats", [2, 6])
        mv = m.sb(n + "_mv", [2])
        rstd = m.sb(n + "_rstd", [1])
        mhalf = m.sb(n + "_mhalf", [1])
        eps = m.sb(n + "_eps", [1])
        idle = m.sb(n + "_idle", [1])
        py = m.ps(n + "_py", [2, 2, BANK])
        pt = m.ps(n + "_pt", [2, 2, BANK])

        w_loaded = [m.sem(f"{n}_w_loaded{i}") for i in range(2)]
        g_loaded = [m.sem(f"{n}_g_loaded{i}") for i in range(2)]
        x_loaded = [m.sem(f"{n}_x_loaded{i}") for i in range(2)]
        stored = [m.sem(f"{n}_stored{i}") for i in range(2)]
        (wh_ready, wl_ready, gh_ready, gl_ready, y_done, sum_done, stats_done, mv_done, rstd_step,
         norm_done, x_ready, turned, th_done, tl_done, ln_loaded, mhalf_set, gain_done) = (
            m.sem(f"{n}_{s}") for s in ("wh_ready wl_ready gh_ready gl_ready y_done sum_done stats_done mv_done "
                                        "rstd_step norm_done x_ready turned th_done tl_done ln_loaded mhalf_set gain_done").split())
        block = ctx.enter_context(nc.Block())
        w_rows = w.rearrange("(a p) e -> a p e", p=P)

        @block.sync
        def _(sp):
            def load_g(t, par, later):
                if later:
                    sp.wait_ge(gl_ready, t - 1)
                sp.dma_start(g_raw[:, par], gated(t)).then_inc(g_loaded[par], 16)

            def load_w(i):
                if i >= 2:
                    sp.wait_ge(wl_ready, i - 1)
                sp.dma_start(w_raw[:, i % 2], w_rows[i]).then_inc(w_loaded[i % 2], 16)

            load_g(0, 0, False)
            load_w(0)
            load_w(1)
            load_g(1, 1, False)
            for i in range(2, nk):
                load_w(i)

            def body(t, par, ge1, ge2):
                if ge2:
                    load_g(t, par, True)

            token_tiles(sp, body)

        @block.gpsimd
        def _(pool):
            nc.gpsimd.memset(mhalf[:], -0.5).then_inc(mhalf_set, 1)
            nc.gpsimd.memset(eps[:], EPS).then_inc(mhalf_set, 1)
            pool.wait_ge(mhalf_set, 2)
            pool.dma_start(gain[:], ln[0].partition_broadcast(P)).then_inc(ln_loaded, 16)
            pool.dma_start(shift[:], ln[1].partition_broadcast(P)).then_inc(ln_loaded, 16)

            def body(t, par, ge1, ge2):
                pool.wait_ge(mv_done, t + 1)
                nc.gpsimd.tensor_tensor(rstd[:], mv[:, 1:2], eps[:], ALU.add).then_inc(rstd_step, 1)
                pool.wait_ge(rstd_step, t * 2 + 1)
                nc.gpsimd.tensor_tensor(rstd[:], rstd[:], mhalf[:], ALU.pow).then_inc(rstd_step, 1)
                pool.wait_ge(norm_done, t + 1)
                if not ge1:
                    pool.wait_ge(ln_loaded, 32)
                nc.gpsimd.tensor_tensor(x[:, par], x[:, par], gain[:], ALU.mult).then_inc(gain_done, 1)
                pool.wait_ge(gain_done, t + 1)
                nc.gpsimd.tensor_tensor(x[:, par], x[:, par], shift[:], ALU.add).then_inc(x_ready, 1)

            token_tiles(pool, body)

        @block.tensor
        def _(pe):
            def turn_tile(t, par, later):
                pe.wait_ge(x_ready, t + 1)
                if later:
                    pe.wait_ge(tl_done, t)
                for c in range(KD):
                    last = nc.tensor.transpose(pt[:, par, c // 4, (c % 4) * P:(c % 4 + 1) * P], x[:, par, c * P:(c + 1) * P], k.ident[:])
                last.then_inc(turned, 1)

            def body(t, par, ge1, ge2):
                pe.wait_ge(gl_ready, t + 1)
                if ge2:
                    pe.wait_ge(sum_done, t - 1)
                for kt in range(nk):
                    if not ge1:
                        pe.wait_ge(wl_ready, kt + 1)
                    for half in range(2):
                        cols = slice(half * BANK, (half + 1) * BANK)
                        last = product(nc, py[:, par, half], (g_h[:, par, kt], g_l[:, par, kt]),
                                       (w_h[:, kt, cols], w_l[:, kt, cols]), kt == 0, kt == nk - 1)
                last.then_inc(y_done, 1)
                if turn and ge1:
                    turn_tile(t - 1, 1 - par, not isinstance(t, int) or t >= 3)

            token_tiles(pe, body)
            if turn:
                turn_tile(NT - 1, (NT - 1) % 2, True)

        @block.scalar
        def _(act):
            def high_g(t, par, ge2):
                act.wait_ge(g_loaded[par], (t - par) * 8 + 16)
                if ge2:
                    act.wait_ge(y_done, t - 1)
                round_high(nc, g_h[:, par], g_raw[:, par]).then_inc(gh_ready, 1)

            def load_x(t, par, ge2):
                if ge2:
                    act.wait_ge(stored[par], (t - par) * 8)
                    if turn:
                        act.wait_ge(turned, t - 1)
                act.dma_start(x[:, par], residual(t)).then_inc(x_loaded[par], 16)

            def finish(t, par):
                act.wait_ge(x_ready, t + 1)
                act.dma_start(store(t), x[:, par]).then_inc(stored[par], 16)
                if turn:
                    act.wait_ge(turned, t + 1)
                    round_high(nc, k.act_h[:, :, tile_cols(t)],
                               pt[:, par].rearrange("p a (b q) -> p (a b) q", b=4)).then_inc(th_done, 1)

            load_x(0, 0, False)
            load_x(1, 1, False)
            high_g(0, 0, False)
            for i in range(nk):
                act.wait_ge(w_loaded[i % 2], 16 * (i // 2 + 1))
                round_high(nc, w_h[:, i], w_raw[:, i % 2]).then_inc(wh_ready, 1)

            def body(t, par, ge1, ge2):
                if ge1:
                    high_g(t, par, ge2)
                    finish(t - 1, 1 - par)
                    if ge2 or t == 1:
                        if not (isinstance(t, int) and t == NT - 1):
                            load_x(t + 1, 1 - par, True)

            token_tiles(act, body)
            finish(NT - 1, (NT - 1) % 2)
            act.wait_ge(stored[0], 16 * ((NT + 1) // 2))
            act.wait_ge(stored[1], 16 * (NT // 2))

        @block.vector
        def _(dve):
            def low_g(t, par):
                dve.wait_ge(gh_ready, t + 1)
                round_low(nc, g_l[:, par], g_raw[:, par], g_h[:, par]).then_inc(gl_ready, 1)

            def turned_low(t, par):
                dve.wait_ge(th_done, t + 1)
                at = k.act_h[:, :, tile_cols(t)]
                round_low(nc, k.act_l[:, :, tile_cols(t)], pt[:, par].rearrange("p a (b q) -> p (a b) q", b=4), at).then_inc(tl_done, 1)

            dve.sem_inc(tl_done, 1)
            low_g(0, 0)
            for i in range(nk):
                dve.wait_ge(wh_ready, i + 1)
                round_low(nc, w_l[:, i], w_raw[:, i % 2], w_h[:, i]).then_inc(wl_ready, 1)

            def norm(t, par):
                dve.wait_ge(y_done, t + 1)
                dve.wait_ge(x_loaded[par], (t - par) * 8 + 16)
                nc.vector.scalar_tensor_tensor(out=x[:, par].rearrange("p (a b) -> p a b", a=2), in0=x[:, par].rearrange("p (a b) -> p a b", a=2), scalar=ALPHA, in1=py[:, par],
                                               op0=ALU.mult, op1=ALU.add).then_inc(sum_done, 1)
                dve.wait_ge(sum_done, t + 1)
                for half in range(2):
                    nc.vector.bn_stats(stats[:, half], x[:, par, half * BANK:(half + 1) * BANK]).then_inc(stats_done, 1)
                dve.wait_ge(stats_done, t * 2 + 2)
                nc.vector.memset(idle[:], 0.0)
                nc.vector.bn_aggr(mv[:], flat(stats[:])).then_inc(mv_done, 1)
                dve.wait_ge(rstd_step, t * 2 + 2)
                nc.vector.tensor_scalar(x[:, par], x[:, par], mv[:, 0:1], rstd[:, 0:1], ALU.subtract, ALU.mult).then_inc(norm_done, 1)

            def body(t, par, ge1, ge2):
                if ge1:
                    low_g(t, par)
                    norm(t - 1, 1 - par)
                    if turn:
                        turned_low(t - 1, 1 - par)

            token_tiles(dve, body)
            norm(NT - 1, (NT - 1) % 2)
            if turn:
                turned_low(NT - 1, (NT - 1) % 2)


def phase_latents(nc, k):
    d = k.d
    KV = KVL + RD
    half = RD // 2
    with ExitStack() as ctx:
        m = Core(nc, ctx)
        w_raw = m.sb("c_w_raw", [2, KV + QL])
        w_h = m.sb("c_w_h", [KD, KV + QL], F32R)
        w_l = m.sb("c_w_l", [KD, KV + QL], F32R)
        cn = m.sb("c_cn", [2, KVL])
        krn = m.sb("c_krn", [2, 2, RD])
        cqn = m.sb("c_cqn", [2, QL])
        sq = m.sb("c_sq", [QL])
        rt = m.sb("c_rt", [2, 2, half])
        cos = m.sb("c_cos", [NT, half])
        sin = m.sb("c_sin", [NT, half])
        ms = m.sb("c_ms", [2])
        inv_n = m.sb("c_inv_n", [2])
        rs = m.sb("c_rs", [2])
        mhalf = m.sb("c_mhalf", [2])
        kvg = m.sb("c_kvg", [KVL])
        qg = m.sb("c_qg", [QL])
        pkv = m.ps("c_pkv", [2, BANK])
        pq = m.ps("c_pq", [2, BANK])
        pc = m.ps("c_pc", [2, 2, BANK])

        w_loaded = [m.sem(f"c_w_loaded{i}") for i in range(2)]
        stored = [m.sem(f"c_stored{i}") for i in range(2)]
        (wh_ready, wl_ready, const_loaded, const_set, kv_done, q_done, ms_done, rs_step, c_ready, rope_step,
         kr_ready, q_ready, turned_k, turned_q, th_k, th_q, tl_k, tl_q) = (m.sem("c_" + s) for s in (
            "wh_ready wl_ready const_loaded const_set kv_done q_done ms_done rs_step c_ready rope_step "
            "kr_ready q_ready turned_k turned_q th_k th_q tl_k tl_q").split())
        block = ctx.enter_context(nc.Block())
        tiles = range(NT)

        @block.sync
        def _(sp):
            kv_rows = d["w_dkv"].rearrange("(a p) e -> a p e", p=P)
            q_rows = d["w_in_b"][0].rearrange("(a p) e -> a p e", p=P)
            for i in range(KD):
                if i >= 2:
                    sp.wait_ge(wl_ready, i - 1)
                sp.dma_start(w_raw[:, i % 2, 0:KV], kv_rows[i]).then_inc(w_loaded[i % 2], 16)
                sp.dma_start(w_raw[:, i % 2, KV:], q_rows[i, :, 0:QL]).then_inc(w_loaded[i % 2], 16)
            for t in tiles:
                ckv, kr = ((d["ckv_prompt"][0, t * P:(t + 1) * P], d["krope_prompt"][0, t * P:(t + 1) * P]) if t < NPB
                           else (d["ckv_sample"].rearrange("b l e -> (b l) e"), d["krope_sample"].rearrange("b l e -> (b l) e")))
                sp.wait_ge(c_ready, t + 1)
                sp.dma_start(ckv, cn[:, t % 2]).then_inc(stored[t % 2], 16)
                sp.wait_ge(kr_ready, t + 1)
                sp.dma_start(kr, krn[:, t % 2, 0]).then_inc(stored[t % 2], 16)
            sp.wait_ge(stored[0], 32 * ((NT + 1) // 2))
            sp.wait_ge(stored[1], 32 * (NT // 2))

        @block.gpsimd
        def _(pool):
            nc.gpsimd.memset(mhalf[:], -0.5).then_inc(const_set, 1)
            nc.gpsimd.memset(inv_n[:, 0:1], 1.0 / KVL).then_inc(const_set, 1)
            nc.gpsimd.memset(inv_n[:, 1:2], 1.0 / QL).then_inc(const_set, 1)
            pool.dma_start(cos[:].rearrange("p a b -> p (a b)"), d["cos_nat"]).then_inc(const_loaded, 16)
            pool.dma_start(sin[:].rearrange("p a b -> p (a b)"), d["sin_nat"]).then_inc(const_loaded, 16)
            pool.dma_start(kvg[:], d["kv_norm_g"].partition_broadcast(P)).then_inc(const_loaded, 16)
            pool.dma_start(qg[:], d["q_norm_g"][0].partition_broadcast(P)).then_inc(const_loaded, 16)
            pool.wait_ge(const_set, 3)
            for t in tiles:
                pool.wait_ge(ms_done, 2 * t + 2)
                if t:
                    pool.wait_ge(q_ready, t)
                nc.gpsimd.tensor_tensor(rs[:], ms[:], inv_n[:], ALU.mult).then_inc(rs_step, 1)
                pool.wait_ge(rs_step, 3 * t + 1)
                nc.gpsimd.tensor_scalar(rs[:], rs[:], 1.0, EPS, ALU.mult, ALU.add).then_inc(rs_step, 1)
                pool.wait_ge(rs_step, 3 * t + 2)
                nc.gpsimd.tensor_tensor(rs[:], rs[:], mhalf[:], ALU.pow).then_inc(rs_step, 1)

        @block.tensor
        def _(pe):
            def turn(t):
                par = t % 2
                pe.wait_ge(c_ready, t + 1)
                pe.wait_ge(kr_ready, t + 1)
                pe.wait_ge(q_ready, t + 1)
                if t >= 2:
                    pe.wait_ge(tl_k, min(t - 1, NPB))
                    pe.wait_ge(tl_q, t - 1)
                if t < NPB:
                    for c in range(2):
                        nc.tensor.transpose(pc[:, par, 0, c * P:(c + 1) * P], cn[:, par, c * P:(c + 1) * P], k.ident[:])
                    nc.tensor.transpose(pc[:, par, 0, 2 * P:3 * P], krn[:, par].rearrange("p a b -> p (a b)"), k.ident[:]).then_inc(turned_k, 1)
                for c in range(4):
                    last = nc.tensor.transpose(pc[:, par, 1, c * P:(c + 1) * P], cqn[:, par, c * P:(c + 1) * P], k.ident[:])
                last.then_inc(turned_q, 1)

            for t in tiles:
                par = t % 2
                if t >= 2:
                    pe.wait_ge(kr_ready, t - 1)
                    pe.wait_ge(c_ready, t - 1)
                    pe.wait_ge(q_ready, t - 1)
                x = [(k.act_h[:, kt, t * P:(t + 1) * P], k.act_l[:, kt, t * P:(t + 1) * P]) for kt in range(KD)]
                for kt in range(KD):
                    if t == 0:
                        pe.wait_ge(wl_ready, kt + 1)
                    last_kv = product(nc, pkv[:, par, 0:KV], x[kt], (w_h[:, kt, 0:KV], w_l[:, kt, 0:KV]), kt == 0, kt == KD - 1)
                    last = product(nc, pq[:, par], x[kt], (w_h[:, kt, KV:], w_l[:, kt, KV:]), kt == 0, kt == KD - 1)
                last.then_inc(q_done, 1)
                if t >= 1:
                    turn(t - 1)
            turn(NT - 1)

        @block.scalar
        def _(act):
            for i in range(KD):
                act.wait_ge(w_loaded[i % 2], 32 * (i // 2 + 1))
                round_high(nc, w_h[:, i], w_raw[:, i % 2]).then_inc(wh_ready, 1)

            def turned_high(t):
                par, cols = t % 2, slice(t * P, (t + 1) * P)
                if t < NPB:
                    act.wait_ge(turned_k, t + 1)
                    round_high(nc, k.ct_h[:, :, cols], pc[:, par, 0, 0:2 * P].rearrange("p (a q) -> p a q", a=2))
                    round_high(nc, k.kr_h[:, cols], pc[:, par, 0, 2 * P:3 * P]).then_inc(th_k, 1)
                act.wait_ge(turned_q, t + 1)
                round_high(nc, k.cq_h[:, :, cols], pc[:, par, 1].rearrange("p (a q) -> p a q", a=4)).then_inc(th_q, 1)

            for t in tiles:
                par = t % 2
                act.wait_ge(q_done, t + 1)
                if t:
                    act.wait_ge(rs_step, 3 * t)
                    act.wait_ge(ms_done, 2 * t)
                nc.scalar.activation(sq[:, 0:KVL], pkv[:, par, 0:KVL], ACT.Square, accum_out=ms[:, 0:1]).then_inc(ms_done, 1)
                act.wait_ge(ms_done, 2 * t + 1)
                nc.scalar.activation(sq[:], pq[:, par], ACT.Square, accum_out=ms[:, 1:2]).then_inc(ms_done, 1)
                if t:
                    turned_high(t - 1)
            turned_high(NT - 1)

        @block.vector
        def _(dve):
            for i in range(KD):
                dve.wait_ge(wh_ready, i + 1)
                round_low(nc, w_l[:, i], w_raw[:, i % 2], w_h[:, i]).then_inc(wl_ready, 1)
            dve.wait_ge(const_loaded, 64)

            def turned_low(t):
                par, cols = t % 2, slice(t * P, (t + 1) * P)
                if t < NPB:
                    dve.wait_ge(th_k, t + 1)
                    round_low(nc, k.ct_l[:, :, cols], pc[:, par, 0, 0:2 * P].rearrange("p (a q) -> p a q", a=2), k.ct_h[:, :, cols])
                    round_low(nc, k.kr_l[:, cols], pc[:, par, 0, 2 * P:3 * P], k.kr_h[:, cols]).then_inc(tl_k, 1)
                dve.wait_ge(th_q, t + 1)
                round_low(nc, k.cq_l[:, :, cols], pc[:, par, 1].rearrange("p (a q) -> p a q", a=4), k.cq_h[:, :, cols]).then_inc(tl_q, 1)

            for t in tiles:
                par = t % 2
                dve.wait_ge(ms_done, 2 * t + 2)
                if t >= 2:
                    dve.wait_ge(stored[par], 32 * (t // 2))
                    dve.wait_ge(turned_q, t - 1)
                x = pkv[:, par, KVL:KV].rearrange("p (a b) -> p a b", a=2)
                if t:
                    dve.wait_ge(kr_ready, t)
                both = lambda a: a[:, t:t + 1].broadcast_to([P, 2, half])
                nc.vector.tensor_tensor(rt[:, 0], x, both(cos), ALU.mult).then_inc(rope_step, 1)
                nc.vector.tensor_tensor(rt[:, 1], x, both(sin), ALU.mult).then_inc(rope_step, 1)
                dve.wait_ge(rope_step, 2 * t + 2)
                for copy in range(2):
                    nc.vector.tensor_tensor(krn[:, par, copy, 0:half], rt[:, 0, 0], rt[:, 1, 1], ALU.subtract)
                    last = nc.vector.tensor_tensor(krn[:, par, copy, half:], rt[:, 1, 0], rt[:, 0, 1], ALU.add)
                last.then_inc(kr_ready, 1)
                dve.wait_ge(rs_step, 3 * t + 3)
                nc.vector.scalar_tensor_tensor(out=cn[:, par], in0=pkv[:, par, 0:KVL], scalar=rs[:, 0:1], in1=kvg[:], op0=ALU.mult, op1=ALU.mult).then_inc(c_ready, 1)
                nc.vector.scalar_tensor_tensor(out=cqn[:, par], in0=pq[:, par], scalar=rs[:, 1:2], in1=qg[:], op0=ALU.mult, op1=ALU.mult).then_inc(q_ready, 1)
                if t:
                    turned_low(t - 1)
            turned_low(NT - 1)


def phase_gates(nc, k):
    d = k.d
    w_in = d["w_in_b"][0].rearrange("(a p) e -> p a e", p=P)
    with ExitStack() as ctx:
        m = Core(nc, ctx)
        w_raw = m.sb("g_w_raw", [2, KD, P])
        w_h = m.sb("g_w_h", [2, KD, P], F32R)
        w_l = m.sb("g_w_l", [2, KD, P], F32R)
        sg = m.sb("g_sg", [2, T])
        pj = m.ps("g_pj", [2, 3, BANK])
        w_loaded = [m.sem(f"g_w_loaded{i}") for i in range(2)]
        stored = [m.sem(f"g_stored{i}") for i in range(2)]
        wh_ready, wl_ready, proj_done, exp_done, step, out_done = (m.sem("g_" + s) for s in "wh_ready wl_ready proj_done exp_done step out_done".split())
        block = ctx.enter_context(nc.Block())

        def tiles(eng, body):
            body(0, 0, False)
            body(1, 1, False)
            with eng.Fori(1, HEADS // 2) as pair:
                body(pair * 2, 0, True)
                body(pair * 2 + 1, 1, True)

        def wide(x):
            return x.rearrange("p (a b) -> p a b", a=3)

        @block.sync
        def _(sp):
            def body(h, par, later):
                if later:
                    sp.wait_ge(wl_ready, h - 1)
                cols = bass.ds(h * P + QL, P)
                sp.dma_start(w_raw[:, par], w_in[:, :, cols]).then_inc(w_loaded[par], 16)
                if later:
                    store(h - 2, par)

            def store(h, par):
                sp.wait_ge(out_done, h + 1)
                sp.dma_start(d["scratch_gate"][bass.ds(h, 1)].rearrange("o p t -> p (o t)"), sg[:, par]).then_inc(stored[par], 16)

            tiles(sp, body)
            for par in range(2):
                store(HEADS - 2 + par, par)
            for par in range(2):
                sp.wait_ge(stored[par], 16 * (HEADS // 2))

        @block.tensor
        def _(pe):
            def body(h, par, later):
                pe.wait_ge(wl_ready, h + 1)
                if later:
                    pe.wait_ge(out_done, h - 1)
                for tg in range(NTG):
                    cols = slice(tg * TG, (tg + 1) * TG)
                    for kt in range(KD):
                        mm = product(nc, pj[:, par, tg, 0:TG], (w_h[:, par, kt], w_l[:, par, kt]),
                                     (k.act_h[:, kt, cols], k.act_l[:, kt, cols]), kt == 0, kt == KD - 1)
                mm.then_inc(proj_done, 1)
            tiles(pe, body)

        @block.scalar
        def _(act):
            def high(h, par, later):
                act.wait_ge(w_loaded[par], (h - par) * 8 + 16)
                if later:
                    act.wait_ge(proj_done, h - 1)
                round_high(nc, w_h[:, par], w_raw[:, par]).then_inc(wh_ready, 1)

            def silu(h, par, later):
                act.wait_ge(proj_done, h + 1)
                if later:
                    act.wait_ge(stored[par], (h - par) * 8)
                nc.scalar.activation(wide(sg[:, par]), pj[:, par, :, 0:TG], ACT.Exp, scale=-1.0).then_inc(exp_done, 1)
            high(0, 0, False)
            high(1, 1, False)

            silu(0, 0, False)
            high(2, 0, True)
            silu(1, 1, False)
            high(3, 1, True)
            with act.Fori(2, HEADS - 2, 2) as h:
                silu(h, 0, True)
                high(h + 2, 0, True)
                silu(h + 1, 1, True)
                high(h + 3, 1, True)
            silu(HEADS - 2, 0, True)
            silu(HEADS - 1, 1, True)

        @block.vector
        def _(dve):
            def low(h, par):
                dve.wait_ge(wh_ready, h + 1)
                round_low(nc, w_l[:, par], w_raw[:, par], w_h[:, par]).then_inc(wl_ready, 1)

            def silu(h, par):
                dve.wait_ge(exp_done, h + 1)
                nc.vector.tensor_scalar(sg[:, par], sg[:, par], 1.0, None, ALU.add).then_inc(step, 1)
                dve.wait_ge(step, h * 2 + 1)
                nc.vector.reciprocal(sg[:, par], sg[:, par]).then_inc(step, 1)
                dve.wait_ge(step, h * 2 + 2)
                nc.vector.tensor_tensor(wide(sg[:, par]), pj[:, par, :, 0:TG], wide(sg[:, par]), ALU.mult).then_inc(out_done, 1)
            low(0, 0)
            low(1, 1)
            with dve.Fori(0, HEADS - 2, 2) as h:
                silu(h, 0)
                low(h + 2, 0)
                silu(h + 1, 1)
                low(h + 3, 1)
            silu(HEADS - 2, 0)
            silu(HEADS - 1, 1)


PAIRS = HEADS // 2
QB = SEQ // P
GQ = 2 * P
GROUPS = SEQ // GQ
ORDER = [(0, 0), (1, 3), (0, 1), (1, 2), (1, 1), (0, 2), (1, 0), (0, 3)]
NG = len(ORDER)
UNITS = 2 * NG


def unit(u):
    return u // 4 * 2 + u % 2, u // 2 % 2


def place_of(u):
    G, half = unit(u)
    e, g = ORDER[G]
    return e, 2 * g + half, g


TSTEPS = [(u, i, min(4, 2 * place_of(u)[2] + 2 - i)) for u in range(UNITS)
          for i in range(1 - unit(u)[1], 2 * place_of(u)[2] + 2, 4)]
PROJ = ["QA0", "QA1", "QA2", "QB0", "R0", "R1", "R2", "QB1", "QB2", "UT", "KA0", "KA1", "KB0", "KB1",
        "V0", "V1", "QL", "V2", "V3"]
READS = ["QA0", "QA1", "QA2", "QB0", "R0", "QB1", "R1", "QB2", "UT", "KA0", "R2", "KA1", "KB0", "KB1",
         "V0", "V1", "QL", "V2", "V3"]
PROJ_BANK = [i % 8 for i in range(12)] + [4, 5, 6, 7, 4, 5, 6]
NP = len(PROJ)
HIGH_COUNT = {s: sum(x[0] != "R" for x in PROJ[:i + 1]) for i, s in enumerate(PROJ)}
HIGHS = HIGH_COUNT[PROJ[-1]]
STEP = {name: i for i, name in enumerate(PROJ)}
EARLY = {14: ["QA0"], 15: ["QA1"], 16: ["QA2", "QB0"]}
NE = 4
WPARTS = 4


def phase_heads(nc, k):
    d = k.d
    with ExitStack() as ctx:
        m = Core(nc, ctx)
        OUK, OUV, WW = 4 * 2 * QD, 4 * 2 * QD + 2 * GQ, 4 * 2 * QD + 4 * GQ
        w_raw = m.sb("h_w_raw", [WW])
        w_h = m.sb("h_w_h", [WW], F32R)
        w_l = m.sb("h_w_l", [WW], F32R)
        qn_h, qn_l = m.sb("h_qn_h", [2, T], F32R), m.sb("h_qn_l", [2, T], F32R)
        rq = m.sb("h_rq", [2, T], F32R)
        kt_h, kt_l = m.sb("h_kt_h", [2, SEQ], F32R), m.sb("h_kt_l", [2, SEQ], F32R)
        v_h, v_l = m.sb("h_v_h", [QB, GQ], F32R), m.sb("h_v_l", [QB, GQ], F32R)
        p = m.sb("h_p", [3, SEQ])
        PLACES = [max(2 * g + 2 for i, (e, g) in enumerate(ORDER) if i % 2 == slot) for slot in range(2)]
        pt_h = [m.sb(f"h_pt_h{i}", [n, GQ], F32R) for i, n in enumerate(PLACES)]
        pt_l = [m.sb(f"h_pt_l{i}", [n, GQ], F32R) for i, n in enumerate(PLACES)]
        cos, sin = m.sb("h_cos", [T]), m.sb("h_sin", [T])
        gate = m.sb("h_gate", [2, GQ])
        ukt = m.sb("h_ukt", [2, KVL])
        qs = m.sb("h_qs", [2, P])
        qlat = m.sb("h_qlat", [4, P])
        qr = m.sb("h_qr", [2, P])
        mx = m.sb("h_mx", [3, 1])
        rsum = m.sb("h_rsum", [3, 1])
        bank = m.ps("h_ps", [8, BANK])
        names = ("w_loaded zeroed wh_ready wl_ready table_loaded proj_done proj_high proj_out rope_step rope_sum rq_high rq_out s_done masked max_done "
                 "exp_done inv_done p_ready t_done t_high t_out pv_done o_out ql_stored qr_stored qs_ready").split()
        S = {n: m.sem("h_" + n) for n in names}
        gate_loaded = [m.sem(f"h_gate_loaded{i}") for i in range(2)]
        og_stored = [m.sem(f"h_og_stored{i}") for i in range(2)]
        block = ctx.enter_context(nc.Block())

        uq = lambda x: x[:, 0:OUK].rearrange("p (a e) -> p a e", a=4)
        uk = lambda x: x[:, OUK:OUV].rearrange("p (a e) -> p a e", a=2)
        uv = lambda x: x[:, OUV:WW].rearrange("p (a e) -> p a e", a=2)

        def view(x, n):
            return x[:, 0, 0:n] if n <= BANK else x[:, :, 0:n // 2]

        def scores_of(u):
            slot = 2 * (u % 2)
            return view(bank[:, slot:slot + 2], P * (place_of(u)[1] + 1))

        def weights_of(u):
            n = P * (place_of(u)[1] + 1)
            x = p[:, u % 3, 0:n]
            return x if n <= BANK else x.rearrange("p (a b) -> p a b", a=2)

        def last_turn(u):
            return max(i for i, (uu, _, _) in enumerate(TSTEPS) if uu == u) + 1

        def piece(x, i):
            return x[:, WW // WPARTS * i:WW // WPARTS * (i + 1)]

        flat_p = p[:].rearrange("p a b -> p (a b)")

        def rope_part(tg, i, n=1):
            at = (tg % 2) * 4 * TG + i * TG
            return flat_p[:, at:at + n * TG]

        def rope_sums(tg):
            return rope_part(tg, 2, 2)[0:RD].rearrange("p (a b) -> p a b", a=2)

        def pairs(eng, body):
            body(0, True, False)
            with eng.Fori(1, PAIRS - 1) as pr:
                body(pr, False, False)
            body(PAIRS - 1, False, True)

        @block.sync
        def _(sp):
            sp.dma_start(cos[:], d["cos_t"]).then_inc(S["table_loaded"], 16)
            sp.dma_start(sin[:], d["sin_t"]).then_inc(S["table_loaded"], 16)

            def load_w(pr, first):
                if not first:
                    sp.wait_ge(S["wl_ready"], pr * WPARTS)
                    sp.wait_ge(S["proj_done"], pr * NP + (STEP["UT"] + 1 - NP))
                for e in range(2):
                    for at, col, w in ((e * NOPE, 0, NOPE), (2 * NOPE + e * RD, NOPE, RD)):
                        sp.dma_start(uq(w_raw)[:, :, at:at + w], d["w_uq"][0].rearrange("(a p) e -> p a e", p=P)[:, :, bass.ds(pr * (2 * QD) + (e * QD + col), w)]).then_inc(S["w_loaded"], 16)
                for dst, src in ((uk, "w_uk"), (uv, "w_uv")):
                    sp.dma_start(dst(w_raw), d[src].rearrange("(a p) h n -> p a (h n)", p=P)[:, :, bass.ds(pr * GQ, GQ)]).then_inc(S["w_loaded"], 16)

            def rows(x, pr, e):
                return d[x].rearrange("(r e) p t -> r e p t", e=2)[bass.ds(pr, 1), e].rearrange("o p t -> p (o t)")

            def load_gate(pr, g, first):
                if not (first and g < 2):
                    sp.wait_ge(og_stored[g % 2], pr * 64 + 16 * (g // 2))
                e, qg = ORDER[g]
                sp.dma_start(gate[:, g % 2], rows("scratch_gate", pr, e)[:, GQ * qg:GQ * qg + GQ]).then_inc(gate_loaded[g % 2], 16)

            def body(pr, first, last):
                load_gate(pr, 0, first)
                load_gate(pr, 1, first)
                sp.wait_ge(S["proj_out"], pr * NP + NP)
                sp.dma_start(d["scratch_ql"][bass.ds(pr, 1)].rearrange("o p t -> p (o t)"), flat(qlat[:])).then_inc(S["ql_stored"], 16)
                sp.dma_start(d["scratch_qr"][bass.ds(pr, 1)].rearrange("o p t -> p (o t)"), flat(qr[0:RD])).then_inc(S["qr_stored"], 16)
                if not last:
                    load_w(pr + 1, False)
                for g in range(NG):
                    sp.wait_ge(S["o_out"], pr * 8 + g + 1)
                    e, qg = ORDER[g]
                    sp.dma_start(rows("scratch_og", pr, e)[:, GQ * qg:GQ * qg + GQ], gate[:, g % 2]).then_inc(og_stored[g % 2], 16)
                    if g + 2 < NG:
                        load_gate(pr, g + 2, False)

            load_w(0, True)
            pairs(sp, body)
            sp.wait_ge(S["ql_stored"], 16 * PAIRS)
            sp.wait_ge(S["qr_stored"], 16 * PAIRS)
            for s in og_stored:
                sp.wait_ge(s, 64 * PAIRS)

        @block.gpsimd
        def _(pool):
            def body(pr, first, last):
                for tg in range(NTG):
                    pool.wait_ge(S["rope_step"], pr * 3 + tg + 1)
                    for e in range(2):
                        rows = slice(e * RD, (e + 1) * RD)
                        last_op = nc.gpsimd.tensor_tensor(rope_sums(tg)[:, e], rope_part(tg, 0)[rows], rope_part(tg, 1)[rows], ALU.add)
                    last_op.then_inc(S["rope_sum"], 1)
            pairs(pool, body)

        @block.tensor
        def _(pe):
            def W(v, a, c):
                return v(w_h)[:, a, c], v(w_l)[:, a, c]

            def proj(pr, s, first):
                i, b = STEP[s], PROJ_BANK[STEP[s]]
                earlier = [j for j in range(i) if PROJ_BANK[j] == b]
                if s == "QA0":
                    pe.wait_ge(S["wl_ready"], pr * WPARTS + WPARTS)
                if earlier:
                    pe.wait_ge(S["proj_out"], pr * NP + earlier[-1] + 1)
                elif not first:
                    if b < 4:
                        pe.wait_ge(S["exp_done"], pr * UNITS - 1 + b // 2)
                    elif b < 6:
                        pe.wait_ge(S["t_out"], pr * len(TSTEPS))
                    else:
                        pe.wait_ge(S["o_out"], pr * NG)
                if s == "QL":
                    pe.wait_ge(S["qs_ready"], pr * 2 + 2)
                    for j in range(4):
                        e, a = j // 2, j % 2
                        mm = nc.tensor.matmul(bank[:, b, j * P:j * P + P], ukt[:, e, a * P:a * P + P], qs[:, e], start=True, stop=True)
                elif s[0] in "QR":
                    tg = int(s[-1])
                    cols = slice(tg * TG, tg * TG + TG)
                    for a in range(4):
                        if s[0] == "R":
                            left = W(uq, a, slice(2 * NOPE, 2 * QD))
                        else:
                            o = NOPE * (s[1] == "B")
                            left = W(uq, a, slice(o, o + NOPE))
                        mm = product(nc, bank[:, b, 0:TG], left, (k.cq_h[:, a, cols], k.cq_l[:, a, cols]), a == 0, a == 3)
                elif s == "UT":
                    for j in range(4):
                        e, a = j // 2, j % 2
                        mm = nc.tensor.transpose(bank[:, b, j * P:j * P + P], uk(w_raw)[:, a, e * P:e * P + P], k.ident[:])
                elif s[0] == "K":
                    o, cols = P * (s[1] == "B"), slice(BANK * int(s[2]), BANK * int(s[2]) + BANK)
                    for a in range(2):
                        mm = product(nc, bank[:, b], W(uk, a, slice(o, o + P)), (k.ct_h[:, a, cols], k.ct_l[:, a, cols]), a == 0, a == 1)
                else:
                    for j in range(2):
                        cols = slice((2 * int(s[1]) + j) * P, (2 * int(s[1]) + j) * P + P)
                        for a in range(2):
                            mm = product(nc, bank[:, b, j * GQ:j * GQ + GQ], (k.ct_h[:, a, cols], k.ct_l[:, a, cols]), W(uv, a, slice(0, GQ)), a == 0, a == 1)
                mm.then_inc(S["proj_done"], 1)

            def scores(pr, u):
                e, qb, g = place_of(u)
                if u < 2:
                    pe.wait_ge(S["proj_out"], pr * NP + STEP[("KA1", "KB1")[u]] + 1)
                    pe.wait_ge(S["rq_out"], pr * 3 + (1, 3)[u])
                else:
                    pe.wait_ge(S["exp_done"], pr * UNITS + u - 1)
                q = slice(qb * P, qb * P + P)
                n = max(GQ, P * (qb + 1))
                w = n if n <= BANK else n // 2
                for c in range(n // w):
                    out, kc = bank[:, 2 * (u % 2) + c, 0:w], slice(c * w, c * w + w)
                    product(nc, out, (qn_h[:, e, q], qn_l[:, e, q]), (kt_h[:, e, kc], kt_l[:, e, kc]), True, False)
                    nc.tensor.matmul(out, rq[:, e, q], k.kr_l[:, kc], start=False, stop=False)
                    mm = nc.tensor.matmul(out, rq[:, e, q], k.kr_h[:, kc], start=False, stop=True)
                mm.then_inc(S["s_done"], 1)

            def turn(pr, u):
                e, qb, g = place_of(u)
                pe.wait_ge(S["p_ready"], pr * UNITS + u + 1)
                for i, (uu, place, w) in enumerate(TSTEPS):
                    if uu != u:
                        continue
                    if i >= 2:
                        pe.wait_ge(S["t_out"], pr * len(TSTEPS) + i - 1)
                    else:
                        pe.wait_ge(S["proj_out"], pr * NP + STEP[("QL", "V2")[i]] + 1)
                    for j in range(w):
                        key = 2 * g + 1 - (place + j)
                        mm = nc.tensor.transpose(bank[:, 4 + i % 2, j * P:j * P + P], p[:, u % 3, key * P:(key + 1) * P], k.ident[:])
                    mm.then_inc(S["t_done"], 1)

            def values(pr, G):
                e, g = ORDER[G]
                pe.wait_ge(S["t_out"], pr * len(TSTEPS) + last_turn(G // 2 * 4 + 2 + G % 2))
                if G == 0:
                    pe.wait_ge(S["proj_out"], pr * NP + NP)
                if G >= 2:
                    pe.wait_ge(S["o_out"], pr * NG + G - 1)
                nb = 2 * (g + 1)
                for i in range(nb):
                    b, cols = nb - 1 - i, slice(e * P, e * P + P)
                    mm = product(nc, bank[:, 6 + G % 2, 0:GQ], (v_h[:, b, cols], v_l[:, b, cols]),
                                 (pt_h[G % 2][:, i], pt_l[G % 2][:, i]), i == 0, i == nb - 1)
                mm.then_inc(S["pv_done"], 1)

            pe.wait_ge(S["table_loaded"], 32)
            pe.wait_ge(S["zeroed"], 4)
            for s in PROJ[:NE]:
                proj(0, s, True)

            def body(pr, first, last):
                for s in PROJ[NE:]:
                    if s in ("V0", "V1"):
                        scores(pr, int(s[1]))
                    proj(pr, s, first)
                for u in range(UNITS):
                    if u + 2 < UNITS:
                        scores(pr, u + 2)
                    if u >= 4 and u % 4 < 2:
                        values(pr, u // 4 * 2 - 2 + u % 2)
                    if u in EARLY and not last:
                        for s in EARLY[u]:
                            proj(pr + 1, s, False)
                    turn(pr, u)
                values(pr, NG - 2)
                if not last:
                    for s in EARLY[UNITS]:
                        proj(pr + 1, s, False)
                values(pr, NG - 1)
            pairs(pe, body)

        @block.scalar
        def _(act):
            def split(pr, i):
                if i == 0:
                    act.wait_ge(S["w_loaded"], pr * 96 + 96)
                    if not (isinstance(pr, int) and pr == 0):
                        act.wait_ge(S["proj_done"], pr * NP)
                round_high(nc, piece(w_h, i), piece(w_raw, i)).then_inc(S["wh_ready"], 1)

            def proj(pr, s, first):
                i, b = STEP[s], bank[:, PROJ_BANK[STEP[s]]]
                if s[0] == "R":
                    tg = int(s[1])
                    act.wait_ge(S["rope_sum"], pr * 3 + tg + 1)
                    if tg == 2:
                        if not first:
                            act.wait_ge(S["qr_stored"], pr * 16)
                        nc.scalar.copy(qr[0:RD], rope_sums(tg)[:, :, SEQ - 2 * TG:TG])
                    nc.scalar.activation(rq[0:RD, :, tg * TG:tg * TG + TG], rope_sums(tg), ACT.Identity, scale=SCALE).then_inc(S["rq_high"], 1)
                    return
                act.wait_ge(S["proj_done"], pr * NP + i + 1)
                if s == "UT":
                    nc.scalar.copy(flat(ukt[:]), b).then_inc(S["proj_high"], 1)
                elif s == "QL":
                    if not first:
                        act.wait_ge(S["ql_stored"], pr * 16)
                    nc.scalar.copy(flat(qlat[:]), b).then_inc(S["proj_high"], 1)
                elif s[0] == "Q":
                    e, tg = "AB".index(s[1]), int(s[2])
                    if tg == 2:
                        nc.scalar.copy(qs[:, e], b[:, SEQ - 2 * TG:TG]).then_inc(S["qs_ready"], 1)
                    nc.scalar.activation(qn_h[:, e, tg * TG:tg * TG + TG], b[:, 0:TG], ACT.Identity, scale=SCALE).then_inc(S["proj_high"], 1)
                elif s[0] == "K":
                    e, c = "AB".index(s[1]), int(s[2])
                    round_high(nc, kt_h[:, e, c * BANK:(c + 1) * BANK], b).then_inc(S["proj_high"], 1)
                else:
                    c = int(s[1])
                    round_high(nc, flat(v_h[:, 2 * c:2 * c + 2]), b).then_inc(S["proj_high"], 1)

            def exp(pr, u):
                act.wait_ge(S["max_done"], pr * UNITS + u + 1)
                if u >= 3:
                    act.wait_ge(S["t_done"], pr * len(TSTEPS) + last_turn(u - 3))
                nc.scalar.activation(weights_of(u), scores_of(u), ACT.Exp, bias=mx[:, u % 3], accum_out=rsum[:, u % 3]).then_inc(S["exp_done"], 1)

            def normed(pr, u):
                act.wait_ge(S["inv_done"], pr * UNITS + u + 1)
                nc.scalar.activation(weights_of(u), weights_of(u), ACT.Identity, scale=rsum[:, u % 3]).then_inc(S["p_ready"], 1)

            def turned(pr, u):
                for i, (uu, place, w) in enumerate(TSTEPS):
                    if uu != u:
                        continue
                    act.wait_ge(S["t_done"], pr * len(TSTEPS) + i + 1)
                    G, half = unit(u)
                    if half == 0 and G >= 2 and place == 1:
                        act.wait_ge(S["pv_done"], pr * NG + G - 1)
                    q = slice(half * P, half * P + P)
                    round_high(nc, pt_h[G % 2][:, place:place + w, q], bank[:, 4 + i % 2, 0:w * P].rearrange("p (a q) -> p a q", a=w)).then_inc(S["t_high"], 1)

            for i in range(WPARTS):
                split(0, i)
            for x in (pt_h[0], pt_h[1], pt_l[0], pt_l[1]):
                nc.scalar.activation(x[:, 0, 0:P], k.ident[:], ACT.Identity, scale=0.0).then_inc(S["zeroed"], 1)
            for s in PROJ[:NE]:
                proj(0, s, True)

            def body(pr, first, last):
                for s in READS[NE:]:
                    if s == "V0":
                        exp(pr, 0)
                    if s == "V1":
                        normed(pr, 0)
                        exp(pr, 1)
                    proj(pr, s, first)
                for u in range(UNITS):
                    if u + 1 < UNITS:
                        normed(pr, u + 1)
                    if u in EARLY and not last:
                        for s in EARLY[u]:
                            proj(pr + 1, s, False)
                    turned(pr, u)
                    if u + 2 < UNITS:
                        exp(pr, u + 2)
                    if 6 <= u < 6 + WPARTS and not last:
                        split(pr + 1, u - 6)
                if not last:
                    for s in EARLY[UNITS]:
                        proj(pr + 1, s, False)
            pairs(act, body)

        @block.vector
        def _(dve):
            dve.wait_ge(S["table_loaded"], 32)

            def split(pr, i):
                dve.wait_ge(S["wh_ready"], pr * WPARTS + i + 1)
                round_low(nc, piece(w_l, i), piece(w_raw, i), piece(w_h, i)).then_inc(S["wl_ready"], 1)

            def rope(pr, tg):
                i = STEP[f"R{tg}"]
                dve.wait_ge(S["proj_done"], pr * NP + i + 1)
                x = bank[:, PROJ_BANK[i], 0:TG]
                cols = slice(tg * TG, tg * TG + TG)
                nc.vector.tensor_tensor(rope_part(tg, 0), x, cos[:, cols], ALU.mult)
                for a, b in ((0, 32), (32, 0), (64, 96), (96, 64)):
                    last = nc.vector.tensor_tensor(rope_part(tg, 1)[b:b + 32], x[a:a + 32], sin[a:a + 32, cols], ALU.mult)
                last.then_inc(S["rope_step"], 1)
                dve.wait_ge(S["rope_step"], pr * 3 + tg + 1)
                dve.sem_inc(S["proj_out"], 1)

            def rope_low(pr, tg):
                dve.wait_ge(S["rq_high"], pr * 3 + tg + 1)
                c = slice(tg * TG, tg * TG + TG)
                scaled_low(rq[RD:P, :, c], rope_sums(tg), rq[0:RD, :, c]).then_inc(S["rq_out"], 1)

            def scaled_low(out, x, high):
                return nc.vector.scalar_tensor_tensor(out=out, in0=x, scalar=SCALE, in1=high.bitcast(F32), op0=ALU.mult, op1=ALU.subtract)

            def proj(pr, s):
                i, b = STEP[s], bank[:, PROJ_BANK[STEP[s]]]
                dve.wait_ge(S["proj_high"], pr * HIGHS + HIGH_COUNT[s])
                if s in ("UT", "QL"):
                    dve.sem_inc(S["proj_out"], 1)
                elif s[0] == "Q":
                    e, tg = "AB".index(s[1]), int(s[2])
                    at = (slice(None), e, slice(tg * TG, tg * TG + TG))
                    scaled_low(qn_l[at], b[:, 0:TG], qn_h[at]).then_inc(S["proj_out"], 1)
                elif s[0] == "K":
                    e, c = "AB".index(s[1]), int(s[2])
                    at = (slice(None), e, slice(c * BANK, (c + 1) * BANK))
                    round_low(nc, kt_l[at], b, kt_h[at]).then_inc(S["proj_out"], 1)
                else:
                    c = int(s[1])
                    round_low(nc, flat(v_l[:, 2 * c:2 * c + 2]), b, flat(v_h[:, 2 * c:2 * c + 2])).then_inc(S["proj_out"], 1)

            def largest(pr, u):
                dve.wait_ge(S["s_done"], pr * UNITS + u + 1)
                n = P * (place_of(u)[1] + 1)
                b, end = (0, n) if n <= BANK else (1, n // 2)
                nc.vector.memset(bank[0:CH, 2 * (u % 2) + b, end - CH:end], MASKED).then_inc(S["masked"], 1)
                dve.wait_ge(S["masked"], pr * UNITS + u + 1)
                if u >= 3:
                    dve.wait_ge(S["exp_done"], pr * UNITS + u - 2)
                nc.vector.tensor_reduce(mx[:, u % 3], scores_of(u), AX.X if n <= BANK else AX.XY, ALU.max, negate=True).then_inc(S["max_done"], 1)

            def inverted(pr, u):
                dve.wait_ge(S["exp_done"], pr * UNITS + u + 1)
                nc.vector.reciprocal(rsum[:, u % 3], rsum[:, u % 3]).then_inc(S["inv_done"], 1)

            def turned(pr, u):
                for i, (uu, place, w) in enumerate(TSTEPS):
                    if uu != u:
                        continue
                    dve.wait_ge(S["t_high"], pr * len(TSTEPS) + i + 1)
                    G, half = unit(u)
                    at = (slice(None), slice(place, place + w), slice(half * P, half * P + P))
                    round_low(nc, pt_l[G % 2][at], bank[:, 4 + i % 2, 0:w * P].rearrange("p (a q) -> p a q", a=w), pt_h[G % 2][at]).then_inc(S["t_out"], 1)

            def gated(pr, G):
                dve.wait_ge(S["pv_done"], pr * NG + G + 1)
                dve.wait_ge(gate_loaded[G % 2], pr * 64 + 16 * (G // 2) + 16)
                nc.vector.tensor_tensor(gate[:, G % 2], bank[:, 6 + G % 2, 0:GQ], gate[:, G % 2], ALU.mult).then_inc(S["o_out"], 1)

            for i in range(WPARTS):
                split(0, i)
            for s in PROJ[:NE]:
                proj(0, s)

            def body(pr, first, last):
                rope(pr, 0)
                rope(pr, 1)
                rope_low(pr, 0)
                dve.wait_ge(S["rq_out"], pr * 3 + 1)
                rope(pr, 2)
                for s in READS[NE + 1:]:
                    if s[0] == "R":
                        rope_low(pr, int(s[1]))
                        continue
                    if s == "V0":
                        largest(pr, 0)
                    if s == "V1":
                        inverted(pr, 0)
                        largest(pr, 1)
                    proj(pr, s)
                for u in range(UNITS):
                    if u + 1 < UNITS:
                        inverted(pr, u + 1)
                    if u + 2 < UNITS:
                        largest(pr, u + 2)
                    if u >= 4 and u % 4 < 2:
                        gated(pr, u // 4 * 2 - 2 + u % 2)
                    if u in EARLY and not last:
                        for s in EARLY[u]:
                            proj(pr + 1, s)
                    turned(pr, u)
                    if 6 <= u < 6 + WPARTS and not last:
                        split(pr + 1, u - 6)
                gated(pr, NG - 2)
                if not last:
                    for s in EARLY[UNITS]:
                        proj(pr + 1, s)
                gated(pr, NG - 1)
            pairs(dve, body)


KB = PAST // P
KS = PAST + SLEN
KC = 352
KPAD = 3 * KC
QS = HEADS * SLEN
TURNS, PTURNS = 7, 5


def phase_samples(nc, k):
    d = k.d
    with ExitStack() as ctx:
        m = Core(nc, ctx)
        ql_raw = m.sb("s_ql_raw", [HEADS, 2, P])
        qr_raw = m.sb("s_qr_raw", [HEADS, P])
        q_h, q_l = m.sb("s_q_h", [2, 2, QS], F32R), m.sb("s_q_l", [2, 2, QS], F32R)
        rq = m.sb("s_rq", [2, QS], F32R)
        c_raw = m.sb("s_c_raw", [2, KB + 1, KVL])
        kr_raw = m.sb("s_kr_raw", [2, KB + 1, 2, RD])
        c_h, c_l = m.sb("s_c_h", [KB + 1, KVL], F32R), m.sb("s_c_l", [KB + 1, KVL], F32R)
        ct_h, ct_l = m.sb("s_ct_h", [2, KPAD], F32R), m.sb("s_ct_l", [2, KPAD], F32R)
        kt_h, kt_l = m.sb("s_kt_h", [KPAD], F32R), m.sb("s_kt_l", [KPAD], F32R)
        p = m.sb("s_p", [2, KPAD])
        pt_h, pt_l = m.sb("s_pt_h", [KB + 1, QS], F32R), m.sb("s_pt_l", [KB + 1, QS], F32R)
        olat = m.sb("s_olat", [2, HEADS, P])
        uv = m.sb("s_uv", [2, HEADS * DV])
        gate = m.sb("s_gate", [HEADS, P])
        mx = m.sb("s_mx", [2, 1])
        rsum = m.sb("s_rsum", [2, 1])
        bank = m.ps("s_ps", [8, BANK])
        names = ("q_loaded uv_loaded zeroed qh_ready ql_ready s_done masked max_step exp_done inv_step p_ready t_done t_high t_out "
                 "o_done o_out ch_ready cl_ready uv_done uv_out og_stored").split()
        S = {n: m.sem("s_" + n) for n in names}
        raw_loaded = [m.sem(f"s_raw_loaded{i}") for i in range(2)]
        block = ctx.enter_context(nc.Block())

        def turn_base(i):
            return 0 if isinstance(i, int) and i == 0 else i * (TURNS + PTURNS) - PTURNS

        def weight_base(i, last):
            return i * (TURNS + PTURNS) + (TURNS if last else 2 * TURNS)

        def parity(base, par):
            return base % 2 if isinstance(base, int) else par

        def seqs(eng, body):
            body(0, 0, False)
            body(1, 1, False)
            with eng.Fori(1, NSEQ // 2 - 1) as pair:
                body(pair * 2, 0, False)
                body(pair * 2 + 1, 1, False)
            body(NSEQ - 2, 0, False)
            body(NSEQ - 1, 1, True)

        def step_of_keys(j):
            return [("c", 0, 0, 4), ("c", 0, 4, 4), ("c", 1, 0, 4), ("c", 1, 4, 4), ("kr", 0, 0, 4), ("kr", 0, 4, 4), ("new", 0, 8, 1)][j]

        @block.sync
        def _(sp):
            sp.dma_start(ql_raw[:].rearrange("p (r e) a t -> p r (e a t)", e=2), d["scratch_ql"].rearrange("r p t -> p r t")).then_inc(S["q_loaded"], 16)
            sp.dma_start(qr_raw[0:RD].rearrange("p (r e) t -> p r (e t)", e=2), d["scratch_qr"].rearrange("r p t -> p r t")).then_inc(S["q_loaded"], 16)
            sp.wait_ge(S["zeroed"], 4)

            def body(i, par, last):
                if not (isinstance(i, int) and i < 2):
                    sp.wait_ge(S["cl_ready"], i - 1)
                    sp.wait_ge(S["t_done"], i * (TURNS + PTURNS) + (TURNS - PTURNS - 2 * (TURNS + PTURNS)))
                row = lambda x: d[x][bass.ds(i, 1)].rearrange("o s e -> (o s) e")
                loads = [(c_raw[:, par, 0:KB], row("cache_ckv").rearrange("(j p) e -> p j e", p=P)),
                         (c_raw[0:SLEN, par, KB], row("ckv_sample"))]
                for copy in range(2):
                    loads += [(kr_raw[:, par, 0:KB, copy], row("cache_krope").rearrange("(j p) e -> p j e", p=P)),
                              (kr_raw[0:SLEN, par, KB, copy], row("krope_sample"))]
                for dst, src in loads:
                    sp.dma_start(dst, src).then_inc(raw_loaded[par], 16)
            seqs(sp, body)
            sp.dma_start(uv[:], d["w_uv"].rearrange("(a p) h n -> p a (h n)", p=P)).then_inc(S["uv_loaded"], 16)
            sp.dma_start(gate[:], d["scratch_gate"][:, :, SEQ:T].rearrange("h p t -> p h t")).then_inc(S["uv_loaded"], 16)
            for j in range(4):
                sp.wait_ge(S["uv_out"], j + 1)
                sp.dma_start(d["scratch_og"][4 * j:4 * j + 4, :, SEQ:T].rearrange("h p t -> p h t"), gate[:, 4 * j:4 * j + 4]).then_inc(S["og_stored"], 16)
            sp.wait_ge(S["og_stored"], 64)

        @block.gpsimd
        def _(pool):
            for x in (c_raw[:, 0, KB], c_raw[:, 1, KB], flat(kr_raw[:, 0, KB:KB + 1].rearrange("p o a b -> p o (a b)")), flat(kr_raw[:, 1, KB:KB + 1].rearrange("p o a b -> p o (a b)"))):
                nc.gpsimd.memset(x, 0.0).then_inc(S["zeroed"], 1)
            for x in (ct_h[:, :, KS:], ct_l[:, :, KS:], kt_h[:, KS:], kt_l[:, KS:], pt_h[:, KB], pt_l[:, KB]):
                nc.gpsimd.memset(x.bitcast(F32), 0.0).then_inc(S["zeroed"], 1)

        @block.tensor
        def _(pe):
            def turn_keys(i, par):
                pe.wait_ge(raw_loaded[par], (i - par) * 48 + 96)
                base = turn_base(i)
                for j in range(TURNS):
                    b = bank[:, 6 + (parity(base, 1) + j) % 2]
                    if not (isinstance(base, int) and base + j < 2):
                        pe.wait_ge(S["zeroed"], 10)
                        pe.wait_ge(S["t_out"], base + (j - 1))
                    what, a, s0, n = step_of_keys(j)
                    if what == "new":
                        for x in range(2):
                            nc.tensor.transpose(b[:, x * P:x * P + SLEN], c_raw[0:SLEN, par, KB, x * P:x * P + P], k.ident[0:SLEN, 0:SLEN])
                        mm = nc.tensor.transpose(b[:, 2 * P:2 * P + SLEN], kr_raw[0:SLEN, par, KB].rearrange("p a b -> p (a b)"), k.ident[0:SLEN, 0:SLEN])
                    else:
                        for x in range(n):
                            src = c_raw[:, par, s0 + x, a * P:a * P + P] if what == "c" else kr_raw[:, par, s0 + x].rearrange("p a b -> p (a b)")
                            mm = nc.tensor.transpose(b[:, x * P:x * P + P], src, k.ident[:])
                    mm.then_inc(S["t_done"], 1)

            def scores(i, par, qt, first):
                if qt == 0:
                    pe.wait_ge(S["ql_ready"], i + 1)
                    pe.wait_ge(S["t_out"], turn_base(i) + TURNS)
                    if not first:
                        pe.wait_ge(S["o_out"], i)
                if not first:
                    pe.wait_ge(S["exp_done"], i * 2 - 1 + qt)
                q = slice(qt * P, qt * P + P)
                for c in range(3):
                    out, kc = bank[:, 3 * qt + c, 0:KC], slice(c * KC, (c + 1) * KC)
                    for a in range(2):
                        product(nc, out, (q_h[:, par, a, q], q_l[:, par, a, q]), (ct_h[:, a, kc], ct_l[:, a, kc]), a == 0, False)
                    nc.tensor.matmul(out, rq[:, par, q], kt_l[:, kc], start=False, stop=False)
                    mm = nc.tensor.matmul(out, rq[:, par, q], kt_h[:, kc], start=False, stop=True)
                mm.then_inc(S["s_done"], 1)

            def turn_weights(i, last):
                base = weight_base(i, last)
                for j in range(PTURNS):
                    b = bank[:, 6 + (parity(base, 0) + j) % 2]
                    pe.wait_ge(S["t_out"], base + (j - 1))
                    if j in (0, 2, 4):
                        pe.wait_ge(S["p_ready"], i * 2 + min(j // 2, 1) + 1)
                    if j < 4:
                        for x in range(4):
                            s = (4 * (j % 2) + x) * P
                            mm = nc.tensor.transpose(b[:, x * P:x * P + P], p[:, j // 2, s:s + P], k.ident[:])
                    else:
                        for x in range(2):
                            mm = nc.tensor.transpose(b[0:SLEN, x * P:x * P + P], p[:, x, PAST:KS], k.ident[:])
                    mm.then_inc(S["t_done"], 1)

            def values(i, last):
                pe.wait_ge(S["t_out"], weight_base(i, last) + PTURNS)
                pe.wait_ge(S["cl_ready"], i + 1)
                for a in range(2):
                    for s in range(KB + 1):
                        mm = product(nc, bank[:, 0, a * QS:a * QS + QS], (c_h[:, s, a * P:a * P + P], c_l[:, s, a * P:a * P + P]),
                                     (pt_h[:, s], pt_l[:, s]), s == 0, s == KB)
                mm.then_inc(S["o_done"], 1)

            pe.wait_ge(S["zeroed"], 10)
            turn_keys(0, 0)

            def body(i, par, last):
                first = isinstance(i, int) and i == 0
                scores(i, par, 0, first)
                scores(i, par, 1, first)
                if not last:
                    turn_keys(i + 1, 1 - par)
                turn_weights(i, last)
                values(i, last)
            seqs(pe, body)
            pe.wait_ge(S["uv_loaded"], 32)
            pe.wait_ge(S["o_out"], NSEQ)
            for h in range(HEADS):
                for a in range(2):
                    mm = nc.tensor.matmul(bank[:, h // 4, h % 4 * P:h % 4 * P + P], uv[:, a, h * DV:h * DV + DV], olat[:, a, h], start=a == 0, stop=a == 1)
                if h % 4 == 3:
                    mm.then_inc(S["uv_done"], 1)

        def step_columns(i):
            return slice(i * SLEN, i * SLEN + SLEN) if isinstance(i, int) else bass.ds(i * SLEN, SLEN)

        @block.scalar
        def _(act):
            act.wait_ge(S["q_loaded"], 32)
            act.wait_ge(S["zeroed"], 10)

            def q_high(i, par):
                if not (isinstance(i, int) and i < 2):
                    act.wait_ge(S["s_done"], i * 2 - 2)
                cols = step_columns(i)
                for a in range(2):
                    round_high(nc, q_h[:, par, a].rearrange("p (h l) -> p h l", h=HEADS), ql_raw[:, :, a, cols])
                round_high(nc, rq[0:RD, par].rearrange("p (h l) -> p h l", h=HEADS), qr_raw[0:RD, :, cols]).then_inc(S["qh_ready"], 1)

            def keys_high(i):
                base = turn_base(i)
                for j in range(TURNS):
                    b = bank[:, 6 + (parity(base, 1) + j) % 2]
                    act.wait_ge(S["t_done"], base + (j + 1))
                    what, a, s0, n = step_of_keys(j)
                    if what == "new":
                        round_high(nc, ct_h[:, :, PAST:KS], b[:, 0:2 * P].rearrange("p (a q) -> p a q", a=2)[:, :, 0:SLEN])
                        o = round_high(nc, kt_h[:, PAST:KS], b[:, 2 * P:2 * P + SLEN])
                    else:
                        dst = ct_h[:, a, s0 * P:(s0 + n) * P] if what == "c" else kt_h[:, s0 * P:(s0 + n) * P]
                        o = round_high(nc, dst, b)
                    o.then_inc(S["t_high"], 1)

            def cache_high(i, par):
                act.wait_ge(raw_loaded[par], (i - par) * 48 + 96)
                round_high(nc, c_h[:], c_raw[:, par]).then_inc(S["ch_ready"], 1)

            q_high(0, 0)
            keys_high(0)
            cache_high(0, 0)

            def body(i, par, last):
                for qt in range(2):
                    act.wait_ge(S["max_step"], i * 4 + 2 * qt + 2)
                    if not (isinstance(i, int) and i == 0):
                        act.wait_ge(S["t_done"], i * (TURNS + PTURNS) + TURNS)
                    nc.scalar.activation(p[:, qt].rearrange("p (a b) -> p a b", a=3), bank[:, 3 * qt:3 * qt + 3, 0:KC], ACT.Exp,
                                         scale=SCALE, bias=mx[:, qt], accum_out=rsum[:, qt]).then_inc(S["exp_done"], 1)
                if not last:
                    q_high(i + 1, 1 - par)
                    keys_high(i + 1)
                base = weight_base(i, last)
                for j in range(PTURNS):
                    b = bank[:, 6 + (parity(base, 0) + j) % 2]
                    act.wait_ge(S["t_done"], base + (j + 1))
                    if j == 0 and not (isinstance(i, int) and i == 0):
                        act.wait_ge(S["o_done"], i)
                    if j < 4:
                        o = round_high(nc, pt_h[:, 4 * (j % 2):4 * (j % 2) + 4, j // 2 * P:j // 2 * P + P], b.rearrange("p (a q) -> p a q", a=4))
                    else:
                        o = round_high(nc, pt_h[0:SLEN, KB], b[0:SLEN, 0:2 * P])
                    o.then_inc(S["t_high"], 1)
                act.wait_ge(S["o_done"], i + 1)
                for a in range(2):
                    o = nc.scalar.copy(olat[:, a, :, step_columns(i)], bank[:, 0, a * QS:a * QS + QS].rearrange("p (h l) -> p h l", h=HEADS))
                o.then_inc(S["o_out"], 1)
                if not last:
                    cache_high(i + 1, 1 - par)
            seqs(act, body)

        @block.vector
        def _(dve):
            dve.wait_ge(S["q_loaded"], 32)
            dve.wait_ge(S["zeroed"], 10)

            def q_low(i, par):
                dve.wait_ge(S["qh_ready"], i + 1)
                cols = step_columns(i)
                for a in range(2):
                    v = lambda x: x[:, par, a].rearrange("p (h l) -> p h l", h=HEADS)
                    round_low(nc, v(q_l), ql_raw[:, :, a, cols], v(q_h))
                r = lambda rows: rq[rows, par].rearrange("p (h l) -> p h l", h=HEADS)
                round_low(nc, r(slice(RD, P)), qr_raw[0:RD, :, cols], r(slice(0, RD))).then_inc(S["ql_ready"], 1)

            def keys_low(i):
                base = turn_base(i)
                for j in range(TURNS):
                    b = bank[:, 6 + (parity(base, 1) + j) % 2]
                    dve.wait_ge(S["t_high"], base + (j + 1))
                    what, a, s0, n = step_of_keys(j)
                    if what == "new":
                        round_low(nc, ct_l[:, :, PAST:KS], b[:, 0:2 * P].rearrange("p (a q) -> p a q", a=2)[:, :, 0:SLEN], ct_h[:, :, PAST:KS])
                        o = round_low(nc, kt_l[:, PAST:KS], b[:, 2 * P:2 * P + SLEN], kt_h[:, PAST:KS])
                    else:
                        at = slice(s0 * P, (s0 + n) * P)
                        lo, hi = (ct_l[:, a, at], ct_h[:, a, at]) if what == "c" else (kt_l[:, at], kt_h[:, at])
                        o = round_low(nc, lo, b, hi)
                    o.then_inc(S["t_out"], 1)

            def cache_low(i, par):
                dve.wait_ge(S["ch_ready"], i + 1)
                round_low(nc, c_l[:], c_raw[:, par], c_h[:]).then_inc(S["cl_ready"], 1)

            q_low(0, 0)
            keys_low(0)
            cache_low(0, 0)

            def body(i, par, last):
                for qt in range(2):
                    dve.wait_ge(S["s_done"], i * 2 + qt + 1)
                    nc.vector.memset(bank[:, 3 * qt + 2, KS - 2 * KC:KC], MASKED).then_inc(S["masked"], 1)
                    dve.wait_ge(S["masked"], i * 2 + qt + 1)
                    if not (isinstance(i, int) and i == 0):
                        dve.wait_ge(S["exp_done"], i * 2 - 1 + qt)
                    nc.vector.tensor_reduce(mx[:, qt], bank[:, 3 * qt:3 * qt + 3, 0:KC], AX.XY, ALU.max).then_inc(S["max_step"], 1)
                    dve.wait_ge(S["max_step"], i * 4 + 2 * qt + 1)
                    nc.vector.tensor_scalar(mx[:, qt], mx[:, qt], -SCALE, None, ALU.mult).then_inc(S["max_step"], 1)
                for qt in range(2):
                    dve.wait_ge(S["exp_done"], i * 2 + qt + 1)
                    nc.vector.reciprocal(rsum[:, qt], rsum[:, qt]).then_inc(S["inv_step"], 1)
                    dve.wait_ge(S["inv_step"], i * 2 + qt + 1)
                    nc.vector.tensor_scalar(p[:, qt], p[:, qt], rsum[:, qt], None, ALU.mult).then_inc(S["p_ready"], 1)
                if not last:
                    q_low(i + 1, 1 - par)
                    keys_low(i + 1)
                base = weight_base(i, last)
                for j in range(PTURNS):
                    b = bank[:, 6 + (parity(base, 0) + j) % 2]
                    dve.wait_ge(S["t_high"], base + (j + 1))
                    if j < 4:
                        at = (slice(None), slice(4 * (j % 2), 4 * (j % 2) + 4), slice(j // 2 * P, j // 2 * P + P))
                        o = round_low(nc, pt_l[at], b.rearrange("p (a q) -> p a q", a=4), pt_h[at])
                    else:
                        o = round_low(nc, pt_l[0:SLEN, KB], b[0:SLEN, 0:2 * P], pt_h[0:SLEN, KB])
                    o.then_inc(S["t_out"], 1)
                if not last:
                    cache_low(i + 1, 1 - par)
            seqs(dve, body)
            dve.wait_ge(S["uv_loaded"], 32)
            for j in range(4):
                dve.wait_ge(S["uv_done"], j + 1)
                g = flat(gate[:, 4 * j:4 * j + 4])
                nc.vector.tensor_tensor(g, bank[:, j], g, ALU.mult).then_inc(S["uv_out"], 1)


INPUTS = ["state_hgrn", "cache_ckv", "cache_krope", "w_in_a", "lb_gamma", "a_norm_g", "w_out_a", "w_dkv",
          "kv_norm_g", "w_uk", "w_uv", "w_in_b", "q_norm_g", "w_uq", "w_out_b", "ln_g", "ln_b"]
OUTPUTS = {"y": (NT, P, D), "state_prompt": (1, 1, AH, P, P), "ckv_prompt": (1, SEQ, KVL), "krope_prompt": (1, SEQ, RD),
           "state_sample": (1, NSEQ, AH, P, P), "ckv_sample": (NSEQ, SLEN, KVL), "krope_sample": (NSEQ, SLEN, RD)}
SCRATCH = {"scratch_o": (AH, P, T), "scratch_x": (NT, P, D), "scratch_gate": (HEADS, P, T), "scratch_og": (HEADS, P, T),
           "scratch_ql": (PAIRS, P, 4 * P), "scratch_qr": (PAIRS, RD, 2 * P)}


def encoder(nc, d):

    class Kept:
        pass

    k = Kept()
    k.d = d

    def keep(stack, name, shape, side):
        return [stack.enter_context(nc.sbuf_tensor(f"{name}_{part}", [P] + shape, F32R, side=side)) for part in "hl"]

    def row(x, t):
        return d[x][bass.ds(t, 1)].rearrange("o t d -> (o t) d")

    def tiles_of(x):
        return d[x].rearrange("h p t -> p h t")

    with nc.sbuf_tensor("ident", [P, P], F32) as k.ident:
        with ExitStack() as low:
            with ExitStack() as acts:
                k.act_h, k.act_l = keep(acts, "act", [KD, T], "right")
                phase_transpose_x(nc, k, lambda t: d["x"][t])
                phase_mixer_a(nc, k)
                phase_output(nc, k, "b", KD, d["w_out_a"][0], lambda t: tiles_of("scratch_o")[:, :, tile_cols(t)],
                             lambda t: row("x", t), (d["ln_g"][0], d["ln_b"][0]), True, lambda t: row("scratch_x", t))
                phase_gates(nc, k)
                k.ct_h, k.ct_l = keep(low, "ct", [2, SEQ], "left")
                k.kr_h, k.kr_l = keep(low, "kr", [SEQ], "left")
                k.cq_h, k.cq_l = keep(low, "cq", [4, T], "left")
                phase_latents(nc, k)
            phase_heads(nc, k)
        phase_samples(nc, k)
        phase_output(nc, k, "o", HEADS, d["w_out_b"][0], lambda t: tiles_of("scratch_og")[:, :, tile_cols(t)],
                     lambda t: row("scratch_x", t), (d["ln_g"][1], d["ln_b"][1]), False, lambda t: row("y", t))


def kernel(**inputs):
    import concourse.bacc as bacc
    from concourse.bass_utils import run_bass_kernel_spmd

    nc = bacc.Bacc("TRN2", target_bir_lowering=False, num_devices=1)
    arrays = {n: np.ascontiguousarray(inputs[n]) for n in INPUTS}
    arrays["x"] = np.concatenate([np.asarray(inputs["x_prompt"]).reshape(NPB, P, D), np.asarray(inputs["x_sample"]).reshape(1, P, D)])
    arrays.update(shape_constants())
    d = {n: nc.dram_tensor("in_" + n, list(a.shape), mybir.dt.from_np(a.dtype), kind="ExternalInput").ap() for n, a in arrays.items()}
    d.update({n: nc.dram_tensor("out_" + n, list(s), F32, kind="ExternalOutput").ap() for n, s in OUTPUTS.items()})
    d.update({n: nc.dram_tensor(n, list(s), F32, kind="Internal").ap() for n, s in SCRATCH.items()})
    encoder(nc, d)
    r = run_bass_kernel_spmd(nc, [{"in_" + n: a for n, a in arrays.items()}], core_ids=[0]).results[0]
    out = {n: r["out_" + n] for n in OUTPUTS}
    return (out["y"][:NPB].reshape(1, SEQ, D), out["y"][NPB].reshape(NSEQ, SLEN, D), out["state_prompt"], out["ckv_prompt"],
            out["krope_prompt"], out["state_sample"], out["ckv_sample"], out["krope_sample"])
```

```python
from contextlib import ExitStack

import numpy as np
import concourse.bass as bass
from concourse import mybir

F32 = mybir.dt.float32
F32R = mybir.dt.float32r
I32 = mybir.dt.int32
ACT = mybir.ActivationFunctionType
ALU = mybir.AluOpType
AX = mybir.AxisListType

P = 128
D = 1024
KD = D // P
SEQ, NSEQ, SLEN, PAST = 1024, 8, 16, 1024
T = SEQ + NSEQ * SLEN
NT = T // P
NPB = SEQ // P
TG = 384
NTG = T // TG
CH = 64
NCH = SEQ // CH
AH = 8
HEADS, QL, KVL, RD, NOPE, DV = 16, 512, 256, 64, 128, 128
QD = NOPE + RD
EPS = 1e-6
ALPHA = 4 ** 0.25
SCALE = QD ** -0.5
MASKED = -1e30
BANK = 512


def flat(ap):
    return ap.rearrange("p a b -> p (a b)")


def shape_constants():
    f = np.float32
    s, l = np.arange(P)[:, None], np.arange(P)[None, :]
    c = {}
    c["ident"] = np.eye(P, dtype=f)
    c["mask_prompt"] = np.tile(((s <= l) & (s // CH == l // CH)).astype(np.int32), (1, 4))
    c["mask_sample"] = ((s <= l) & (s // SLEN == l // SLEN)).astype(np.int32)
    r = np.ones((P, T), f)
    r[:, 0:SEQ:CH] = 0
    r[:, SEQ::SLEN] = 0
    c["restart"] = r
    c["member"] = (s // SLEN == np.arange(NSEQ)[None, :]).astype(f)
    pos = np.concatenate([np.arange(SEQ), np.tile(PAST + np.arange(SLEN), NSEQ)]).astype(f)
    half = RD // 2
    inv = np.power(f(10000.0), -np.arange(half, dtype=f) / f(half)).astype(f)
    ang = (pos[:, None] * inv[None, :]).astype(f)
    cos, sin = np.cos(ang).astype(f), np.sin(ang).astype(f)
    c["cos_nat"] = cos.reshape(NT, P, half).transpose(1, 0, 2).reshape(P, NT * half).copy()
    c["sin_nat"] = sin.reshape(NT, P, half).transpose(1, 0, 2).reshape(P, NT * half).copy()
    c["cos_t"] = np.tile(cos.T, (4, 1))
    c["sin_t"] = np.concatenate([sin.T, -sin.T] * 2, 0)
    return c


class Core:

    def __init__(self, nc, ctx):
        self.nc, self.ctx, self.sems = nc, ctx, []
        ctx.callback(self.clear)

    def clear(self):
        self.nc.all_engine_barrier()
        numbers = sorted(s.num for s in self.sems)
        start = 0
        for i in range(1, len(numbers) + 1):
            if i == len(numbers) or numbers[i] != numbers[i - 1] + 1:
                self.nc.gpsimd.sem_clear(range(numbers[start], numbers[i - 1] + 1))
                start = i
        self.nc.all_engine_barrier()
        for s in reversed(self.sems):
            self.nc.release_semaphore(s)

    def sb(self, name, shape, dt=F32):
        return self.ctx.enter_context(self.nc.sbuf_tensor(name, [P] + list(shape), dt))

    def ps(self, name, shape, dt=F32):
        return self.ctx.enter_context(self.nc.psum_tensor(name, [P] + list(shape), dt))

    def sem(self, name):
        self.sems.append(self.nc.alloc_semaphore(name))
        return self.sems[-1]


def round_high(nc, high, x):
    return nc.scalar.activation(high, x, ACT.Identity)


def round_low(nc, low, x, high):
    return nc.vector.tensor_tensor(low, x, high.bitcast(F32), ALU.subtract)


def product(nc, out, left, right, first, last):
    (lh, ll), (rh, rl) = left, right
    nc.tensor.matmul(out, ll, rh, start=first, stop=False)
    nc.tensor.matmul(out, lh, rl, start=False, stop=False)
    return nc.tensor.matmul(out, lh, rh, start=False, stop=last)


GLA_STEPS = ["V0", "V1", "K0", "C0", "S0", "S1", "O0", "SI", "K1", "C1", "S2", "OT0", "S3", "O1",
             "SO", "SS0", "OT1", "SS1", "SOT"]


def phase_mixer_a(nc, k, x_all):
    d = k.d
    w_in = d["w_in_a"][0].rearrange("(a p) e -> p a e", p=P)
    COLUMN = [D, 0, 2 * D, 3 * D]
    with ExitStack() as ctx:
        m = Core(nc, ctx)
        xn = m.sb("a_xn", [3, D])
        w_raw = m.sb("a_w_raw", [2, KD, P])
        w_h = m.sb("a_w_h", [2, KD, P], F32R)
        w_l = m.sb("a_w_l", [2, KD, P], F32R)
        bm = m.sb("a_bm", [T])
        nz = m.sb("a_nz", [T])
        fz = m.sb("a_fz", [T])
        kk = m.sb("a_kk", [T])
        bb = m.sb("a_bb", [T])
        qq = m.sb("a_qq", [T])
        vt = m.sb("a_vt", [T])
        sg = m.sb("a_sg", [T])
        qin = m.sb("a_qin", [T])
        kin = m.sb("a_kin", [T])
        qex = m.sb("a_qex", [T])
        kdec = m.sb("a_kdec", [T])
        decay = m.sb("a_decay", [NCH + NSEQ])
        vn = m.sb("a_vn", [NT, P])
        kdn = m.sb("a_kdn", [4, 2, P])
        kd8 = m.sb("a_kd8", [P])
        sct = m.sb("a_sct", [4, P])
        sct8 = m.sb("a_sct8", [P])
        vexp = m.sb("a_vexp", [NSEQ, P])
        qdiag = m.sb("a_qdiag", [NSEQ, P])
        st = m.sb("a_st", [9, P])
        sts = m.sb("a_sts", [NSEQ, P])
        osb = m.sb("a_osb", [4, P])
        on = m.sb("a_on", [4, P])
        og = m.sb("a_og", [T])
        ms = m.sb("a_ms", [4])
        rs = m.sb("a_rs", [4])
        mhalf = m.sb("a_mhalf", [4])
        eps = m.sb("a_eps", [4])
        mask_p = m.sb("a_mask_p", [4 * P], I32)
        mask_s = m.sb("a_mask_s", [P], I32)
        restart = m.sb("a_restart", [T])
        member = m.sb("a_member", [NSEQ])
        lbg = m.sb("a_lbg", [2, AH])
        lbe = m.sb("a_lbe", [2, AH])
        lbs = m.sb("a_lbs", [AH])
        lb = m.sb("a_lb", [AH])
        oml = m.sb("a_oml", [AH])
        ang = m.sb("a_ang", [1])
        pj = m.ps("a_pj", [2, 3, BANK])
        gb = m.ps("a_gb", [2, BANK])

        x_loaded = [m.sem(f"a_x_loaded{i}") for i in range(3)]
        ident_loaded, x_turned, xh_done, xl_done = (m.sem("a_" + x) for x in ("ident_loaded", "x_turned", "xh_done", "xl_done"))
        w_loaded = [m.sem(f"a_w_loaded{i}") for i in range(2)]
        wh_ready, wl_ready, proj_done = m.sem("a_wh_ready"), m.sem("a_wl_ready"), m.sem("a_proj_done")
        const_loaded = m.sem("a_const_loaded")
        states_loaded, states_stored = m.sem("a_states_loaded"), m.sem("a_states_stored")
        final_stored, og_stored = m.sem("a_final_stored"), m.sem("a_og_stored")
        prep = m.sem("a_prep")
        zeroed = m.sem("a_zeroed")
        z_out, q_out, v_out, g_out = (m.sem(f"a_{x}_out") for x in "zqvg")
        g_step = m.sem("a_g_step")
        logf_done = m.sem("a_logf_done")
        key_done = m.sem("a_key_done")
        b_step = m.sem("a_b_step")
        gates = [m.sem(f"a_gate{i}") for i in range(4)]
        operand = [m.sem(f"a_operand{i}") for i in range(4)]
        pe_did = {s: m.sem(f"a_pe_{s}") for s in GLA_STEPS}
        out_of = {s: m.sem(f"a_out_{s}") for s in GLA_STEPS}
        spread_done = m.sem("a_spread")
        sq_done, ms_done, rs_step, on_ready = (m.sem("a_" + x) for x in
                                               ("sq_done", "ms_done", "rs_step", "on_ready"))
        state_step = m.sem("a_state_step")
        decay_done = m.sem("a_decay_done")
        block = ctx.enter_context(nc.Block())

        x_banks = [gb[:, 0], gb[:, 1], pj[:, 1, 0], pj[:, 1, 1], pj[:, 1, 2]]

        def x_half(n):
            return slice(None), slice(4 * (n % 2), 4 * (n % 2) + 4), slice(n // 2 * P, n // 2 * P + P)

        def x_bank(n):
            return x_banks[n % len(x_banks)].rearrange("p (j q) -> p j q", j=4)

        def heads(eng, body):
            body(0, True, False)
            body(1, True, True)
            with eng.Fori(2, AH - 1) as h:
                body(h, True, True)
            body(AH - 1, True, True)
            body(AH, False, True)

        def step_out(eng, s, h):
            if s in ("S0", "S1", "S2", "S3"):
                eng.wait_ge(state_step, h * NCH + (4 * int(s[1]) + 4 - NCH))
            else:
                eng.wait_ge(out_of[s], h)

        def chunks(x):
            return (x[:, 0:SEQ].rearrange("p (c l) -> p c l", l=CH),
                    x[:, SEQ:T].rearrange("p (c l) -> p c l", l=SLEN))

        @block.sync
        def _(sp):
            def load_w(h, c):
                if not (isinstance(h, int) and h == 0 and c < 2):
                    sp.wait_ge(w_loaded[c % 2], 16)
                    sp.wait_ge(wl_ready, h * 4 + (c - 1))
                sp.dma_start(w_raw[:, c % 2], w_in[:, :, bass.ds(h * P + COLUMN[c], P)]).then_inc(w_loaded[c % 2], 16)

            def body(h, proj, gla):
                if gla:
                    g = h - 1
                    if not (isinstance(h, int) and h == 1):
                        sp.wait_ge(states_stored, h * 16 - 16)
                    sp.dma_start(sts[:], d["state_hgrn"][0, :, bass.ds(g, 1)].rearrange("b o k v -> k (b o) v")).then_inc(states_loaded, 16)
                if proj:
                    load_w(h, 2)
                    load_w(h, 3)
                    if not (isinstance(h, int) and h == AH - 1):
                        load_w(h + 1, 0)
                        load_w(h + 1, 1)
                if gla:
                    g = h - 1
                    step_out(sp, "S3", h)
                    sp.dma_start(d["state_prompt"][0, 0, bass.ds(g, 1)].rearrange("o k v -> k (o v)"), st[:, 8]).then_inc(final_stored, 16)
                    sp.wait_ge(out_of["SS1"], h)
                    sp.dma_start(d["state_sample"][0, :, bass.ds(g, 1)].rearrange("b o k v -> k (b o) v"), sts[:]).then_inc(states_stored, 16)
                    sp.wait_ge(out_of["SOT"], h)
                    sp.dma_start(d["scratch_o"][bass.ds(g, 1)].rearrange("o p t -> p (o t)"), og[:]).then_inc(og_stored, 16)

            load_w(0, 0)
            sp.dma_start(k.ident[:], d["ident"]).then_inc(ident_loaded, 16)
            for t in range(NT):
                if t >= 3:
                    sp.wait_ge(x_turned, 2 * (t - 2))
                sp.dma_start(xn[:, t % 3, :], x_all(t)).then_inc(x_loaded[t % 3], 16)
                if t == 2:
                    load_w(0, 1)
            loads = [(mask_p, d["mask_prompt"]), (mask_s, d["mask_sample"]), (restart, d["restart"]),
                     (member, d["member"])]
            with nc.allow_non_contiguous_dma(reason="a few KB of vectors, once"):
                for row in range(2):
                    sp.dma_start(lbg[:, row, :], d["lb_gamma"][row].rearrange("(h p) -> p h", p=P)).then_inc(const_loaded, 16)
                sp.dma_start(ang[:], d["a_norm_g"].rearrange("o p -> p o")).then_inc(const_loaded, 16)
                for dst, src in loads:
                    sp.dma_start(dst[:], src).then_inc(const_loaded, 16)
            heads(sp, body)
            for s in (states_stored, final_stored, og_stored):
                sp.wait_ge(s, AH * 16)

        @block.tensor
        def _(pe):
            def tr(bank, slot, src):
                return nc.tensor.transpose(gb[:, bank, slot * P:(slot + 1) * P], src, k.ident[:])

            def blk(x, b):
                return x[:, b * P:(b + 1) * P]

            def step(i, h):
                s = GLA_STEPS[i]
                bank = i % 2
                if i >= 2:
                    step_out(pe, GLA_STEPS[i - 2], h)
                elif not (isinstance(h, int) and h == 1):
                    last = len(GLA_STEPS) - 1
                    pe.wait_ge(out_of[GLA_STEPS[last - (last - i) % 2]], h - 1)

                def out(slot, n=1):
                    return gb[:, bank, slot * P:(slot + n) * P]

                if s in ("V0", "V1"):
                    pe.wait_ge(v_out, h)
                    for j in range(4):
                        mm = tr(bank, j, blk(vt, 4 * int(s[1]) + j))
                elif s in ("K0", "K1"):
                    pe.wait_ge(operand[0], h)
                    for j in range(4):
                        mm = tr(bank, j, blk(kdec, 4 * int(s[1]) + j))
                elif s in ("C0", "C1"):
                    pe.wait_ge(operand[1], h)
                    pe.wait_ge(operand[2], h)
                    for j in range(4):
                        b = 4 * int(s[1]) + j
                        mm = nc.tensor.matmul(out(j), blk(kin, b), blk(qin, b), start=True, stop=True)
                elif s in ("S0", "S1", "S2", "S3"):
                    n = int(s[1])
                    if n % 2 == 0:
                        pe.wait_ge(out_of[f"V{n // 2}"], h)
                        pe.wait_ge(out_of[f"K{n // 2}"], h)
                    for j in range(4):
                        c = 4 * n + j
                        mm = nc.tensor.matmul(out(j), kdn[:, c // 2 % 4, c % 2], vn[:, c // 2], start=True, stop=True)
                elif s in ("O0", "O1"):
                    n = int(s[1])
                    pe.wait_ge(out_of[f"C{n}"], h)
                    step_out(pe, f"S{2 * n + 1}", h)
                    pe.wait_ge(operand[3], h)
                    for j in range(4):
                        b = 4 * n + j
                        if b == 0:
                            for half in range(2):
                                rows = slice(CH * half, CH * half + CH)
                                nc.tensor.matmul(gb[rows, bank, 0:P], sct[:, 0, rows], vn[:, 0], start=True, stop=half == 0)
                        else:
                            nc.tensor.matmul(out(j), sct[:, j], vn[:, b], start=True, stop=False)
                        for half in range(2):
                            c = 2 * b + half
                            if c == 0:
                                continue
                            rows = slice(CH * half, CH * half + CH)
                            mm = nc.tensor.matmul(gb[rows, bank, j * P:(j + 1) * P],
                                                  qex[:, c * CH:(c + 1) * CH], st[:, c % 8],
                                                  start=False, stop=True)
                elif s in ("OT0", "OT1", "SOT"):
                    n = ["OT0", "OT1", "SOT"].index(s)
                    pe.wait_ge(on_ready, h * 3 + (n - 2))
                    for j in range(4 if n < 2 else 1):
                        mm = tr(bank, j, on[:, j])
                elif s == "SI":
                    tr(bank, 0, blk(vt, NPB))
                    tr(bank, 1, blk(kdec, NPB))
                    mm = nc.tensor.matmul(out(2), blk(kin, NPB), blk(qin, NPB), start=True, stop=True)
                elif s == "SO":
                    pe.wait_ge(out_of["SI"], h)
                    pe.wait_ge(spread_done, h * 2)
                    pe.wait_ge(states_loaded, h * 16)
                    nc.tensor.matmul(out(0), sct8[:], vn[:, NPB], start=True, stop=False)
                    for i in range(NSEQ):
                        mm = nc.tensor.matmul(out(0), qdiag[:, i], sts[:, i], start=False, stop=i == NSEQ - 1)
                else:
                    n = int(s[2])
                    mm = nc.tensor.matmul(out(0, 4), kd8[:], flat(vexp[:, 4 * n:4 * n + 4]), start=True, stop=True)
                mm.then_inc(pe_did[s], 1)

            def turn_x(tg):
                for n in range(tg * 2 * TG // P, (tg + 1) * 2 * TG // P):
                    t = n // 2
                    if n % 2 == 0:
                        pe.wait_ge(x_loaded[t % 3], 16 * (t // 3 + 1))
                    if n >= len(x_banks):
                        pe.wait_ge(xl_done, n - len(x_banks) + 1)
                    for j in range(4):
                        c = 4 * (n % 2) + j
                        last = nc.tensor.transpose(x_bank(n)[:, j], xn[:, t % 3, c * P:(c + 1) * P], k.ident[:])
                    last.then_inc(x_turned, 1)

            def body(h, proj, gla):
                if not proj:
                    for i in range(len(GLA_STEPS)):
                        step(i, h)
                    return
                hook = 0
                for c in range(4):
                    pe.wait_ge(wl_ready, h * 4 + c + 1)
                    if c >= 2:
                        pe.wait_ge((z_out, q_out)[c - 2], h + 1)
                    elif gla:
                        pe.wait_ge((v_out, g_out)[c], h)
                    for tg in range(NTG):
                        if isinstance(h, int) and h == 0 and c == 0:
                            turn_x(tg)
                            pe.wait_ge(xl_done, (tg + 1) * 2 * TG // P)
                        for kt in range(KD):
                            cols = slice(tg * TG, (tg + 1) * TG)
                            mm = product(nc, pj[:, c % 2, tg, 0:TG],
                                         (w_h[:, c % 2, kt], w_l[:, c % 2, kt]),
                                         (k.act_h[:, kt, cols], k.act_l[:, kt, cols]),
                                         kt == 0, kt == KD - 1)
                            if kt == KD - 1 and tg == NTG - 1:
                                mm.then_inc(proj_done, 1)
                            if kt % 4 == 3:
                                if gla and 2 <= hook < 2 + len(GLA_STEPS):
                                    step(hook - 2, h)
                                hook += 1

            pe.wait_ge(ident_loaded, 16)
            heads(pe, body)

        @block.scalar
        def _(act):
            def high(h, c):
                act.wait_ge(w_loaded[c % 2], h * 32 + 16 * (c // 2 + 1))
                if not (isinstance(h, int) and h == 0 and c < 2):
                    act.wait_ge(proj_done, h * 4 + (c - 1))
                round_high(nc, w_h[:, c % 2], w_raw[:, c % 2]).then_inc(wh_ready, 1)

            def copy_o(s, n, h):
                act.wait_ge(pe_did[s], h)
                if not (isinstance(h, int) and h == 1 and n == 0):
                    act.wait_ge(on_ready, h * 3 + (n - 3))
                w = 4 * P if n < 2 else P
                nc.scalar.copy(flat(osb[:])[:, 0:w], gb[:, GLA_STEPS.index(s) % 2, 0:w]).then_inc(out_of[s], 1)

            high(0, 0)
            for n in range(2 * NT):
                act.wait_ge(x_turned, n + 1)
                round_high(nc, k.act_h[x_half(n)], x_bank(n)).then_inc(xh_done, 1)
                if n == 6:
                    high(0, 1)
            act.wait_ge(const_loaded, 16 * 7)
            act.wait_ge(prep, 3)
            nc.scalar.activation(flat(lbe[:]), flat(lbg[:]), ACT.Exp).then_inc(prep, 1)

            def body(h, proj, gla):
                if proj and not (isinstance(h, int) and h == 0):
                    high(h, 1)
                if gla:
                    act.wait_ge(proj_done, h * 4)
                    if not (isinstance(h, int) and h == 1):
                        act.wait_ge(out_of["SOT"], h - 1)
                    nc.scalar.activation(sg[:].rearrange("p (a b) -> p a b", a=3), pj[:, 1, :, 0:TG], ACT.Sigmoid).then_inc(g_step, 1)
                    for n in range(2):
                        act.wait_ge(pe_did[f"V{n}"], h)
                        nc.scalar.copy(flat(vn[:, 4 * n:4 * n + 4]), gb[:, n]).then_inc(out_of[f"V{n}"], 1)
                if proj:
                    act.wait_ge(proj_done, h * 4 + 1)
                    if gla:
                        act.wait_ge(gates[2], h)
                    for dst, sign in ((fz, 1.0), (nz, -1.0)):
                        last = nc.scalar.activation(dst[:].rearrange("p (a b) -> p a b", a=3), pj[:, 0, :, 0:TG], ACT.Sigmoid, scale=sign)
                    last.then_inc(z_out, 1)
                    high(h, 2)
                if gla:
                    copy_o("O0", 0, h)
                if proj:
                    act.wait_ge(z_out, h + 1)
                    if isinstance(h, int):
                        a, b = oml[:, h:h + 1], lb[:, h:h + 1]
                    else:
                        a, b = oml[:, bass.ds(h, 1)], lb[:, bass.ds(h, 1)]
                    if isinstance(h, int) and h == 0:
                        act.wait_ge(prep, 7)
                    nc.scalar.activation(fz[:], fz[:], ACT.Ln, scale=a, bias=b).then_inc(logf_done, 1)
                    act.wait_ge(proj_done, h * 4 + 2)
                    if gla:
                        act.wait_ge(operand[2], h)
                        act.wait_ge(operand[3], h)
                    nc.scalar.copy(qq[:].rearrange("p (a b) -> p a b", a=3), pj[:, 1, :, 0:TG]).then_inc(q_out, 1)
                    high(h, 3)
                if gla:
                    copy_o("O1", 1, h)
                    copy_o("SO", 2, h)
                if proj:
                    act.wait_ge(proj_done, h * 4 + 3)
                    if gla:
                        act.wait_ge(pe_did["SI"], h)
                    nc.scalar.copy(vt[:].rearrange("p (a b) -> p a b", a=3), pj[:, 0, :, 0:TG]).then_inc(v_out, 1)
                    if not (isinstance(h, int) and h == AH - 1):
                        high(h + 1, 0)
                    act.wait_ge(b_step, h * 2 + 2)
                    for i, (dst, src, sc) in enumerate(((kdec, nz, 1.0), (kin, bm, -1.0), (qin, bm, 1.0), (qex, bb, 1.0))):
                        if gla:
                            act.wait_ge(pe_did["SO"], h)
                        nc.scalar.activation(dst[:], src[:], ACT.Exp, scale=sc).then_inc(gates[i], 1)

            heads(act, body)

        @block.gpsimd
        def _(pool):
            for x in (flat(kdn[:].rearrange("p a b c -> p (a b) c")), flat(sct[:]), sct8[:], flat(qdiag[:])):
                nc.gpsimd.memset(x, 0.0).then_inc(zeroed, 1)
            nc.gpsimd.memset(mhalf[:], -0.5).then_inc(zeroed, 1)
            nc.gpsimd.memset(eps[:], EPS).then_inc(zeroed, 1)
            pool.wait_ge(zeroed, 6)

            def body(h, proj, gla):
                if gla:
                    def norm(n):
                        w = 4 if n < 2 else 1
                        pool.wait_ge(ms_done, h * 3 + (n - 2))
                        nc.gpsimd.tensor_tensor(rs[:, 0:w], ms[:, 0:w], eps[:, 0:w], ALU.add).then_inc(rs_step, 1)
                        pool.wait_ge(rs_step, h * 6 + (2 * n - 5))
                        nc.gpsimd.tensor_tensor(rs[:, 0:w], rs[:, 0:w], mhalf[:, 0:w], ALU.pow).then_inc(rs_step, 1)
                    pool.wait_ge(zeroed, 5)
                    pool.wait_ge(operand[3], h)
                    q = qdiag[:]
                    diag = bass.AP(q.tensor, q.offset, [q.ap[0], [P + SLEN, NSEQ], [1, SLEN]])
                    nc.gpsimd.tensor_copy(diag, qex[:, SEQ:T].rearrange("p (a b) -> p a b", a=NSEQ)).then_inc(spread_done, 1)
                    norm(0)
                    pool.wait_ge(out_of["SI"], h)
                    v8 = vn[:, NPB:NPB + 1].broadcast_to([P, NSEQ, P])
                    nc.gpsimd.tensor_tensor(vexp[:], v8, member[:].rearrange("p (a o) -> p a o", o=1).broadcast_to([P, NSEQ, P]), ALU.mult).then_inc(spread_done, 1)
                    norm(1)
                    norm(2)
                if proj:
                    for i, (dst, src) in enumerate(((kdec, kk), (kin, kk))):
                        pool.wait_ge(gates[i], h + 1)
                        nc.gpsimd.tensor_tensor(dst[:], dst[:], src[:], ALU.mult).then_inc(operand[i], 1)

            pool.wait_ge(const_loaded, 16 * 7)
            heads(pool, body)

        @block.vector
        def _(dve):
            def low(h, c):
                dve.wait_ge(wh_ready, h * 4 + c + 1)
                round_low(nc, w_l[:, c % 2], w_raw[:, c % 2], w_h[:, c % 2]).then_inc(wl_ready, 1)

            low(0, 0)
            for n in range(2 * NT):
                dve.wait_ge(xh_done, n + 1)
                round_low(nc, k.act_l[x_half(n)], x_bank(n), k.act_h[x_half(n)]).then_inc(xl_done, 1)
                if n == 6:
                    low(0, 1)

            dve.wait_ge(const_loaded, 16 * 7)
            nc.vector.tensor_tensor(lbs[:], lbg[:, 0], lbg[:, 1], ALU.max).then_inc(prep, 1)
            dve.wait_ge(prep, 1)
            for row in range(2):
                nc.vector.tensor_tensor(lbg[:, row], lbg[:, row], lbs[:], ALU.subtract).then_inc(prep, 1)
            dve.wait_ge(prep, 4)
            nc.vector.tensor_tensor(lbs[:], lbe[:, 0], lbe[:, 1], ALU.add).then_inc(prep, 1)
            dve.wait_ge(prep, 5)
            nc.vector.reciprocal(lbs[:], lbs[:]).then_inc(prep, 1)
            dve.wait_ge(prep, 6)
            nc.vector.tensor_tensor(lb[:], lbe[:, 0], lbs[:], ALU.mult)
            nc.vector.tensor_tensor(oml[:], lbe[:, 1], lbs[:], ALU.mult).then_inc(prep, 1)
            dve.wait_ge(prep, 7)
            dve.wait_ge(zeroed, 6)

            def body(h, proj, gla):
                def bank(s):
                    return gb[:, GLA_STEPS.index(s) % 2]

                def keys(n):
                    dve.wait_ge(pe_did[f"K{n}"], h)
                    for half in range(2):
                        rows = slice(CH * half, CH * half + CH)
                        last = nc.vector.tensor_copy(kdn[rows, :, half], gb[rows, GLA_STEPS.index(f"K{n}") % 2].rearrange("p (j q) -> p j q", j=4))
                    last.then_inc(out_of[f"K{n}"], 1)

                def scores(n):
                    dve.wait_ge(zeroed, 5)
                    dve.wait_ge(pe_did[f"C{n}"], h)
                    nc.vector.copy_predicated(flat(sct[:]), mask_p[:], bank(f"C{n}")).then_inc(out_of[f"C{n}"], 1)

                def states(n):
                    dve.wait_ge(pe_did[f"S{n}"], h)
                    if n == 0:
                        dve.wait_ge(operand[3], h)
                    if n == 3 and not (isinstance(h, int) and h == 1):
                        dve.wait_ge(final_stored, h * 16 - 16)
                    for j in range(4):
                        c = 4 * n + j
                        to = st[:, (c + 1) % 8 if c + 1 < NCH else 8]
                        cs = bank(f"S{n}")[:, j * P:(j + 1) * P]
                        if c == 0:
                            last = nc.vector.tensor_copy(to, cs)
                        else:
                            dve.wait_ge(state_step, h * NCH + (c - NCH))
                            last = nc.vector.scalar_tensor_tensor(out=to, in0=st[:, c % 8], scalar=decay[:, c:c + 1], in1=cs, op0=ALU.mult, op1=ALU.add)
                        last.then_inc(state_step, 1)

                def square(n):
                    w = 4 if n < 2 else 1
                    dve.wait_ge(out_of[("O0", "O1", "SO")[n]], h)
                    if n == 0:
                        if not (isinstance(h, int) and h == 1):
                            dve.wait_ge(pe_did["SOT"], h - 1)
                    else:
                        dve.wait_ge(pe_did[f"OT{n - 1}"], h)
                    nc.vector.scalar_tensor_tensor(out=on[:, 0:w], in0=osb[:, 0:w], scalar=1.0 / P, in1=osb[:, 0:w], op0=ALU.mult, op1=ALU.mult).then_inc(sq_done, 1)
                    dve.wait_ge(sq_done, h * 3 + (n - 2))
                    nc.vector.tensor_reduce(ms[:, 0:w], on[:, 0:w], AX.X, ALU.add).then_inc(ms_done, 1)

                def normed(n):
                    w = 4 if n < 2 else 1
                    dve.wait_ge(rs_step, h * 6 + (2 * n - 4))
                    nc.vector.tensor_tensor(on[:, 0:w], osb[:, 0:w], rs[:, 0:w].rearrange("p (a o) -> p a o", o=1).broadcast_to([P, w, P]), ALU.mult).then_inc(on_ready, 1)

                def gated(s, n):
                    dve.wait_ge(pe_did[s], h)
                    if n == 0 and not (isinstance(h, int) and h == 1):
                        dve.wait_ge(og_stored, h * 16 - 16)
                    w = 4 * P if n < 2 else P
                    cols = slice(4 * P * n, 4 * P * n + w)
                    nc.vector.scalar_tensor_tensor(out=og[:, cols], in0=bank(s)[:, 0:w], scalar=ang[:, 0:1], in1=sg[:, cols], op0=ALU.mult, op1=ALU.mult).then_inc(out_of[s], 1)

                def sample_states(n):
                    dve.wait_ge(pe_did[f"SS{n}"], h)
                    for j in range(4):
                        i = 4 * n + j
                        last = nc.vector.scalar_tensor_tensor(out=sts[:, i], in0=sts[:, i], scalar=decay[:, NCH + i:NCH + i + 1], in1=bank(f"SS{n}")[:, j * P:(j + 1) * P], op0=ALU.mult, op1=ALU.add)
                    last.then_inc(out_of[f"SS{n}"], 1)

                if proj and not (isinstance(h, int) and h == 0):
                    low(h, 1)
                if gla:
                    dve.wait_ge(g_step, h)
                    nc.vector.tensor_tensor(sg[:].rearrange("p (a b) -> p a b", a=3), pj[:, 1, :, 0:TG], sg[:].rearrange("p (a b) -> p a b", a=3), ALU.mult).then_inc(g_out, 1)
                    dve.wait_ge(gates[3], h)
                    keys(0)
                    scores(0)
                    states(0)
                    states(1)
                if gla:
                    square(0)
                if proj:
                    low(h, 2)
                    dve.wait_ge(z_out, h + 1)
                    o1 = oml[:, h:h + 1] if isinstance(h, int) else oml[:, bass.ds(h, 1)]
                    if gla:
                        dve.wait_ge(operand[0], h)
                        dve.wait_ge(operand[1], h)
                    nc.vector.tensor_scalar(kk[:], nz[:], o1, None, ALU.mult).then_inc(key_done, 1)
                if gla:
                    dve.wait_ge(pe_did["SI"], h)
                    nc.vector.tensor_copy(vn[:, NPB], bank("SI")[:, 0:P])
                    nc.vector.tensor_copy(kd8[:], bank("SI")[:, P:2 * P])
                    nc.vector.copy_predicated(sct8[:], mask_s[:], bank("SI")[:, 2 * P:3 * P]).then_inc(out_of["SI"], 1)
                    normed(0)
                    keys(1)
                    scores(1)
                    states(2)
                    gated("OT0", 0)
                    states(3)
                if proj:
                    dve.wait_ge(logf_done, h + 1)
                    nc.vector.tensor_tensor_scan(bb[:], restart[:], fz[:], 0.0, ALU.mult, ALU.add).then_inc(b_step, 1)
                    dve.wait_ge(b_step, h * 2 + 1)
                    dve.wait_ge(key_done, h + 1)
                    if gla:
                        dve.wait_ge(gates[2], h)
                    (bp, bs), (zp, zs), (ep, es) = chunks(bb), chunks(bm), chunks(nz)
                    for b, o, n, w in ((bp, zp, NCH, CH), (bs, zs, NSEQ, SLEN)):
                        last = nc.vector.tensor_tensor(o, b, b[:, :, w // 2:w // 2 + 1].broadcast_to([P, n, w]), ALU.subtract)
                    for b, o, n, w in ((bp, ep, NCH, CH), (bs, es, NSEQ, SLEN)):
                        last = nc.vector.tensor_tensor(o, b[:, :, w - 1:w].broadcast_to([P, n, w]), b, ALU.subtract)
                    last.then_inc(b_step, 1)
                    low(h, 3)
                if gla:
                    square(1)
                    normed(1)
                    sample_states(0)
                    gated("OT1", 1)
                    square(2)
                    normed(2)
                    sample_states(1)
                    gated("SOT", 2)
                if proj:
                    if not (isinstance(h, int) and h == AH - 1):
                        low(h + 1, 0)
                    for i, (dst, src) in enumerate(((qin, qq), (qex, qq))):
                        dve.wait_ge(gates[2 + i], h + 1)
                        if i == 1:
                            xp, xs = chunks(qex)
                            if gla:
                                dve.wait_ge(out_of["SS1"], h)
                            for at, x, w in ((slice(0, NCH), xp, CH), (slice(NCH, NCH + NSEQ), xs, SLEN)):
                                nc.vector.tensor_copy(decay[:, at].rearrange("p (c o) -> p c o", o=1), x[:, :, w - 1:w]).then_inc(decay_done, 1)
                            dve.wait_ge(decay_done, h * 2 + 2)
                        nc.vector.tensor_tensor(dst[:], dst[:], src[:], ALU.mult).then_inc(operand[2 + i], 1)

            heads(dve, body)


def token_tiles(eng, body):
    body(0, 0, False, False)
    body(1, 1, True, False)
    with eng.Fori(1, NT // 2) as pair:
        body(pair * 2, 0, True, True)
        body(pair * 2 + 1, 1, True, True)
    body(NT - 1, (NT - 1) % 2, True, True)


def tile_cols(t):
    return slice(t * P, (t + 1) * P) if isinstance(t, int) else bass.ds(t * P, P)


def phase_output(nc, k, name, nk, w, gated, residual, ln, turn, store):
    with ExitStack() as ctx:
        m = Core(nc, ctx)
        n = name
        RAW = 4 if nk == KD else 3
        w_raw = m.sb(n + "_w_raw", [RAW, D])
        w_h = m.sb(n + "_w_h", [nk, D], F32R)
        w_l = m.sb(n + "_w_l", [nk, D], F32R)
        g_raw = m.sb(n + "_g_raw", [2, nk, P])
        g_h = m.sb(n + "_g_h", [2, nk, P], F32R)
        g_l = m.sb(n + "_g_l", [2, nk, P], F32R)
        x = m.sb(n + "_x", [2, D])
        gain = m.sb(n + "_gain", [D])
        shift = m.sb(n + "_shift", [D])
        stats = m.sb(n + "_stats", [2, 6])
        mv = m.sb(n + "_mv", [2])
        rstd = m.sb(n + "_rstd", [1])
        mhalf = m.sb(n + "_mhalf", [1])
        eps = m.sb(n + "_eps", [1])
        idle = m.sb(n + "_idle", [1])
        py = m.ps(n + "_py", [2, 2, BANK])
        pt = m.ps(n + "_pt", [2, 2, BANK])

        w_loaded = [m.sem(f"{n}_w_loaded{i}") for i in range(RAW)]
        g_loaded = [m.sem(f"{n}_g_loaded{i}") for i in range(2)]
        x_loaded = [m.sem(f"{n}_x_loaded{i}") for i in range(2)]
        stored = [m.sem(f"{n}_stored{i}") for i in range(2)]
        (wh_ready, wl_ready, gh_ready, gl_ready, y_done, sum_done, stats_done, mv_done, rstd_step,
         norm_done, x_ready, turned, th_done, tl_done, ln_loaded, mhalf_set, gain_done) = (
            m.sem(f"{n}_{s}") for s in ("wh_ready wl_ready gh_ready gl_ready y_done sum_done stats_done mv_done "
                                        "rstd_step norm_done x_ready turned th_done tl_done ln_loaded mhalf_set gain_done").split())
        block = ctx.enter_context(nc.Block())
        w_rows = w.rearrange("(a p) e -> a p e", p=P)

        @block.sync
        def _(sp):
            def load_g(t, par, later):
                if later:
                    sp.wait_ge(gl_ready, t - 1)
                sp.dma_start(g_raw[:, par], gated(t)).then_inc(g_loaded[par], 16)

            def load_w(i):
                if i >= RAW:
                    sp.wait_ge(wl_ready, i - RAW + 1)
                sp.dma_start(w_raw[:, i % RAW], w_rows[i]).then_inc(w_loaded[i % RAW], 16)

            load_g(0, 0, False)
            load_w(0)
            load_w(1)
            load_g(1, 1, False)
            for i in range(2, nk):
                load_w(i)

            def body(t, par, ge1, ge2):
                if ge2:
                    load_g(t, par, True)

            token_tiles(sp, body)

        @block.gpsimd
        def _(pool):
            nc.gpsimd.memset(mhalf[:], -0.5).then_inc(mhalf_set, 1)
            nc.gpsimd.memset(eps[:], EPS).then_inc(mhalf_set, 1)
            pool.wait_ge(mhalf_set, 2)
            pool.dma_start(gain[:], ln[0].partition_broadcast(P)).then_inc(ln_loaded, 16)
            pool.dma_start(shift[:], ln[1].partition_broadcast(P)).then_inc(ln_loaded, 16)

            def body(t, par, ge1, ge2):
                pool.wait_ge(mv_done, t + 1)
                nc.gpsimd.tensor_tensor(rstd[:], mv[:, 1:2], eps[:], ALU.add).then_inc(rstd_step, 1)
                pool.wait_ge(rstd_step, t * 2 + 1)
                nc.gpsimd.tensor_tensor(rstd[:], rstd[:], mhalf[:], ALU.pow).then_inc(rstd_step, 1)
                if not ge1:
                    pool.wait_ge(ln_loaded, 32)
                pool.wait_ge(gain_done, t + 1)
                nc.gpsimd.tensor_tensor(x[:, par], x[:, par], shift[:], ALU.add).then_inc(x_ready, 1)

            token_tiles(pool, body)

        @block.tensor
        def _(pe):
            def turn_tile(t, par, later):
                pe.wait_ge(x_ready, t + 1)
                if later:
                    pe.wait_ge(tl_done, t)
                for c in range(KD):
                    last = nc.tensor.transpose(pt[:, par, c // 4, (c % 4) * P:(c % 4 + 1) * P], x[:, par, c * P:(c + 1) * P], k.ident[:])
                last.then_inc(turned, 1)

            def body(t, par, ge1, ge2):
                pe.wait_ge(gl_ready, t + 1)
                if ge2:
                    pe.wait_ge(sum_done, t - 1)
                for kt in range(nk):
                    if not ge1:
                        pe.wait_ge(wl_ready, kt + 1)
                    for half in range(2):
                        cols = slice(half * BANK, (half + 1) * BANK)
                        last = product(nc, py[:, par, half], (g_h[:, par, kt], g_l[:, par, kt]),
                                       (w_h[:, kt, cols], w_l[:, kt, cols]), kt == 0, kt == nk - 1)
                last.then_inc(y_done, 1)
                if turn and ge1:
                    turn_tile(t - 1, 1 - par, not isinstance(t, int) or t >= 3)

            token_tiles(pe, body)
            if turn:
                turn_tile(NT - 1, (NT - 1) % 2, True)

        @block.scalar
        def _(act):
            def high_g(t, par, ge2):
                act.wait_ge(g_loaded[par], (t - par) * 8 + 16)
                if ge2:
                    act.wait_ge(y_done, t - 1)
                round_high(nc, g_h[:, par], g_raw[:, par]).then_inc(gh_ready, 1)

            def load_x(t, par, ge2):
                if ge2:
                    act.wait_ge(stored[par], (t - par) * 8)
                    if turn:
                        act.wait_ge(turned, t - 1)
                act.dma_start(x[:, par], residual(t)).then_inc(x_loaded[par], 16)

            def finish(t, par):
                act.wait_ge(x_ready, t + 1)
                act.dma_start(store(t), x[:, par]).then_inc(stored[par], 16)
                if turn:
                    act.wait_ge(turned, t + 1)
                    round_high(nc, k.act_h[:, :, tile_cols(t)],
                               pt[:, par].rearrange("p a (b q) -> p (a b) q", b=4)).then_inc(th_done, 1)

            load_x(0, 0, False)
            load_x(1, 1, False)
            high_g(0, 0, False)
            for i in range(nk):
                act.wait_ge(w_loaded[i % RAW], 16 * (i // RAW + 1))
                round_high(nc, w_h[:, i], w_raw[:, i % RAW]).then_inc(wh_ready, 1)
            high_g(1, 1, False)

            def body(t, par, ge1, ge2):
                if ge1:
                    if not (isinstance(t, int) and t == NT - 1):
                        high_g(t + 1, 1 - par, True)
                    finish(t - 1, 1 - par)
                    if ge2 or t == 1:
                        if not (isinstance(t, int) and t == NT - 1):
                            load_x(t + 1, 1 - par, True)

            token_tiles(act, body)
            finish(NT - 1, (NT - 1) % 2)
            act.wait_ge(stored[0], 16 * ((NT + 1) // 2))
            act.wait_ge(stored[1], 16 * (NT // 2))

        @block.vector
        def _(dve):
            def low_g(t, par):
                dve.wait_ge(gh_ready, t + 1)
                round_low(nc, g_l[:, par], g_raw[:, par], g_h[:, par]).then_inc(gl_ready, 1)

            def turned_low(t, par):
                dve.wait_ge(th_done, t + 1)
                at = k.act_h[:, :, tile_cols(t)]
                round_low(nc, k.act_l[:, :, tile_cols(t)], pt[:, par].rearrange("p a (b q) -> p (a b) q", b=4), at).then_inc(tl_done, 1)

            dve.sem_inc(tl_done, 1)
            low_g(0, 0)
            for i in range(nk):
                dve.wait_ge(wh_ready, i + 1)
                round_low(nc, w_l[:, i], w_raw[:, i % RAW], w_h[:, i]).then_inc(wl_ready, 1)
            low_g(1, 1)

            def norm(t, par):
                dve.wait_ge(y_done, t + 1)
                dve.wait_ge(x_loaded[par], (t - par) * 8 + 16)
                nc.vector.scalar_tensor_tensor(out=x[:, par].rearrange("p (a b) -> p a b", a=2), in0=x[:, par].rearrange("p (a b) -> p a b", a=2), scalar=ALPHA, in1=py[:, par],
                                               op0=ALU.mult, op1=ALU.add).then_inc(sum_done, 1)
                dve.wait_ge(sum_done, t + 1)
                for half in range(2):
                    nc.vector.bn_stats(stats[:, half], x[:, par, half * BANK:(half + 1) * BANK]).then_inc(stats_done, 1)
                dve.wait_ge(stats_done, t * 2 + 2)
                nc.vector.memset(idle[:], 0.0)
                nc.vector.bn_aggr(mv[:], flat(stats[:])).then_inc(mv_done, 1)
                dve.wait_ge(rstd_step, t * 2 + 2)
                nc.vector.tensor_scalar(x[:, par], x[:, par], mv[:, 0:1], rstd[:, 0:1], ALU.subtract, ALU.mult).then_inc(norm_done, 1)
                if isinstance(t, int) and t == 0:
                    dve.wait_ge(ln_loaded, 32)
                dve.wait_ge(norm_done, t + 1)
                nc.vector.tensor_tensor(x[:, par], x[:, par], gain[:], ALU.mult).then_inc(gain_done, 1)

            def body(t, par, ge1, ge2):
                if ge1:
                    norm(t - 1, 1 - par)
                    if not (isinstance(t, int) and t == NT - 1):
                        low_g(t + 1, 1 - par)
                    if turn:
                        turned_low(t - 1, 1 - par)

            token_tiles(dve, body)
            norm(NT - 1, (NT - 1) % 2)
            if turn:
                turned_low(NT - 1, (NT - 1) % 2)


def phase_latents(nc, k):
    d = k.d
    KV = KVL + RD
    half = RD // 2
    with ExitStack() as ctx:
        m = Core(nc, ctx)
        w_raw = m.sb("c_w_raw", [2, KV + QL])
        w_h = m.sb("c_w_h", [KD, KV + QL], F32R)
        w_l = m.sb("c_w_l", [KD, KV + QL], F32R)
        cn = m.sb("c_cn", [2, KVL])
        krn = m.sb("c_krn", [2, 2, RD])
        cqn = m.sb("c_cqn", [2, QL])
        sq = m.sb("c_sq", [QL])
        rt = m.sb("c_rt", [2, 2, half])
        cos = m.sb("c_cos", [NT, half])
        sin = m.sb("c_sin", [NT, half])
        ms = m.sb("c_ms", [2])
        inv_n = m.sb("c_inv_n", [2])
        rs = m.sb("c_rs", [2])
        mhalf = m.sb("c_mhalf", [2])
        kvg = m.sb("c_kvg", [KVL])
        qg = m.sb("c_qg", [QL])
        pkv = m.ps("c_pkv", [2, BANK])
        pq = m.ps("c_pq", [2, BANK])
        pc = m.ps("c_pc", [2, 2, BANK])

        w_loaded = [m.sem(f"c_w_loaded{i}") for i in range(2)]
        stored = [m.sem(f"c_stored{i}") for i in range(2)]
        (wh_ready, wl_ready, const_loaded, const_set, kv_done, q_done, ms_done, rs_step, c_ready, rope_step,
         kr_ready, q_ready, turned_k, turned_q, th_k, th_q, tl_k, tl_q) = (m.sem("c_" + s) for s in (
            "wh_ready wl_ready const_loaded const_set kv_done q_done ms_done rs_step c_ready rope_step "
            "kr_ready q_ready turned_k turned_q th_k th_q tl_k tl_q").split())
        block = ctx.enter_context(nc.Block())
        tiles = range(NT)

        @block.sync
        def _(sp):
            kv_rows = d["w_dkv"].rearrange("(a p) e -> a p e", p=P)
            q_rows = d["w_in_b"][0].rearrange("(a p) e -> a p e", p=P)
            for i in range(KD):
                if i >= 2:
                    sp.wait_ge(wl_ready, i - 1)
                sp.dma_start(w_raw[:, i % 2, 0:KV], kv_rows[i]).then_inc(w_loaded[i % 2], 16)
                sp.dma_start(w_raw[:, i % 2, KV:], q_rows[i, :, 0:QL]).then_inc(w_loaded[i % 2], 16)
            for t in tiles:
                ckv, kr = ((d["ckv_prompt"][0, t * P:(t + 1) * P], d["krope_prompt"][0, t * P:(t + 1) * P]) if t < NPB
                           else (d["ckv_sample"].rearrange("b l e -> (b l) e"), d["krope_sample"].rearrange("b l e -> (b l) e")))
                sp.wait_ge(c_ready, t + 1)
                sp.dma_start(ckv, cn[:, t % 2]).then_inc(stored[t % 2], 16)
                sp.wait_ge(kr_ready, t + 1)
                sp.dma_start(kr, krn[:, t % 2, 0]).then_inc(stored[t % 2], 16)
            sp.wait_ge(stored[0], 32 * ((NT + 1) // 2))
            sp.wait_ge(stored[1], 32 * (NT // 2))

        @block.gpsimd
        def _(pool):
            nc.gpsimd.memset(mhalf[:], -0.5).then_inc(const_set, 1)
            nc.gpsimd.memset(inv_n[:, 0:1], 1.0 / KVL).then_inc(const_set, 1)
            nc.gpsimd.memset(inv_n[:, 1:2], 1.0 / QL).then_inc(const_set, 1)
            pool.dma_start(cos[:].rearrange("p a b -> p (a b)"), d["cos_nat"]).then_inc(const_loaded, 16)
            pool.dma_start(sin[:].rearrange("p a b -> p (a b)"), d["sin_nat"]).then_inc(const_loaded, 16)
            pool.dma_start(kvg[:], d["kv_norm_g"].partition_broadcast(P)).then_inc(const_loaded, 16)
            pool.dma_start(qg[:], d["q_norm_g"][0].partition_broadcast(P)).then_inc(const_loaded, 16)
            pool.wait_ge(const_set, 3)
            for t in tiles:
                pool.wait_ge(ms_done, 2 * t + 2)
                if t:
                    pool.wait_ge(q_ready, t)
                nc.gpsimd.tensor_tensor(rs[:], ms[:], inv_n[:], ALU.mult).then_inc(rs_step, 1)
                pool.wait_ge(rs_step, 3 * t + 1)
                nc.gpsimd.tensor_scalar(rs[:], rs[:], 1.0, EPS, ALU.mult, ALU.add).then_inc(rs_step, 1)
                pool.wait_ge(rs_step, 3 * t + 2)
                nc.gpsimd.tensor_tensor(rs[:], rs[:], mhalf[:], ALU.pow).then_inc(rs_step, 1)

        @block.tensor
        def _(pe):
            def turn(t):
                par = t % 2
                pe.wait_ge(c_ready, t + 1)
                pe.wait_ge(kr_ready, t + 1)
                pe.wait_ge(q_ready, t + 1)
                if t >= 2:
                    pe.wait_ge(tl_k, min(t - 1, NPB))
                    pe.wait_ge(tl_q, t - 1)
                if t < NPB:
                    for c in range(2):
                        nc.tensor.transpose(pc[:, par, 0, c * P:(c + 1) * P], cn[:, par, c * P:(c + 1) * P], k.ident[:])
                    nc.tensor.transpose(pc[:, par, 0, 2 * P:3 * P], krn[:, par].rearrange("p a b -> p (a b)"), k.ident[:]).then_inc(turned_k, 1)
                for c in range(4):
                    last = nc.tensor.transpose(pc[:, par, 1, c * P:(c + 1) * P], cqn[:, par, c * P:(c + 1) * P], k.ident[:])
                last.then_inc(turned_q, 1)

            for t in tiles:
                par = t % 2
                if t >= 2:
                    pe.wait_ge(kr_ready, t - 1)
                    pe.wait_ge(c_ready, t - 1)
                    pe.wait_ge(q_ready, t - 1)
                x = [(k.act_h[:, kt, t * P:(t + 1) * P], k.act_l[:, kt, t * P:(t + 1) * P]) for kt in range(KD)]
                for kt in range(KD):
                    if t == 0:
                        pe.wait_ge(wl_ready, kt + 1)
                    last_kv = product(nc, pkv[:, par, 0:KV], x[kt], (w_h[:, kt, 0:KV], w_l[:, kt, 0:KV]), kt == 0, kt == KD - 1)
                    last = product(nc, pq[:, par], x[kt], (w_h[:, kt, KV:], w_l[:, kt, KV:]), kt == 0, kt == KD - 1)
                last.then_inc(q_done, 1)
                if t >= 1:
                    turn(t - 1)
            turn(NT - 1)

        @block.scalar
        def _(act):
            for i in range(KD):
                act.wait_ge(w_loaded[i % 2], 32 * (i // 2 + 1))
                round_high(nc, w_h[:, i], w_raw[:, i % 2]).then_inc(wh_ready, 1)

            def turned_high(t):
                par, cols = t % 2, slice(t * P, (t + 1) * P)
                if t < NPB:
                    act.wait_ge(turned_k, t + 1)
                    round_high(nc, k.ct_h[:, :, cols], pc[:, par, 0, 0:2 * P].rearrange("p (a q) -> p a q", a=2))
                    round_high(nc, k.kr_h[:, cols], pc[:, par, 0, 2 * P:3 * P]).then_inc(th_k, 1)
                act.wait_ge(turned_q, t + 1)
                round_high(nc, k.cq_h[:, :, cols], pc[:, par, 1].rearrange("p (a q) -> p a q", a=4)).then_inc(th_q, 1)

            for t in tiles:
                par = t % 2
                act.wait_ge(q_done, t + 1)
                if t:
                    act.wait_ge(rs_step, 3 * t)
                    act.wait_ge(ms_done, 2 * t)
                nc.scalar.activation(sq[:, 0:KVL], pkv[:, par, 0:KVL], ACT.Square, accum_out=ms[:, 0:1]).then_inc(ms_done, 1)
                act.wait_ge(ms_done, 2 * t + 1)
                nc.scalar.activation(sq[:], pq[:, par], ACT.Square, accum_out=ms[:, 1:2]).then_inc(ms_done, 1)
                if t:
                    turned_high(t - 1)
            turned_high(NT - 1)

        @block.vector
        def _(dve):
            for i in range(KD):
                dve.wait_ge(wh_ready, i + 1)
                round_low(nc, w_l[:, i], w_raw[:, i % 2], w_h[:, i]).then_inc(wl_ready, 1)
            dve.wait_ge(const_loaded, 64)

            def turned_low(t):
                par, cols = t % 2, slice(t * P, (t + 1) * P)
                if t < NPB:
                    dve.wait_ge(th_k, t + 1)
                    round_low(nc, k.ct_l[:, :, cols], pc[:, par, 0, 0:2 * P].rearrange("p (a q) -> p a q", a=2), k.ct_h[:, :, cols])
                    round_low(nc, k.kr_l[:, cols], pc[:, par, 0, 2 * P:3 * P], k.kr_h[:, cols]).then_inc(tl_k, 1)
                dve.wait_ge(th_q, t + 1)
                round_low(nc, k.cq_l[:, :, cols], pc[:, par, 1].rearrange("p (a q) -> p a q", a=4), k.cq_h[:, :, cols]).then_inc(tl_q, 1)

            for t in tiles:
                par = t % 2
                dve.wait_ge(ms_done, 2 * t + 2)
                if t >= 2:
                    dve.wait_ge(stored[par], 32 * (t // 2))
                    dve.wait_ge(turned_q, t - 1)
                x = pkv[:, par, KVL:KV].rearrange("p (a b) -> p a b", a=2)
                if t:
                    dve.wait_ge(kr_ready, t)
                both = lambda a: a[:, t:t + 1].broadcast_to([P, 2, half])
                nc.vector.tensor_tensor(rt[:, 0], x, both(cos), ALU.mult).then_inc(rope_step, 1)
                nc.vector.tensor_tensor(rt[:, 1], x, both(sin), ALU.mult).then_inc(rope_step, 1)
                dve.wait_ge(rope_step, 2 * t + 2)
                for copy in range(2):
                    nc.vector.tensor_tensor(krn[:, par, copy, 0:half], rt[:, 0, 0], rt[:, 1, 1], ALU.subtract)
                    last = nc.vector.tensor_tensor(krn[:, par, copy, half:], rt[:, 1, 0], rt[:, 0, 1], ALU.add)
                last.then_inc(kr_ready, 1)
                dve.wait_ge(rs_step, 3 * t + 3)
                nc.vector.scalar_tensor_tensor(out=cn[:, par], in0=pkv[:, par, 0:KVL], scalar=rs[:, 0:1], in1=kvg[:], op0=ALU.mult, op1=ALU.mult).then_inc(c_ready, 1)
                nc.vector.scalar_tensor_tensor(out=cqn[:, par], in0=pq[:, par], scalar=rs[:, 1:2], in1=qg[:], op0=ALU.mult, op1=ALU.mult).then_inc(q_ready, 1)
                if t:
                    turned_low(t - 1)
            turned_low(NT - 1)


def phase_gates(nc, k):
    d = k.d
    w_in = d["w_in_b"][0].rearrange("(a p) e -> p a e", p=P)
    with ExitStack() as ctx:
        m = Core(nc, ctx)
        w_raw = m.sb("g_w_raw", [2, KD, P])
        w_h = m.sb("g_w_h", [2, KD, P], F32R)
        w_l = m.sb("g_w_l", [2, KD, P], F32R)
        sg = m.sb("g_sg", [2, T])
        pj = m.ps("g_pj", [2, 3, BANK])
        w_loaded = [m.sem(f"g_w_loaded{i}") for i in range(2)]
        stored = [m.sem(f"g_stored{i}") for i in range(2)]
        wh_ready, wl_ready, proj_done, sigmoid_done, out_done = (m.sem("g_" + s) for s in "wh_ready wl_ready proj_done sigmoid_done out_done".split())
        block = ctx.enter_context(nc.Block())

        def tiles(eng, body):
            body(0, 0, False)
            body(1, 1, False)
            with eng.Fori(1, HEADS // 2) as pair:
                body(pair * 2, 0, True)
                body(pair * 2 + 1, 1, True)

        def wide(x):
            return x.rearrange("p (a b) -> p a b", a=3)

        @block.sync
        def _(sp):
            def body(h, par, later):
                if later:
                    sp.wait_ge(wl_ready, h - 1)
                cols = bass.ds(h * P + QL, P)
                sp.dma_start(w_raw[:, par], w_in[:, :, cols]).then_inc(w_loaded[par], 16)
                if later:
                    store(h - 2, par)

            def store(h, par):
                sp.wait_ge(out_done, h + 1)
                sp.dma_start(d["scratch_gate"][bass.ds(h, 1)].rearrange("o p t -> p (o t)"), sg[:, par]).then_inc(stored[par], 16)

            tiles(sp, body)
            for par in range(2):
                store(HEADS - 2 + par, par)
            for par in range(2):
                sp.wait_ge(stored[par], 16 * (HEADS // 2))

        @block.tensor
        def _(pe):
            def body(h, par, later):
                pe.wait_ge(wl_ready, h + 1)
                if later:
                    pe.wait_ge(out_done, h - 1)
                for tg in range(NTG):
                    cols = slice(tg * TG, (tg + 1) * TG)
                    for kt in range(KD):
                        mm = product(nc, pj[:, par, tg, 0:TG], (w_h[:, par, kt], w_l[:, par, kt]),
                                     (k.act_h[:, kt, cols], k.act_l[:, kt, cols]), kt == 0, kt == KD - 1)
                mm.then_inc(proj_done, 1)
            tiles(pe, body)

        @block.scalar
        def _(act):
            def high(h, par, later):
                act.wait_ge(w_loaded[par], (h - par) * 8 + 16)
                if later:
                    act.wait_ge(proj_done, h - 1)
                round_high(nc, w_h[:, par], w_raw[:, par]).then_inc(wh_ready, 1)

            def silu(h, par, later):
                act.wait_ge(proj_done, h + 1)
                if later:
                    act.wait_ge(stored[par], (h - par) * 8)
                nc.scalar.activation(wide(sg[:, par]), pj[:, par, :, 0:TG], ACT.Sigmoid).then_inc(sigmoid_done, 1)
            high(0, 0, False)
            high(1, 1, False)

            silu(0, 0, False)
            high(2, 0, True)
            silu(1, 1, False)
            high(3, 1, True)
            with act.Fori(2, HEADS - 2, 2) as h:
                silu(h, 0, True)
                high(h + 2, 0, True)
                silu(h + 1, 1, True)
                high(h + 3, 1, True)
            silu(HEADS - 2, 0, True)
            silu(HEADS - 1, 1, True)

        @block.vector
        def _(dve):
            def low(h, par):
                dve.wait_ge(wh_ready, h + 1)
                round_low(nc, w_l[:, par], w_raw[:, par], w_h[:, par]).then_inc(wl_ready, 1)

            def silu(h, par):
                dve.wait_ge(sigmoid_done, h + 1)
                nc.vector.tensor_tensor(wide(sg[:, par]), pj[:, par, :, 0:TG], wide(sg[:, par]), ALU.mult).then_inc(out_done, 1)
            low(0, 0)
            low(1, 1)
            with dve.Fori(0, HEADS - 2, 2) as h:
                silu(h, 0)
                low(h + 2, 0)
                silu(h + 1, 1)
                low(h + 3, 1)
            silu(HEADS - 2, 0)
            silu(HEADS - 1, 1)


PAIRS = HEADS // 2
QB = SEQ // P
GQ = 2 * P
GROUPS = SEQ // GQ
ORDER = [(0, 0), (1, 3), (0, 1), (1, 2), (1, 1), (0, 2), (1, 0), (0, 3)]
NG = len(ORDER)
UNITS = 2 * NG


def unit(u):
    return u // 4 * 2 + u % 2, u // 2 % 2


def place_of(u):
    G, half = unit(u)
    e, g = ORDER[G]
    return e, 2 * g + half, g


TSTEPS = [(u, i, min(4, 2 * place_of(u)[2] + 2 - i)) for u in range(UNITS)
          for i in range(1 - unit(u)[1], 2 * place_of(u)[2] + 2, 4)]
PROJ = ["QA0", "QA1", "QA2", "QB0", "R0", "R1", "R2", "QB1", "QB2", "UT", "KA0", "KA1", "KB0", "KB1",
        "V0", "V1", "QL", "V2", "V3"]
READS = ["QA0", "QA1", "QA2", "QB0", "R0", "QB1", "R1", "QB2", "UT", "KA0", "R2", "KA1", "KB0", "KB1",
         "V0", "V1", "QL", "V2", "V3"]
PROJ_BANK = [i % 8 for i in range(12)] + [4, 5, 6, 7, 4, 5, 6]
NP = len(PROJ)
HIGH_COUNT = {s: sum(x[0] != "R" for x in PROJ[:i + 1]) for i, s in enumerate(PROJ)}
HIGHS = HIGH_COUNT[PROJ[-1]]
STEP = {name: i for i, name in enumerate(PROJ)}
EARLY = {14: ["QA0"], 15: ["QA1"], 16: ["QA2", "QB0"]}
NE = 4
PIECES = [2 * QD] * 4 + [2 * GQ] * 2
WPARTS = len(PIECES)


def phase_heads(nc, k):
    d = k.d
    with ExitStack() as ctx:
        m = Core(nc, ctx)
        OUK, OUV, WW = 4 * 2 * QD, 4 * 2 * QD + 2 * GQ, 4 * 2 * QD + 4 * GQ
        w_raw = m.sb("h_w_raw", [WW])
        w_h = m.sb("h_w_h", [WW], F32R)
        w_l = m.sb("h_w_l", [WW], F32R)
        qn_h, qn_l = m.sb("h_qn_h", [2, T], F32R), m.sb("h_qn_l", [2, T], F32R)
        rq = m.sb("h_rq", [2, T], F32R)
        kt_h, kt_l = m.sb("h_kt_h", [2, SEQ], F32R), m.sb("h_kt_l", [2, SEQ], F32R)
        v_h, v_l = m.sb("h_v_h", [QB, GQ], F32R), m.sb("h_v_l", [QB, GQ], F32R)
        p = m.sb("h_p", [3, SEQ])
        PLACES = [max(2 * g + 2 for i, (e, g) in enumerate(ORDER) if i % 2 == slot) for slot in range(2)]
        pt_h = [m.sb(f"h_pt_h{i}", [n, GQ], F32R) for i, n in enumerate(PLACES)]
        pt_l = [m.sb(f"h_pt_l{i}", [n, GQ], F32R) for i, n in enumerate(PLACES)]
        cos, sin = m.sb("h_cos", [T]), m.sb("h_sin", [T])
        gate = m.sb("h_gate", [2, GQ])
        ukt = m.sb("h_ukt", [2, KVL])
        qs = m.sb("h_qs", [2, P])
        qlat = m.sb("h_qlat", [4, P])
        qr = m.sb("h_qr", [2, P])
        mx = m.sb("h_mx", [3, 1])
        rsum = m.sb("h_rsum", [3, 1])
        bank = m.ps("h_ps", [8, BANK])
        names = ("uq_loaded ukv_loaded zeroed wh_ready wl_ready table_loaded proj_done proj_high proj_out rope_step rope_sum rq_high rq_out s_done masked max_done "
                 "exp_done inv_done p_ready t_done t_high t_out pv_done o_out ql_stored qr_stored qs_ready").split()
        S = {n: m.sem("h_" + n) for n in names}
        gate_loaded = [m.sem(f"h_gate_loaded{i}") for i in range(2)]
        og_stored = [m.sem(f"h_og_stored{i}") for i in range(2)]
        block = ctx.enter_context(nc.Block())

        uq = lambda x: x[:, 0:OUK].rearrange("p (a e) -> p a e", a=4)
        uk = lambda x: x[:, OUK:OUV].rearrange("p (a e) -> p a e", a=2)
        uv = lambda x: x[:, OUV:WW].rearrange("p (a e) -> p a e", a=2)

        def view(x, n):
            return x[:, 0, 0:n] if n <= BANK else x[:, :, 0:n // 2]

        def scores_of(u):
            slot = 2 * (u % 2)
            return view(bank[:, slot:slot + 2], P * (place_of(u)[1] + 1))

        def weights_of(u):
            n = P * (place_of(u)[1] + 1)
            x = p[:, u % 3, 0:n]
            return x if n <= BANK else x.rearrange("p (a b) -> p a b", a=2)

        def last_turn(u):
            return max(i for i, (uu, _, _) in enumerate(TSTEPS) if uu == u) + 1

        def piece(x, i):
            return x[:, sum(PIECES[:i]):sum(PIECES[:i + 1])]

        flat_p = p[:].rearrange("p a b -> p (a b)")

        def rope_part(tg, i, n=1):
            at = (tg % 2) * 4 * TG + i * TG
            return flat_p[:, at:at + n * TG]

        def rope_sums(tg):
            return rope_part(tg, 2, 2)[0:RD].rearrange("p (a b) -> p a b", a=2)

        def pairs(eng, body):
            body(0, True, False)
            with eng.Fori(1, PAIRS - 1) as pr:
                body(pr, False, False)
            body(PAIRS - 1, False, True)

        @block.sync
        def _(sp):
            def load_w(pr, first):
                if not first:
                    sp.wait_ge(S["wl_ready"], pr * WPARTS)
                    sp.wait_ge(S["proj_done"], pr * NP + (STEP["UT"] + 1 - NP))
                for e in range(2):
                    for at, col, w in ((e * NOPE, 0, NOPE), (2 * NOPE + e * RD, NOPE, RD)):
                        sp.dma_start(uq(w_raw)[:, :, at:at + w], d["w_uq"][0].rearrange("(a p) e -> p a e", p=P)[:, :, bass.ds(pr * (2 * QD) + (e * QD + col), w)]).then_inc(S["uq_loaded"], 16)
                for dst, src in ((uk, "w_uk"), (uv, "w_uv")):
                    sp.dma_start(dst(w_raw), d[src].rearrange("(a p) h n -> p a (h n)", p=P)[:, :, bass.ds(pr * GQ, GQ)]).then_inc(S["ukv_loaded"], 16)

            def rows(x, pr, e):
                return d[x].rearrange("(r e) p t -> r e p t", e=2)[bass.ds(pr, 1), e].rearrange("o p t -> p (o t)")

            def load_gate(pr, g, first):
                if not (first and g < 2):
                    sp.wait_ge(og_stored[g % 2], pr * 64 + 16 * (g // 2))
                e, qg = ORDER[g]
                sp.dma_start(gate[:, g % 2], rows("scratch_gate", pr, e)[:, GQ * qg:GQ * qg + GQ]).then_inc(gate_loaded[g % 2], 16)

            def body(pr, first, last):
                load_gate(pr, 0, first)
                load_gate(pr, 1, first)
                sp.wait_ge(S["proj_out"], pr * NP + NP)
                sp.dma_start(d["scratch_ql"][bass.ds(pr, 1)].rearrange("o p t -> p (o t)"), flat(qlat[:])).then_inc(S["ql_stored"], 16)
                sp.dma_start(d["scratch_qr"][bass.ds(pr, 1)].rearrange("o p t -> p (o t)"), flat(qr[0:RD])).then_inc(S["qr_stored"], 16)
                if not last:
                    load_w(pr + 1, False)
                for g in range(NG):
                    sp.wait_ge(S["o_out"], pr * 8 + g + 1)
                    e, qg = ORDER[g]
                    sp.dma_start(rows("scratch_og", pr, e)[:, GQ * qg:GQ * qg + GQ], gate[:, g % 2]).then_inc(og_stored[g % 2], 16)
                    if g + 2 < NG:
                        load_gate(pr, g + 2, False)

            load_w(0, True)
            sp.dma_start(cos[:], d["cos_t"]).then_inc(S["table_loaded"], 16)
            sp.dma_start(sin[:], d["sin_t"]).then_inc(S["table_loaded"], 16)
            pairs(sp, body)
            sp.wait_ge(S["ql_stored"], 16 * PAIRS)
            sp.wait_ge(S["qr_stored"], 16 * PAIRS)
            for s in og_stored:
                sp.wait_ge(s, 64 * PAIRS)

        @block.gpsimd
        def _(pool):
            def body(pr, first, last):
                for tg in range(NTG):
                    pool.wait_ge(S["rope_step"], pr * 3 + tg + 1)
                    for e in range(2):
                        rows = slice(e * RD, (e + 1) * RD)
                        last_op = nc.gpsimd.tensor_tensor(rope_sums(tg)[:, e], rope_part(tg, 0)[rows], rope_part(tg, 1)[rows], ALU.add)
                    last_op.then_inc(S["rope_sum"], 1)
            pairs(pool, body)

        @block.tensor
        def _(pe):
            def W(v, a, c):
                return v(w_h)[:, a, c], v(w_l)[:, a, c]

            def proj(pr, s, first):
                i, b = STEP[s], PROJ_BANK[STEP[s]]
                earlier = [j for j in range(i) if PROJ_BANK[j] == b]
                if s == "QA0":
                    pe.wait_ge(S["wl_ready"], pr * WPARTS + 4)
                if s == "UT":
                    pe.wait_ge(S["wl_ready"], pr * WPARTS + WPARTS)
                if earlier:
                    pe.wait_ge(S["proj_out"], pr * NP + earlier[-1] + 1)
                elif not first:
                    if b < 4:
                        pe.wait_ge(S["exp_done"], pr * UNITS - 1 + b // 2)
                    elif b < 6:
                        pe.wait_ge(S["t_out"], pr * len(TSTEPS))
                    else:
                        pe.wait_ge(S["o_out"], pr * NG)
                if s == "QL":
                    pe.wait_ge(S["qs_ready"], pr * 2 + 2)
                    for j in range(4):
                        e, a = j // 2, j % 2
                        mm = nc.tensor.matmul(bank[:, b, j * P:j * P + P], ukt[:, e, a * P:a * P + P], qs[:, e], start=True, stop=True)
                elif s[0] in "QR":
                    tg = int(s[-1])
                    cols = slice(tg * TG, tg * TG + TG)
                    for a in range(4):
                        if s[0] == "R":
                            left = W(uq, a, slice(2 * NOPE, 2 * QD))
                        else:
                            o = NOPE * (s[1] == "B")
                            left = W(uq, a, slice(o, o + NOPE))
                        mm = product(nc, bank[:, b, 0:TG], left, (k.cq_h[:, a, cols], k.cq_l[:, a, cols]), a == 0, a == 3)
                elif s == "UT":
                    for j in range(4):
                        e, a = j // 2, j % 2
                        mm = nc.tensor.transpose(bank[:, b, j * P:j * P + P], uk(w_raw)[:, a, e * P:e * P + P], k.ident[:])
                elif s[0] == "K":
                    o, cols = P * (s[1] == "B"), slice(BANK * int(s[2]), BANK * int(s[2]) + BANK)
                    for a in range(2):
                        mm = product(nc, bank[:, b], W(uk, a, slice(o, o + P)), (k.ct_h[:, a, cols], k.ct_l[:, a, cols]), a == 0, a == 1)
                else:
                    for j in range(2):
                        cols = slice((2 * int(s[1]) + j) * P, (2 * int(s[1]) + j) * P + P)
                        for a in range(2):
                            mm = product(nc, bank[:, b, j * GQ:j * GQ + GQ], (k.ct_h[:, a, cols], k.ct_l[:, a, cols]), W(uv, a, slice(0, GQ)), a == 0, a == 1)
                mm.then_inc(S["proj_done"], 1)

            def scores(pr, u):
                e, qb, g = place_of(u)
                if u < 2:
                    pe.wait_ge(S["proj_out"], pr * NP + STEP[("KA1", "KB1")[u]] + 1)
                    pe.wait_ge(S["rq_out"], pr * 3 + (1, 3)[u])
                else:
                    pe.wait_ge(S["exp_done"], pr * UNITS + u - 1)
                q = slice(qb * P, qb * P + P)
                n = max(GQ, P * (qb + 1))
                w = n if n <= BANK else n // 2
                for c in range(n // w):
                    out, kc = bank[:, 2 * (u % 2) + c, 0:w], slice(c * w, c * w + w)
                    product(nc, out, (qn_h[:, e, q], qn_l[:, e, q]), (kt_h[:, e, kc], kt_l[:, e, kc]), True, False)
                    nc.tensor.matmul(out, rq[:, e, q], k.kr_l[:, kc], start=False, stop=False)
                    mm = nc.tensor.matmul(out, rq[:, e, q], k.kr_h[:, kc], start=False, stop=True)
                mm.then_inc(S["s_done"], 1)

            def turn(pr, u):
                e, qb, g = place_of(u)
                pe.wait_ge(S["p_ready"], pr * UNITS + u + 1)
                for i, (uu, place, w) in enumerate(TSTEPS):
                    if uu != u:
                        continue
                    if i >= 2:
                        pe.wait_ge(S["t_out"], pr * len(TSTEPS) + i - 1)
                    else:
                        pe.wait_ge(S["proj_out"], pr * NP + STEP[("QL", "V2")[i]] + 1)
                    for j in range(w):
                        key = 2 * g + 1 - (place + j)
                        mm = nc.tensor.transpose(bank[:, 4 + i % 2, j * P:j * P + P], p[:, u % 3, key * P:(key + 1) * P], k.ident[:])
                    mm.then_inc(S["t_done"], 1)

            def values(pr, G):
                e, g = ORDER[G]
                pe.wait_ge(S["t_out"], pr * len(TSTEPS) + last_turn(G // 2 * 4 + 2 + G % 2))
                if G == 0:
                    pe.wait_ge(S["proj_out"], pr * NP + NP)
                if G >= 2:
                    pe.wait_ge(S["o_out"], pr * NG + G - 1)
                nb = 2 * (g + 1)
                for i in range(nb):
                    b, cols = nb - 1 - i, slice(e * P, e * P + P)
                    mm = product(nc, bank[:, 6 + G % 2, 0:GQ], (v_h[:, b, cols], v_l[:, b, cols]),
                                 (pt_h[G % 2][:, i], pt_l[G % 2][:, i]), i == 0, i == nb - 1)
                mm.then_inc(S["pv_done"], 1)

            pe.wait_ge(S["zeroed"], 4)
            for s in PROJ[:NE]:
                proj(0, s, True)

            def body(pr, first, last):
                for s in PROJ[NE:]:
                    if s in ("V0", "V1"):
                        scores(pr, int(s[1]))
                    proj(pr, s, first)
                for u in range(UNITS):
                    if u + 2 < UNITS:
                        scores(pr, u + 2)
                    if u >= 4 and u % 4 < 2:
                        values(pr, u // 4 * 2 - 2 + u % 2)
                    if u in EARLY and not last:
                        for s in EARLY[u]:
                            proj(pr + 1, s, False)
                    turn(pr, u)
                values(pr, NG - 2)
                if not last:
                    for s in EARLY[UNITS]:
                        proj(pr + 1, s, False)
                values(pr, NG - 1)
            pairs(pe, body)

        @block.scalar
        def _(act):
            def split(pr, i):
                if i == 0:
                    act.wait_ge(S["uq_loaded"], pr * 64 + 64)
                    if not (isinstance(pr, int) and pr == 0):
                        act.wait_ge(S["proj_done"], pr * NP)
                if i == 4:
                    act.wait_ge(S["ukv_loaded"], pr * 32 + 32)
                round_high(nc, piece(w_h, i), piece(w_raw, i)).then_inc(S["wh_ready"], 1)

            def proj(pr, s, first):
                i, b = STEP[s], bank[:, PROJ_BANK[STEP[s]]]
                if s[0] == "R":
                    tg = int(s[1])
                    act.wait_ge(S["rope_sum"], pr * 3 + tg + 1)
                    if tg == 2:
                        if not first:
                            act.wait_ge(S["qr_stored"], pr * 16)
                        nc.scalar.copy(qr[0:RD], rope_sums(tg)[:, :, SEQ - 2 * TG:TG])
                    nc.scalar.activation(rq[0:RD, :, tg * TG:tg * TG + TG], rope_sums(tg), ACT.Identity, scale=SCALE).then_inc(S["rq_high"], 1)
                    return
                act.wait_ge(S["proj_done"], pr * NP + i + 1)
                if s == "UT":
                    nc.scalar.copy(flat(ukt[:]), b).then_inc(S["proj_high"], 1)
                elif s == "QL":
                    if not first:
                        act.wait_ge(S["ql_stored"], pr * 16)
                    nc.scalar.copy(flat(qlat[:]), b).then_inc(S["proj_high"], 1)
                elif s[0] == "Q":
                    e, tg = "AB".index(s[1]), int(s[2])
                    if tg == 2:
                        nc.scalar.copy(qs[:, e], b[:, SEQ - 2 * TG:TG]).then_inc(S["qs_ready"], 1)
                    nc.scalar.activation(qn_h[:, e, tg * TG:tg * TG + TG], b[:, 0:TG], ACT.Identity, scale=SCALE).then_inc(S["proj_high"], 1)
                elif s[0] == "K":
                    e, c = "AB".index(s[1]), int(s[2])
                    round_high(nc, kt_h[:, e, c * BANK:(c + 1) * BANK], b).then_inc(S["proj_high"], 1)
                else:
                    c = int(s[1])
                    round_high(nc, flat(v_h[:, 2 * c:2 * c + 2]), b).then_inc(S["proj_high"], 1)

            def exp(pr, u):
                act.wait_ge(S["max_done"], pr * UNITS + u + 1)
                if u >= 3:
                    act.wait_ge(S["t_done"], pr * len(TSTEPS) + last_turn(u - 3))
                nc.scalar.activation(weights_of(u), scores_of(u), ACT.Exp, bias=mx[:, u % 3], accum_out=rsum[:, u % 3]).then_inc(S["exp_done"], 1)

            def normed(pr, u):
                act.wait_ge(S["inv_done"], pr * UNITS + u + 1)
                nc.scalar.activation(weights_of(u), weights_of(u), ACT.Identity, scale=rsum[:, u % 3]).then_inc(S["p_ready"], 1)

            def turned(pr, u):
                for i, (uu, place, w) in enumerate(TSTEPS):
                    if uu != u:
                        continue
                    act.wait_ge(S["t_done"], pr * len(TSTEPS) + i + 1)
                    G, half = unit(u)
                    if half == 0 and G >= 2 and place == 1:
                        act.wait_ge(S["pv_done"], pr * NG + G - 1)
                    q = slice(half * P, half * P + P)
                    round_high(nc, pt_h[G % 2][:, place:place + w, q], bank[:, 4 + i % 2, 0:w * P].rearrange("p (a q) -> p a q", a=w)).then_inc(S["t_high"], 1)

            for i in range(WPARTS):
                split(0, i)
            for x in (pt_h[0], pt_h[1], pt_l[0], pt_l[1]):
                nc.scalar.activation(x[:, 0, 0:P], k.ident[:], ACT.Identity, scale=0.0).then_inc(S["zeroed"], 1)
            for s in PROJ[:NE]:
                proj(0, s, True)

            def body(pr, first, last):
                for s in READS[NE:]:
                    if s == "V0":
                        exp(pr, 0)
                    if s == "V1":
                        normed(pr, 0)
                        exp(pr, 1)
                    proj(pr, s, first)
                for u in range(UNITS):
                    if u + 1 < UNITS:
                        normed(pr, u + 1)
                    if u in EARLY and not last:
                        for s in EARLY[u]:
                            proj(pr + 1, s, False)
                    turned(pr, u)
                    if u + 2 < UNITS:
                        exp(pr, u + 2)
                    if 5 <= u < 5 + WPARTS and not last:
                        split(pr + 1, u - 5)
                if not last:
                    for s in EARLY[UNITS]:
                        proj(pr + 1, s, False)
            pairs(act, body)

        @block.vector
        def _(dve):
            def split(pr, i):
                dve.wait_ge(S["wh_ready"], pr * WPARTS + i + 1)
                round_low(nc, piece(w_l, i), piece(w_raw, i), piece(w_h, i)).then_inc(S["wl_ready"], 1)

            def rope(pr, tg):
                i = STEP[f"R{tg}"]
                dve.wait_ge(S["proj_done"], pr * NP + i + 1)
                x = bank[:, PROJ_BANK[i], 0:TG]
                cols = slice(tg * TG, tg * TG + TG)
                nc.vector.tensor_tensor(rope_part(tg, 0), x, cos[:, cols], ALU.mult)
                for a, b in ((0, 32), (32, 0), (64, 96), (96, 64)):
                    last = nc.vector.tensor_tensor(rope_part(tg, 1)[b:b + 32], x[a:a + 32], sin[a:a + 32, cols], ALU.mult)
                last.then_inc(S["rope_step"], 1)
                dve.wait_ge(S["rope_step"], pr * 3 + tg + 1)
                dve.sem_inc(S["proj_out"], 1)

            def rope_low(pr, tg):
                dve.wait_ge(S["rq_high"], pr * 3 + tg + 1)
                c = slice(tg * TG, tg * TG + TG)
                scaled_low(rq[RD:P, :, c], rope_sums(tg), rq[0:RD, :, c]).then_inc(S["rq_out"], 1)

            def scaled_low(out, x, high):
                return nc.vector.scalar_tensor_tensor(out=out, in0=x, scalar=SCALE, in1=high.bitcast(F32), op0=ALU.mult, op1=ALU.subtract)

            def proj(pr, s):
                i, b = STEP[s], bank[:, PROJ_BANK[STEP[s]]]
                dve.wait_ge(S["proj_high"], pr * HIGHS + HIGH_COUNT[s])
                if s in ("UT", "QL"):
                    dve.sem_inc(S["proj_out"], 1)
                elif s[0] == "Q":
                    e, tg = "AB".index(s[1]), int(s[2])
                    at = (slice(None), e, slice(tg * TG, tg * TG + TG))
                    scaled_low(qn_l[at], b[:, 0:TG], qn_h[at]).then_inc(S["proj_out"], 1)
                elif s[0] == "K":
                    e, c = "AB".index(s[1]), int(s[2])
                    at = (slice(None), e, slice(c * BANK, (c + 1) * BANK))
                    round_low(nc, kt_l[at], b, kt_h[at]).then_inc(S["proj_out"], 1)
                else:
                    c = int(s[1])
                    round_low(nc, flat(v_l[:, 2 * c:2 * c + 2]), b, flat(v_h[:, 2 * c:2 * c + 2])).then_inc(S["proj_out"], 1)

            def largest(pr, u):
                dve.wait_ge(S["s_done"], pr * UNITS + u + 1)
                n = P * (place_of(u)[1] + 1)
                b, end = (0, n) if n <= BANK else (1, n // 2)
                nc.vector.memset(bank[0:CH, 2 * (u % 2) + b, end - CH:end], MASKED).then_inc(S["masked"], 1)
                dve.wait_ge(S["masked"], pr * UNITS + u + 1)
                if u >= 3:
                    dve.wait_ge(S["exp_done"], pr * UNITS + u - 2)
                nc.vector.tensor_reduce(mx[:, u % 3], scores_of(u), AX.X if n <= BANK else AX.XY, ALU.max, negate=True).then_inc(S["max_done"], 1)

            def inverted(pr, u):
                dve.wait_ge(S["exp_done"], pr * UNITS + u + 1)
                nc.vector.reciprocal(rsum[:, u % 3], rsum[:, u % 3]).then_inc(S["inv_done"], 1)

            def turned(pr, u):
                for i, (uu, place, w) in enumerate(TSTEPS):
                    if uu != u:
                        continue
                    dve.wait_ge(S["t_high"], pr * len(TSTEPS) + i + 1)
                    G, half = unit(u)
                    at = (slice(None), slice(place, place + w), slice(half * P, half * P + P))
                    round_low(nc, pt_l[G % 2][at], bank[:, 4 + i % 2, 0:w * P].rearrange("p (a q) -> p a q", a=w), pt_h[G % 2][at]).then_inc(S["t_out"], 1)

            def gated(pr, G):
                dve.wait_ge(S["pv_done"], pr * NG + G + 1)
                dve.wait_ge(gate_loaded[G % 2], pr * 64 + 16 * (G // 2) + 16)
                nc.vector.tensor_tensor(gate[:, G % 2], bank[:, 6 + G % 2, 0:GQ], gate[:, G % 2], ALU.mult).then_inc(S["o_out"], 1)

            for i in range(WPARTS):
                split(0, i)
            for s in PROJ[:NE]:
                proj(0, s)
            dve.wait_ge(S["table_loaded"], 32)

            def body(pr, first, last):
                rope(pr, 0)
                rope(pr, 1)
                rope_low(pr, 0)
                dve.wait_ge(S["rq_out"], pr * 3 + 1)
                rope(pr, 2)
                for s in READS[NE + 1:]:
                    if s[0] == "R":
                        rope_low(pr, int(s[1]))
                        continue
                    if s == "V0":
                        largest(pr, 0)
                    if s == "V1":
                        inverted(pr, 0)
                        largest(pr, 1)
                    proj(pr, s)
                for u in range(UNITS):
                    if u + 1 < UNITS:
                        inverted(pr, u + 1)
                    if u + 2 < UNITS:
                        largest(pr, u + 2)
                    if u >= 4 and u % 4 < 2:
                        gated(pr, u // 4 * 2 - 2 + u % 2)
                    if u in EARLY and not last:
                        for s in EARLY[u]:
                            proj(pr + 1, s)
                    turned(pr, u)
                    if 5 <= u < 5 + WPARTS and not last:
                        split(pr + 1, u - 5)
                gated(pr, NG - 2)
                if not last:
                    for s in EARLY[UNITS]:
                        proj(pr + 1, s)
                gated(pr, NG - 1)
            pairs(dve, body)


KB = PAST // P
KS = PAST + SLEN
KC = 352
KPAD = 3 * KC
QS = HEADS * SLEN
TURNS = ["K0", "K1", "K2", "W4", "W2", "W3", "K3", "K4", "K5", "K6", "W0", "W1"]
NKT = 7


def phase_samples(nc, k):
    d = k.d
    with ExitStack() as ctx:
        m = Core(nc, ctx)
        ql_raw = m.sb("s_ql_raw", [HEADS, 2, P])
        qr_raw = m.sb("s_qr_raw", [HEADS, P])
        q_h, q_l = m.sb("s_q_h", [2, 2, QS], F32R), m.sb("s_q_l", [2, 2, QS], F32R)
        rq = m.sb("s_rq", [2, QS], F32R)
        c_raw = m.sb("s_c_raw", [2, KB + 1, KVL])
        kr_raw = m.sb("s_kr_raw", [2, KB + 1, 2, RD])
        c_h, c_l = m.sb("s_c_h", [2, KB + 1, KVL], F32R), m.sb("s_c_l", [2, KB + 1, KVL], F32R)
        ct_h, ct_l = m.sb("s_ct_h", [2, 2, KPAD], F32R), m.sb("s_ct_l", [2, 2, KPAD], F32R)
        kt_h, kt_l = m.sb("s_kt_h", [2, KPAD], F32R), m.sb("s_kt_l", [2, KPAD], F32R)
        p = m.sb("s_p", [2, KPAD])
        pt_h, pt_l = m.sb("s_pt_h", [KB + 1, QS], F32R), m.sb("s_pt_l", [KB + 1, QS], F32R)
        olat = m.sb("s_olat", [2, HEADS, P])
        uv = flat(ql_raw[:].rearrange("p h a t -> p h (a t)")).rearrange("p (a e) -> p a e", a=2)
        gate = m.sb("s_gate", [HEADS, P])
        mx = m.sb("s_mx", [2, 1])
        rsum = m.sb("s_rsum", [2, 1])
        bank = m.ps("s_ps", [8, BANK])
        names = ("q_loaded uv_loaded zeroed qh_ready ql_ready s_done masked max_done exp_done inv_done p_ready t_done t_high t_out "
                 "o_done o_out ch_ready cl_ready uv_done uv_out og_stored").split()
        S = {n: m.sem("s_" + n) for n in names}
        c_loaded = [m.sem(f"s_c_loaded{i}") for i in range(2)]
        kr_loaded = [m.sem(f"s_kr_loaded{i}") for i in range(2)]
        block = ctx.enter_context(nc.Block())

        def turns(i):
            if not isinstance(i, int):
                return TURNS
            return [x for x in TURNS if not (i == 0 and x in ("W4", "W2", "W3")) and not (i == NSEQ - 1 and x[0] == "K")]

        def turn_number(i, x):
            if isinstance(i, int):
                n = NKT + sum(len(turns(j)) for j in range(i)) + (turns(i).index(x) if i < NSEQ else ("W4", "W2", "W3").index(x))
                return n, 6 + n % 2
            at = NKT + len(turns(0)) - len(TURNS) + TURNS.index(x)
            return i * len(TURNS) + at, 6 + at % 2

        def seqs(eng, body):
            body(0, 0, True, False)
            body(1, 1, False, False)
            with eng.Fori(1, NSEQ // 2 - 1) as pair:
                body(pair * 2, 0, False, False)
                body(pair * 2 + 1, 1, False, False)
            body(NSEQ - 2, 0, False, False)
            body(NSEQ - 1, 1, False, True)

        def step_of_keys(j):
            return [("c", 0, 0, 4), ("c", 0, 4, 4), ("c", 1, 0, 4), ("c", 1, 4, 4), ("kr", 0, 0, 4), ("kr", 0, 4, 4), ("new", 0, 8, 1)][j]

        @block.sync
        def _(sp):
            sp.wait_ge(S["zeroed"], 4)

            def body(i, par, first, last):
                if not (isinstance(i, int) and i < 2):
                    sp.wait_ge(S["cl_ready"], i - 1)
                row = lambda x: d[x][bass.ds(i, 1)].rearrange("o s e -> (o s) e")
                loads = [(c_raw[:, par, 0:KB], row("cache_ckv").rearrange("(j p) e -> p j e", p=P)),
                         (c_raw[0:SLEN, par, KB], row("ckv_sample"))]
                for copy in range(2):
                    loads += [(kr_raw[:, par, 0:KB, copy], row("cache_krope").rearrange("(j p) e -> p j e", p=P)),
                              (kr_raw[0:SLEN, par, KB, copy], row("krope_sample"))]
                for j, (dst, src) in enumerate(loads):
                    sp.dma_start(dst, src).then_inc((c_loaded if j < 2 else kr_loaded)[par], 16)
            seqs(sp, body)
            sp.wait_ge(S["ql_ready"], NSEQ)
            sp.dma_start(uv, d["w_uv"].rearrange("(a p) h n -> p a (h n)", p=P)).then_inc(S["uv_loaded"], 16)
            sp.dma_start(gate[:], d["scratch_gate"][:, :, SEQ:T].rearrange("h p t -> p h t")).then_inc(S["uv_loaded"], 16)
            for j in range(4):
                sp.wait_ge(S["uv_out"], j + 1)
                sp.dma_start(d["scratch_og"][4 * j:4 * j + 4, :, SEQ:T].rearrange("h p t -> p h t"), gate[:, 4 * j:4 * j + 4]).then_inc(S["og_stored"], 16)
            sp.wait_ge(S["og_stored"], 64)

        @block.gpsimd
        def _(pool):
            for x in (c_raw[:, 0, KB], c_raw[:, 1, KB], flat(kr_raw[:, 0, KB:KB + 1].rearrange("p o a b -> p o (a b)")), flat(kr_raw[:, 1, KB:KB + 1].rearrange("p o a b -> p o (a b)"))):
                nc.gpsimd.memset(x, 0.0).then_inc(S["zeroed"], 1)
            for x in (ct_h[:, :, :, KS:], ct_l[:, :, :, KS:], kt_h[:, :, KS:], kt_l[:, :, KS:], pt_h[:, KB], pt_l[:, KB]):
                nc.gpsimd.memset(x.bitcast(F32), 0.0).then_inc(S["zeroed"], 1)

        @block.tensor
        def _(pe):
            def turn_bank(n, at):
                if not (isinstance(n, int) and n < 2):
                    pe.wait_ge(S["t_out"], n - 1)
                return bank[:, at]

            def turn_keys(j, n, at, par):
                b = turn_bank(n, at)
                what, a, s0, w = step_of_keys(j)
                if what == "new":
                    for x in range(2):
                        nc.tensor.transpose(b[:, x * P:x * P + P], c_raw[:, par, KB, x * P:x * P + P], k.ident[:])
                    mm = nc.tensor.transpose(b[:, 2 * P:3 * P], kr_raw[:, par, KB].rearrange("p a b -> p (a b)"), k.ident[:])
                else:
                    for x in range(w):
                        src = c_raw[:, par, s0 + x, a * P:a * P + P] if what == "c" else kr_raw[:, par, s0 + x].rearrange("p a b -> p (a b)")
                        mm = nc.tensor.transpose(b[:, x * P:x * P + P], src, k.ident[:])
                mm.then_inc(S["t_done"], 1)

            def turn_weights(j, i, n, at):
                b = turn_bank(n, at)
                pe.wait_ge(S["p_ready"], i * 2 + (1 if j < 2 else 2))
                if j < 4:
                    for x in range(4):
                        s = (4 * (j % 2) + x) * P
                        mm = nc.tensor.transpose(b[:, x * P:x * P + P], p[:, j // 2, s:s + P], k.ident[:])
                else:
                    for x in range(2):
                        mm = nc.tensor.transpose(b[0:SLEN, x * P:x * P + P], p[:, x, PAST:KS], k.ident[:])
                mm.then_inc(S["t_done"], 1)

            def turn(x, i, par):
                if isinstance(i, int) and i < NSEQ and x not in turns(i):
                    return
                n, at = turn_number(i, x)
                if x[0] == "K":
                    if x == "K0":
                        pe.wait_ge(c_loaded[1 - par], (i + par) * 16 + 32)
                    if x == "K4":
                        pe.wait_ge(kr_loaded[1 - par], (i + par) * 32 + 64)
                    turn_keys(int(x[1]), n, at, 1 - par)
                else:
                    j = int(x[1])
                    turn_weights(j, i if j < 2 else i - 1, n, at)

            def scores(i, par, qt, beside):
                q = slice(qt * P, qt * P + P)
                for c in range(3):
                    out, kc = bank[:, 3 * qt + c, 0:KC], slice(c * KC, (c + 1) * KC)
                    for a in range(2):
                        product(nc, out, (q_h[:, par, a, q], q_l[:, par, a, q]), (ct_h[:, par, a, kc], ct_l[:, par, a, kc]), a == 0, False)
                    nc.tensor.matmul(out, rq[:, par, q], kt_l[:, par, kc], start=False, stop=False)
                    mm = nc.tensor.matmul(out, rq[:, par, q], kt_h[:, par, kc], start=False, stop=True)
                    if c == 2:
                        mm.then_inc(S["s_done"], 1)
                    if c < len(beside):
                        turn(beside[c], i, par)

            def values(i, par, a, waits):
                if waits:
                    if isinstance(i, int):
                        pe.wait_ge(S["t_out"], turn_number(i + 1, "W3")[0] + 1)
                    else:
                        pe.wait_ge(S["t_out"], i * len(TURNS) + (turn_number(1, "W3")[0] + 1))
                    pe.wait_ge(S["cl_ready"], i + 1)
                    pe.wait_ge(S["exp_done"], i * 2 + 3 if not (isinstance(i, int) and i == NSEQ - 1) else 2 * NSEQ)
                for s in range(KB + 1):
                    mm = product(nc, bank[:, 0, a * QS:a * QS + QS], (c_h[:, par, s, a * P:a * P + P], c_l[:, par, s, a * P:a * P + P]),
                                 (pt_h[:, s], pt_l[:, s]), s == 0, s == KB)
                if a == 1:
                    mm.then_inc(S["o_done"], 1)

            pe.wait_ge(S["zeroed"], 10)
            pe.wait_ge(c_loaded[0], 32)
            for j in range(NKT):
                if j == 4:
                    pe.wait_ge(kr_loaded[0], 64)
                turn_keys(j, j, 6 + j % 2, 0)

            def body(i, par, first, last):
                pe.wait_ge(S["ql_ready"], i + 1)
                if first:
                    pe.wait_ge(S["t_out"], NKT)
                else:
                    pe.wait_ge(S["t_out"], turn_number(i, "K0" if not last else "W4")[0] - 2)
                    pe.wait_ge(S["exp_done"], i * 2 - 1)
                    if not (isinstance(i, int) and i < 2):
                        pe.wait_ge(S["o_out"], i - 1)
                scores(i, par, 0, ["K0", "K1", "K2"])
                for x in ("W4", "W2", "W3"):
                    turn(x, i, par)
                if not first:
                    pe.wait_ge(S["exp_done"], i * 2)
                scores(i, par, 1, ["K3", "K4"])
                if not first:
                    values(i - 1, 1 - par, 0, True)
                turn("K5", i, par)
                if not first:
                    values(i - 1, 1 - par, 1, False)
                for x in ("K6", "W0", "W1"):
                    turn(x, i, par)
            seqs(pe, body)
            for x in ("W4", "W2", "W3"):
                turn(x, NSEQ, 0)
            pe.wait_ge(S["o_out"], NSEQ - 1)
            for a in range(2):
                values(NSEQ - 1, 1, a, a == 0)
            pe.wait_ge(S["uv_loaded"], 32)
            pe.wait_ge(S["o_out"], NSEQ)
            for h in range(HEADS):
                for a in range(2):
                    mm = nc.tensor.matmul(bank[:, h // 4, h % 4 * P:h % 4 * P + P], uv[:, a, h * DV:h * DV + DV], olat[:, a, h], start=a == 0, stop=a == 1)
                if h % 4 == 3:
                    mm.then_inc(S["uv_done"], 1)

        def step_columns(i):
            return slice(i * SLEN, i * SLEN + SLEN) if isinstance(i, int) else bass.ds(i * SLEN, SLEN)

        @block.scalar
        def _(act):
            act.dma_start(ql_raw[:].rearrange("p (r e) a t -> p r (e a t)", e=2), d["scratch_ql"].rearrange("r p t -> p r t")).then_inc(S["q_loaded"], 16)
            act.dma_start(qr_raw[0:RD].rearrange("p (r e) t -> p r (e t)", e=2), d["scratch_qr"].rearrange("r p t -> p r t")).then_inc(S["q_loaded"], 16)
            act.wait_ge(S["q_loaded"], 32)
            act.wait_ge(S["zeroed"], 10)

            def q_high(i, par):
                if not (isinstance(i, int) and i < 2):
                    act.wait_ge(S["s_done"], i * 2 - 2)
                cols = step_columns(i)
                for a in range(2):
                    nc.scalar.activation(q_h[:, par, a].rearrange("p (h l) -> p h l", h=HEADS), ql_raw[:, :, a, cols], ACT.Identity, scale=SCALE)
                nc.scalar.activation(rq[0:RD, par].rearrange("p (h l) -> p h l", h=HEADS), qr_raw[0:RD, :, cols], ACT.Identity, scale=SCALE).then_inc(S["qh_ready"], 1)

            def keys_high(j, n, at, par):
                b = bank[:, at]
                act.wait_ge(S["t_done"], n + 1)
                what, a, s0, w = step_of_keys(j)
                if what == "new":
                    round_high(nc, ct_h[:, par, :, PAST:KS], b[:, 0:2 * P].rearrange("p (a q) -> p a q", a=2)[:, :, 0:SLEN])
                    o = round_high(nc, kt_h[:, par, PAST:KS], b[:, 2 * P:2 * P + SLEN])
                else:
                    dst = ct_h[:, par, a, s0 * P:(s0 + w) * P] if what == "c" else kt_h[:, par, s0 * P:(s0 + w) * P]
                    o = round_high(nc, dst, b)
                o.then_inc(S["t_high"], 1)

            def high(x, i, par):
                if isinstance(i, int) and i < NSEQ and x not in turns(i):
                    return
                n, at = turn_number(i, x)
                j = int(x[1])
                if x[0] == "K":
                    if j == 0 and not (isinstance(i, int) and i == 0):
                        act.wait_ge(S["s_done"], i * 2)
                    return keys_high(j, n, at, 1 - par)
                b = bank[:, at]
                if j == 0 and not (isinstance(i, int) and i == 0):
                    act.wait_ge(S["o_done"], i)
                act.wait_ge(S["t_done"], n + 1)
                if j < 4:
                    o = round_high(nc, pt_h[:, 4 * (j % 2):4 * (j % 2) + 4, j // 2 * P:j // 2 * P + P], b.rearrange("p (a q) -> p a q", a=4))
                else:
                    o = round_high(nc, pt_h[0:SLEN, KB], b[0:SLEN, 0:2 * P])
                o.then_inc(S["t_high"], 1)

            def cache_high(i, par):
                act.wait_ge(c_loaded[par], (i - par) * 16 + 32)
                if not (isinstance(i, int) and i < 2):
                    act.wait_ge(S["o_done"], i - 1)
                round_high(nc, c_h[:, par], c_raw[:, par]).then_inc(S["ch_ready"], 1)

            def exp(i, qt):
                act.wait_ge(S["max_done"], i * 2 + qt + 1)
                if qt == 0 and not (isinstance(i, int) and i == 0):
                    act.wait_ge(S["t_done"], turn_number(i, "W4")[0] + 1)
                elif qt == 1 and not (isinstance(i, int) and i == 0):
                    act.wait_ge(S["t_done"], turn_number(i, "W3")[0] + 1)
                nc.scalar.activation(p[:, qt].rearrange("p (a b) -> p a b", a=3), bank[:, 3 * qt:3 * qt + 3, 0:KC], ACT.Exp,
                                     bias=mx[:, qt], accum_out=rsum[:, qt]).then_inc(S["exp_done"], 1)

            def normed(i, qt):
                act.wait_ge(S["inv_done"], i * 2 + qt + 1)
                nc.scalar.activation(p[:, qt], p[:, qt], ACT.Identity, scale=rsum[:, qt]).then_inc(S["p_ready"], 1)

            def result(i):
                act.wait_ge(S["o_done"], i + 1)
                for a in range(2):
                    o = nc.scalar.copy(olat[:, a, :, step_columns(i)], bank[:, 0, a * QS:a * QS + QS].rearrange("p (h l) -> p h l", h=HEADS))
                o.then_inc(S["o_out"], 1)

            q_high(0, 0)
            for j in range(NKT):
                keys_high(j, j, 6 + j % 2, 0)
            cache_high(0, 0)

            def body(i, par, first, last):
                for x in ("K0", "K1", "K2", "W4", "W2"):
                    high(x, i, par)
                exp(i, 0)
                high("W3", i, par)
                normed(i, 0)
                for x in ("K3", "K4"):
                    high(x, i, par)
                exp(i, 1)
                if not last:
                    q_high(i + 1, 1 - par)
                normed(i, 1)
                high("K5", i, par)
                if not first:
                    result(i - 1)
                for x in ("K6", "W0", "W1"):
                    high(x, i, par)
                if not last:
                    cache_high(i + 1, 1 - par)
            seqs(act, body)
            for x in ("W4", "W2", "W3"):
                high(x, NSEQ, 0)
            result(NSEQ - 1)

        @block.vector
        def _(dve):
            dve.wait_ge(S["q_loaded"], 32)
            dve.wait_ge(S["zeroed"], 10)

            def scaled_low(out, x, high):
                return nc.vector.scalar_tensor_tensor(out=out, in0=x, scalar=SCALE, in1=high.bitcast(F32), op0=ALU.mult, op1=ALU.subtract)

            def q_low(i, par):
                dve.wait_ge(S["qh_ready"], i + 1)
                cols = step_columns(i)
                for a in range(2):
                    v = lambda x: x[:, par, a].rearrange("p (h l) -> p h l", h=HEADS)
                    scaled_low(v(q_l), ql_raw[:, :, a, cols], v(q_h))
                r = lambda rows: rq[rows, par].rearrange("p (h l) -> p h l", h=HEADS)
                scaled_low(r(slice(RD, P)), qr_raw[0:RD, :, cols], r(slice(0, RD))).then_inc(S["ql_ready"], 1)

            def keys_low(j, n, at, par):
                b = bank[:, at]
                dve.wait_ge(S["t_high"], n + 1)
                what, a, s0, w = step_of_keys(j)
                if what == "new":
                    round_low(nc, ct_l[:, par, :, PAST:KS], b[:, 0:2 * P].rearrange("p (a q) -> p a q", a=2)[:, :, 0:SLEN], ct_h[:, par, :, PAST:KS])
                    o = round_low(nc, kt_l[:, par, PAST:KS], b[:, 2 * P:2 * P + SLEN], kt_h[:, par, PAST:KS])
                else:
                    cols = slice(s0 * P, (s0 + w) * P)
                    lo, hi = (ct_l[:, par, a, cols], ct_h[:, par, a, cols]) if what == "c" else (kt_l[:, par, cols], kt_h[:, par, cols])
                    o = round_low(nc, lo, b, hi)
                o.then_inc(S["t_out"], 1)

            def low(x, i, par):
                if isinstance(i, int) and i < NSEQ and x not in turns(i):
                    return
                n, at = turn_number(i, x)
                j = int(x[1])
                if x[0] == "K":
                    return keys_low(j, n, at, 1 - par)
                b = bank[:, at]
                dve.wait_ge(S["t_high"], n + 1)
                if j < 4:
                    to = (slice(None), slice(4 * (j % 2), 4 * (j % 2) + 4), slice(j // 2 * P, j // 2 * P + P))
                    o = round_low(nc, pt_l[to], b.rearrange("p (a q) -> p a q", a=4), pt_h[to])
                else:
                    o = round_low(nc, pt_l[0:SLEN, KB], b[0:SLEN, 0:2 * P], pt_h[0:SLEN, KB])
                o.then_inc(S["t_out"], 1)

            def cache_low(i, par):
                dve.wait_ge(S["ch_ready"], i + 1)
                round_low(nc, c_l[:, par], c_raw[:, par], c_h[:, par]).then_inc(S["cl_ready"], 1)

            def largest(i, qt):
                dve.wait_ge(S["s_done"], i * 2 + qt + 1)
                nc.vector.memset(bank[:, 3 * qt + 2, KS - 2 * KC:KC], MASKED).then_inc(S["masked"], 1)
                dve.wait_ge(S["masked"], i * 2 + qt + 1)
                if not (isinstance(i, int) and i == 0):
                    dve.wait_ge(S["exp_done"], i * 2 - 1 + qt)
                nc.vector.tensor_reduce(mx[:, qt], bank[:, 3 * qt:3 * qt + 3, 0:KC], AX.XY, ALU.max, negate=True).then_inc(S["max_done"], 1)

            def inverted(i, qt):
                dve.wait_ge(S["exp_done"], i * 2 + qt + 1)
                nc.vector.reciprocal(rsum[:, qt], rsum[:, qt]).then_inc(S["inv_done"], 1)

            q_low(0, 0)
            for j in range(NKT):
                keys_low(j, j, 6 + j % 2, 0)
            cache_low(0, 0)

            def body(i, par, first, last):
                for x in ("K0", "K1", "K2", "W4"):
                    low(x, i, par)
                largest(i, 0)
                low("W2", i, par)
                inverted(i, 0)
                for x in ("W3", "K3", "K4"):
                    low(x, i, par)
                largest(i, 1)
                inverted(i, 1)
                if not last:
                    q_low(i + 1, 1 - par)
                for x in ("K5", "K6", "W0", "W1"):
                    low(x, i, par)
                if not last:
                    cache_low(i + 1, 1 - par)
            seqs(dve, body)
            for x in ("W4", "W2", "W3"):
                low(x, NSEQ, 0)
            dve.wait_ge(S["uv_loaded"], 32)
            for j in range(4):
                dve.wait_ge(S["uv_done"], j + 1)
                g = flat(gate[:, 4 * j:4 * j + 4])
                nc.vector.tensor_tensor(g, bank[:, j], g, ALU.mult).then_inc(S["uv_out"], 1)


INPUTS = ["state_hgrn", "cache_ckv", "cache_krope", "w_in_a", "lb_gamma", "a_norm_g", "w_out_a", "w_dkv",
          "kv_norm_g", "w_uk", "w_uv", "w_in_b", "q_norm_g", "w_uq", "w_out_b", "ln_g", "ln_b"]
OUTPUTS = {"y": (NT, P, D), "state_prompt": (1, 1, AH, P, P), "ckv_prompt": (1, SEQ, KVL), "krope_prompt": (1, SEQ, RD),
           "state_sample": (1, NSEQ, AH, P, P), "ckv_sample": (NSEQ, SLEN, KVL), "krope_sample": (NSEQ, SLEN, RD)}
SCRATCH = {"scratch_o": (AH, P, T), "scratch_x": (NT, P, D), "scratch_gate": (HEADS, P, T), "scratch_og": (HEADS, P, T),
           "scratch_ql": (PAIRS, P, 4 * P), "scratch_qr": (PAIRS, RD, 2 * P)}


def encoder(nc, d):

    class Kept:
        pass

    k = Kept()
    k.d = d

    def keep(stack, name, shape, side):
        return [stack.enter_context(nc.sbuf_tensor(f"{name}_{part}", [P] + shape, F32R, side=side)) for part in "hl"]

    def row(x, t):
        return d[x][bass.ds(t, 1)].rearrange("o t d -> (o t) d")

    def tiles_of(x):
        return d[x].rearrange("h p t -> p h t")

    with nc.sbuf_tensor("ident", [P, P], F32) as k.ident:
        with ExitStack() as low:
            with ExitStack() as acts:
                k.act_h, k.act_l = keep(acts, "act", [KD, T], "right")
                phase_mixer_a(nc, k, lambda t: d["x"][t])
                phase_output(nc, k, "b", KD, d["w_out_a"][0], lambda t: tiles_of("scratch_o")[:, :, tile_cols(t)],
                             lambda t: row("x", t), (d["ln_g"][0], d["ln_b"][0]), True, lambda t: row("scratch_x", t))
                phase_gates(nc, k)
                k.ct_h, k.ct_l = keep(low, "ct", [2, SEQ], "left")
                k.kr_h, k.kr_l = keep(low, "kr", [SEQ], "left")
                k.cq_h, k.cq_l = keep(low, "cq", [4, T], "left")
                phase_latents(nc, k)
            phase_heads(nc, k)
        phase_samples(nc, k)
        phase_output(nc, k, "o", HEADS, d["w_out_b"][0], lambda t: tiles_of("scratch_og")[:, :, tile_cols(t)],
                     lambda t: row("scratch_x", t), (d["ln_g"][1], d["ln_b"][1]), False, lambda t: row("y", t))


def kernel(**inputs):
    import concourse.bacc as bacc
    from concourse.bass_utils import run_bass_kernel_spmd

    nc = bacc.Bacc("TRN2", target_bir_lowering=False, num_devices=1)
    arrays = {n: np.ascontiguousarray(inputs[n]) for n in INPUTS}
    arrays["x"] = np.concatenate([np.asarray(inputs["x_prompt"]).reshape(NPB, P, D), np.asarray(inputs["x_sample"]).reshape(1, P, D)])
    arrays.update(shape_constants())
    d = {n: nc.dram_tensor("in_" + n, list(a.shape), mybir.dt.from_np(a.dtype), kind="ExternalInput").ap() for n, a in arrays.items()}
    d.update({n: nc.dram_tensor("out_" + n, list(s), F32, kind="ExternalOutput").ap() for n, s in OUTPUTS.items()})
    d.update({n: nc.dram_tensor(n, list(s), F32, kind="Internal").ap() for n, s in SCRATCH.items()})
    encoder(nc, d)
    r = run_bass_kernel_spmd(nc, [{"in_" + n: a for n, a in arrays.items()}], core_ids=[0]).results[0]
    out = {n: r["out_" + n] for n in OUTPUTS}
    return (out["y"][:NPB].reshape(1, SEQ, D), out["y"][NPB].reshape(NSEQ, SLEN, D), out["state_prompt"], out["ckv_prompt"],
            out["krope_prompt"], out["state_sample"], out["ckv_sample"], out["krope_sample"])
```
